# Optimizing a Trainium2 kernel written in Bass

```python
import math
import jax, jax.numpy as jnp
from jax import lax
import numpy as np
import jax
import jax.numpy as jnp

D_MODEL = 1024
BATCH = 1
SEQ = 256
DEPTH = 1

CHUNK = 64
N_META = 16
BLOCK = math.gcd(N_META, CHUNK)
N_MIXERS = 2
N_LAYERS_A = (DEPTH + N_MIXERS - 1) // N_MIXERS
N_LAYERS_B = DEPTH // N_MIXERS
EPS = 1e-6

D_FF = 2816

A_HEADS = 8
A_DK = D_MODEL // 2 // A_HEADS
A_DV = D_MODEL // A_HEADS
A_CONV = 4
A_QK = A_HEADS * A_DK
A_V = A_HEADS * A_DV
A_COLS = 2 * A_QK + 2 * A_V + 2 * A_HEADS

B_HEADS = 8
B_DK = 128
B_DV = D_MODEL // B_HEADS
B_F = B_HEADS * B_DK
B_I = B_HEADS * B_DV
B_COLS = 2 * B_F + 2 * B_I


def rmsnorm(x, g):
    xf = x.astype(jnp.float32)
    y = xf * lax.rsqrt(jnp.mean(xf * xf, axis=-1, keepdims=True) + EPS)
    return (y * g.astype(jnp.float32)).astype(x.dtype)

def swiglu(x, w_in, w_out):
    gu = x @ w_in
    return (jax.nn.silu(gu[..., :D_FF]) * gu[..., D_FF:]) @ w_out

def causal_conv(x, w, b):
    kw, c = w.shape
    y = lax.conv_general_dilated(x, w[:, None, :].astype(x.dtype), window_strides=(1,),
                                 padding=[(kw - 1, 0)], dimension_numbers=('NWC', 'WIO', 'NWC'),
                                 feature_group_count=c)
    return y + b.astype(y.dtype)

def to_blocks(x):
    bsz, t = x.shape[0], x.shape[1]
    x = x.reshape((bsz, t // BLOCK, BLOCK) + x.shape[2:])
    return jnp.swapaxes(jnp.moveaxis(x, 1, 0), 2, 3)

def from_blocks(x):
    nb, bsz, h, l, d = x.shape
    x = jnp.moveaxis(jnp.swapaxes(x, 2, 3), 0, 1)
    return x.reshape(bsz, nb * l, h * d)

def mlstm_scan(q, k, v, ig, lf):
    _, bsz, nh, l, dk = q.shape
    dv = v.shape[-1]
    causal = jnp.tril(jnp.ones((l, l), dtype=bool))

    def step(carry, xs):
        c_prev, n_prev, m_prev = carry
        qb, kb, vb, ib, fb = xs
        bcum = jnp.cumsum(fb, axis=-1)
        dmat = jnp.where(causal, bcum[..., :, None] - bcum[..., None, :] + ib[..., None, :], -jnp.inf)
        g_inter = bcum + m_prev[..., None]
        m = jnp.maximum(g_inter, jnp.max(dmat, axis=-1))
        w_intra = jnp.exp(dmat - m[..., None])
        w_inter = jnp.exp(g_inter - m)
        s = jnp.einsum('bhld,bhsd->bhls', qb, kb) * w_intra
        num = jnp.einsum('bhls,bhsv->bhlv', s, vb) + w_inter[..., None] * jnp.einsum('bhvd,bhld->bhlv', c_prev, qb)
        den = jnp.sum(s, axis=-1) + w_inter * jnp.einsum('bhd,bhld->bhl', n_prev, qb)
        hb = num / jnp.maximum(jnp.abs(den), jnp.exp(-m))[..., None]
        b_last = bcum[..., -1]
        g_state = b_last[..., None] - bcum + ib
        m_new = jnp.maximum(b_last + m_prev, jnp.max(g_state, axis=-1))
        w_s = jnp.exp(g_state - m_new[..., None])
        decay = jnp.exp(b_last + m_prev - m_new)
        c_new = decay[..., None, None] * c_prev + jnp.einsum('bhsv,bhsd->bhvd', vb * w_s[..., None], kb)
        n_new = decay[..., None] * n_prev + jnp.einsum('bhs,bhsd->bhd', w_s, kb)
        return (c_new, n_new, m_new), hb

    init = (jnp.zeros((bsz, nh, dv, dk), jnp.float32), jnp.zeros((bsz, nh, dk), jnp.float32),
            jnp.zeros((bsz, nh), jnp.float32))
    _, hs = lax.scan(step, init, (q, k, v, ig, lf))
    return hs

def hgrn2_scan(q, k, v, lf):
    _, bsz, nh, l, dk = q.shape
    dv = v.shape[-1]
    causal = jnp.tril(jnp.ones((l, l), dtype=bool))

    def step(s_prev, xs):
        qb, kb, vb, fb = xs
        bcum = jnp.cumsum(fb, axis=-2)
        rel = jnp.where(causal[:, :, None], bcum[..., :, None, :] - bcum[..., None, :, :], -jnp.inf)
        a = jnp.sum(qb[..., :, None, :] * jnp.exp(rel) * kb[..., None, :, :], axis=-1)
        o = jnp.einsum('bhls,bhsv->bhlv', a, vb) + jnp.einsum('bhld,bhdv->bhlv', qb * jnp.exp(bcum), s_prev)
        b_last = bcum[..., -1, :]
        s_new = jnp.exp(b_last)[..., None] * s_prev + jnp.einsum(
            'bhsd,bhsv->bhdv', kb * jnp.exp(b_last[..., None, :] - bcum), vb)
        return s_new, o

    _, os_ = lax.scan(step, jnp.zeros((bsz, nh, dk, dv), jnp.float32), (q, k, v, lf))
    return os_

def mlstm_mixer(u, w_in, conv_w, conv_b, gate_b, w_out):
    bsz, t, _ = u.shape
    z = u @ w_in
    qk = jax.nn.silu(causal_conv(z[..., :2 * A_QK], conv_w, conv_b))
    v = z[..., 2 * A_QK:2 * A_QK + A_V]
    og = z[..., 2 * A_QK + A_V:2 * A_QK + 2 * A_V]
    gates = z[..., 2 * A_QK + 2 * A_V:].astype(jnp.float32) + gate_b.astype(jnp.float32)
    q = qk[..., :A_QK].reshape(bsz, t, A_HEADS, A_DK).astype(jnp.float32) * (A_DK ** -0.5)
    k = qk[..., A_QK:].reshape(bsz, t, A_HEADS, A_DK).astype(jnp.float32)
    v = v.reshape(bsz, t, A_HEADS, A_DV).astype(jnp.float32)
    ig = gates[..., :A_HEADS]
    lf = jax.nn.log_sigmoid(gates[..., A_HEADS:])
    hs = mlstm_scan(to_blocks(q), to_blocks(k), to_blocks(v), to_blocks(ig), to_blocks(lf))
    y = from_blocks(hs).astype(u.dtype) * jax.nn.sigmoid(og)
    return y @ w_out

def hgrn2_mixer(u, w_in, f_bias, lower_bound, g_norm, w_out):
    bsz, t, _ = u.shape
    z = u @ w_in
    q = jax.nn.silu(z[..., :B_F])
    fpre = z[..., B_F:2 * B_F].astype(jnp.float32) + f_bias.astype(jnp.float32)
    i_in = z[..., 2 * B_F:2 * B_F + B_I]
    g = z[..., 2 * B_F + B_I:]
    lf = jnp.logaddexp(jnp.log(lower_bound), jnp.log1p(-lower_bound) + jax.nn.log_sigmoid(fpre))
    k = (1.0 - lower_bound) * jax.nn.sigmoid(-fpre)
    q = q.reshape(bsz, t, B_HEADS, B_DK).astype(jnp.float32)
    k = k.reshape(bsz, t, B_HEADS, B_DK)
    lf = lf.reshape(bsz, t, B_HEADS, B_DK)
    v = i_in.reshape(bsz, t, B_HEADS, B_DV).astype(jnp.float32)
    o = hgrn2_scan(to_blocks(q), to_blocks(k), to_blocks(v), to_blocks(lf))
    y = from_blocks(o).astype(u.dtype) * jax.nn.sigmoid(g)
    return rmsnorm(y, g_norm) @ w_out

def first_inputs(seed: int = 0) -> dict:
    key = jax.random.key(seed)
    ks = jax.random.split(key, 16)
    f32 = jnp.float32
    x = jax.random.normal(ks[0], (BATCH, SEQ, D_MODEL), f32)
    meta_tokens = jax.random.normal(ks[1], (N_META, D_MODEL), f32)
    norm_gains = 1.0 + 0.1 * jax.random.normal(ks[2], (DEPTH, 6, D_MODEL), f32)
    ffn_w_in = jax.random.normal(ks[3], (DEPTH, 2, D_MODEL, 2 * D_FF), f32) * D_MODEL ** -0.5
    ffn_w_out = jax.random.normal(ks[4], (DEPTH, 2, D_FF, D_MODEL), f32) * D_FF ** -0.5
    a_w_in = jax.random.normal(ks[5], (N_LAYERS_A, D_MODEL, A_COLS), f32) * D_MODEL ** -0.5
    a_conv_w = jax.random.normal(ks[6], (N_LAYERS_A, A_CONV, 2 * A_QK), f32) * A_CONV ** -0.5
    a_conv_b = 0.01 * jax.random.normal(ks[7], (N_LAYERS_A, 2 * A_QK), f32)
    i_bias = 0.1 * jax.random.normal(ks[8], (N_LAYERS_A, A_HEADS), f32)
    f_bias_a = jnp.linspace(3.0, 6.0, A_HEADS, dtype=f32)[None, :] + 0.1 * jax.random.normal(ks[9], (N_LAYERS_A, A_HEADS), f32)
    a_gate_b = jnp.concatenate([i_bias, f_bias_a], axis=-1)
    a_w_out = jax.random.normal(ks[10], (N_LAYERS_A, A_V, D_MODEL), f32) * A_V ** -0.5
    b_w_in = jax.random.normal(ks[11], (N_LAYERS_B, D_MODEL, B_COLS), f32) * D_MODEL ** -0.5
    b_f_bias = 0.1 * jax.random.normal(ks[12], (N_LAYERS_B, B_F), f32)
    b_lb_raw = 0.5 * jax.random.normal(ks[13], (DEPTH, B_F), f32)
    b_g_norm = 1.0 + 0.1 * jax.random.normal(ks[14], (N_LAYERS_B, B_I), f32)
    b_w_out = jax.random.normal(ks[15], (N_LAYERS_B, B_I, D_MODEL), f32) * B_I ** -0.5
    return {'x': x, 'meta_tokens': meta_tokens, 'norm_gains': norm_gains, 'ffn_w_in': ffn_w_in,
            'ffn_w_out': ffn_w_out, 'a_w_in': a_w_in, 'a_conv_w': a_conv_w, 'a_conv_b': a_conv_b,
            'a_gate_b': a_gate_b, 'a_w_out': a_w_out, 'b_w_in': b_w_in, 'b_f_bias': b_f_bias,
            'b_lb_raw': b_lb_raw, 'b_g_norm': b_g_norm, 'b_w_out': b_w_out}

def first_block(x, meta_tokens, norm_gains, ffn_w_in, ffn_w_out, a_w_in, a_conv_w, a_conv_b, a_gate_b,
              a_w_out, b_w_in, b_f_bias, b_lb_raw, b_g_norm, b_w_out):
    bsz = x.shape[0]
    meta = jnp.broadcast_to(meta_tokens[None].astype(x.dtype), (bsz, N_META, D_MODEL))
    h = jnp.concatenate([meta, x], axis=1)
    sm = jax.nn.softmax(b_lb_raw.astype(jnp.float32), axis=0)
    lb_all = jnp.cumsum(sm, axis=0) - sm[0]
    for i in range(DEPTH):
        gn = norm_gains[i]
        h = h + 0.5 * rmsnorm(swiglu(rmsnorm(h, gn[0]), ffn_w_in[i, 0], ffn_w_out[i, 0]), gn[1])
        u = rmsnorm(h, gn[2])
        j = i // N_MIXERS
        if i % N_MIXERS == 0:
            y = mlstm_mixer(u, a_w_in[j], a_conv_w[j], a_conv_b[j], a_gate_b[j], a_w_out[j])
        else:
            y = hgrn2_mixer(u, b_w_in[j], b_f_bias[j], lb_all[i], b_g_norm[j], b_w_out[j])
        h = h + rmsnorm(y, gn[3])
        h = h + 0.5 * rmsnorm(swiglu(rmsnorm(h, gn[4]), ffn_w_in[i, 1], ffn_w_out[i, 1]), gn[5])
    return h[:, N_META:]


DEPTH_2 = 2

N_A_LAYERS = DEPTH_2 // 2
N_B_LAYERS = DEPTH_2 - N_A_LAYERS
NEG_INF = -1e30

GDN_QK_HEADS = 8
GDN_V_HEADS = 16
GDN_HEAD_DIM = 128
GDN_QK_DIM = GDN_QK_HEADS * GDN_HEAD_DIM
GDN_V_DIM = GDN_V_HEADS * GDN_HEAD_DIM
GDN_CONV_DIM = 2 * GDN_QK_DIM + GDN_V_DIM
GDN_IN_DIM = GDN_CONV_DIM + GDN_V_DIM + 2 * GDN_V_HEADS
GDN_CONV_WIDTH = 4
GDN_CHUNK = 64

SWA_Q_HEADS = 16
SWA_KV_HEADS = 4
SWA_GROUP = SWA_Q_HEADS // SWA_KV_HEADS
SWA_HEAD_DIM = 64
SWA_WINDOW = 128
SWA_BLOCK = 128

REL_BUCKETS = 32
REL_MAX_DISTANCE = 128

FFN_CONV_WIDTH = 3


def rmsnorm_2(x, w):
    xf = x.astype(jnp.float32)
    y = xf * lax.rsqrt(jnp.mean(xf * xf, axis=-1, keepdims=True) + EPS)
    return (y * w.astype(jnp.float32)).astype(x.dtype)

def l2norm(x):
    return x * lax.rsqrt(jnp.sum(x * x, axis=-1, keepdims=True) + EPS)

def causal_dwconv(x, w, b=None):
    width = w.shape[0]
    t = x.shape[1]
    xp = jnp.pad(x, ((0, 0), (width - 1, 0), (0, 0)))
    y = sum(xp[:, j:j + t] * w[j] for j in range(width))
    return y if b is None else y + b

def chunked_gated_delta_rule(q, k, v, g, beta):
    bsz, t, h, dk = q.shape
    dv = v.shape[-1]
    c = GDN_CHUNK
    n = t // c
    f32 = jnp.float32
    q = q.astype(f32).reshape(bsz, n, c, h, dk).transpose(0, 1, 3, 2, 4)
    k = k.astype(f32).reshape(bsz, n, c, h, dk).transpose(0, 1, 3, 2, 4)
    v = v.astype(f32).reshape(bsz, n, c, h, dv).transpose(0, 1, 3, 2, 4)
    g = g.astype(f32).reshape(bsz, n, c, h).transpose(0, 1, 3, 2)
    beta = beta.astype(f32).reshape(bsz, n, c, h).transpose(0, 1, 3, 2)

    gc = jnp.cumsum(g, axis=-1)
    tril = jnp.tril(jnp.ones((c, c), dtype=bool))
    strict = jnp.tril(jnp.ones((c, c), dtype=bool), -1)
    diff = gc[..., :, None] - gc[..., None, :]
    decay = jnp.where(tril, jnp.exp(jnp.where(tril, diff, 0.0)), 0.0)

    k_beta = k * beta[..., None]
    v_beta = v * beta[..., None]
    m = jnp.where(strict, jnp.einsum('bnhcd,bnhsd->bnhcs', k_beta, k) * decay, 0.0)
    eye = jnp.broadcast_to(jnp.eye(c, dtype=f32), m.shape)
    t_mat = lax.linalg.triangular_solve(m + eye, eye, left_side=True, lower=True,
                                        unit_diagonal=True)
    u = jnp.einsum('bnhcs,bnhse->bnhce', t_mat, v_beta)
    w = jnp.einsum('bnhcs,bnhsd->bnhcd', t_mat, k_beta * jnp.exp(gc)[..., None])
    a_intra = jnp.einsum('bnhcd,bnhsd->bnhcs', q, k) * decay
    q_dec = q * jnp.exp(gc)[..., None]
    k_dec = k * jnp.exp(gc[..., -1:] - gc)[..., None]
    g_last = jnp.exp(gc[..., -1])

    def step(state, inp):
        w_i, u_i, qd_i, kd_i, a_i, gl_i = inp
        v_new = u_i - jnp.einsum('bhcd,bhde->bhce', w_i, state)
        o_i = (jnp.einsum('bhcd,bhde->bhce', qd_i, state)
               + jnp.einsum('bhcs,bhse->bhce', a_i, v_new))
        state = state * gl_i[..., None, None] + jnp.einsum('bhcd,bhce->bhde', kd_i, v_new)
        return state, o_i

    xs = tuple(jnp.moveaxis(z, 1, 0) for z in (w, u, q_dec, k_dec, a_intra, g_last))
    s0 = jnp.zeros((bsz, h, dk, dv), f32)
    _, o = lax.scan(step, s0, xs)
    return o.transpose(1, 0, 3, 2, 4).reshape(bsz, t, h, dv)

def gated_deltanet(hn, w_in, conv_w, a_log, dt_bias, out_norm_w, w_out):
    bsz, t, _ = hn.shape
    proj = hn @ w_in
    qkv, z, b, a = jnp.split(
        proj, [GDN_CONV_DIM, GDN_CONV_DIM + GDN_V_DIM, GDN_CONV_DIM + GDN_V_DIM + GDN_V_HEADS],
        axis=-1)
    qkv = jax.nn.silu(causal_dwconv(qkv, conv_w))
    q, k, v = jnp.split(qkv, [GDN_QK_DIM, 2 * GDN_QK_DIM], axis=-1)
    q = l2norm(q.reshape(bsz, t, GDN_QK_HEADS, GDN_HEAD_DIM)) * (GDN_HEAD_DIM ** -0.5)
    k = l2norm(k.reshape(bsz, t, GDN_QK_HEADS, GDN_HEAD_DIM))
    v = v.reshape(bsz, t, GDN_V_HEADS, GDN_HEAD_DIM)
    rep = GDN_V_HEADS // GDN_QK_HEADS
    q = jnp.repeat(q, rep, axis=2)
    k = jnp.repeat(k, rep, axis=2)
    beta = jax.nn.sigmoid(b.astype(jnp.float32))
    g = -jnp.exp(a_log.astype(jnp.float32)) * jax.nn.softplus(
        a.astype(jnp.float32) + dt_bias.astype(jnp.float32))
    o = chunked_gated_delta_rule(q, k, v, g, beta)
    z = z.reshape(bsz, t, GDN_V_HEADS, GDN_HEAD_DIM).astype(jnp.float32)
    o = rmsnorm_2(o, out_norm_w) * jax.nn.silu(z)
    return o.reshape(bsz, t, GDN_V_DIM).astype(hn.dtype) @ w_out

def shared_kv(h, kv_norm_w, w_kv):
    bsz, t, _ = h.shape
    kv = rmsnorm_2(h, kv_norm_w) @ w_kv
    k, v = jnp.split(kv, 2, axis=-1)
    shape = (bsz, t, SWA_KV_HEADS, SWA_HEAD_DIM)
    return k.reshape(shape), v.reshape(shape)

def t5_bucket(dist):
    n = jnp.maximum(dist, 0)
    max_exact = REL_BUCKETS // 2
    nf = jnp.maximum(n, 1).astype(jnp.float32)
    large = max_exact + (jnp.log(nf / max_exact) / math.log(REL_MAX_DISTANCE / max_exact)
                         * (REL_BUCKETS - max_exact)).astype(jnp.int32)
    large = jnp.minimum(large, REL_BUCKETS - 1)
    return jnp.where(n < max_exact, n, large)

def band_bias_and_mask(rel_table, nb):
    qi = jnp.arange(SWA_BLOCK)[:, None]
    ki = jnp.arange(2 * SWA_BLOCK)[None, :]
    dist = qi + SWA_BLOCK - ki
    bias = rel_table.astype(jnp.float32)[t5_bucket(dist)]
    bias = jnp.transpose(bias, (2, 0, 1)).reshape(
        SWA_KV_HEADS, SWA_GROUP, SWA_BLOCK, 2 * SWA_BLOCK)
    in_window = (dist >= 0) & (dist < SWA_WINDOW)
    key_pos = jnp.arange(nb)[:, None, None] * SWA_BLOCK + ki[None] - SWA_BLOCK
    mask = in_window[None] & (key_pos >= 0)
    return bias, mask

def sliding_window_sink_attention(hn, k, v, w_q, sinks, w_o, bias, mask):
    bsz, t, _ = hn.shape
    nb = t // SWA_BLOCK
    q = (hn @ w_q).reshape(bsz, nb, SWA_BLOCK, SWA_KV_HEADS, SWA_GROUP, SWA_HEAD_DIM)
    q = q * (SWA_HEAD_DIM ** -0.5)

    def band(z):
        prev = jnp.concatenate([jnp.zeros_like(z[:, :SWA_BLOCK]), z[:, :-SWA_BLOCK]], axis=1)
        shape = (bsz, nb, SWA_BLOCK, SWA_KV_HEADS, SWA_HEAD_DIM)
        return jnp.concatenate([prev.reshape(shape), z.reshape(shape)], axis=2)

    kb, vb = band(k), band(v)
    s = jnp.einsum('bnqhgd,bnkhd->bnhgqk', q, kb).astype(jnp.float32) + bias
    s = jnp.where(mask[None, :, None, None], s, NEG_INF)
    sink = sinks.astype(jnp.float32).reshape(SWA_KV_HEADS, SWA_GROUP)[:, :, None]
    m = jnp.maximum(jnp.max(s, axis=-1), sink)
    p = jnp.exp(s - m[..., None])
    denom = jnp.sum(p, axis=-1) + jnp.exp(sink - m)
    probs = (p / denom[..., None]).astype(vb.dtype)
    o = jnp.einsum('bnhgqk,bnkhd->bnqhgd', probs, vb)
    return o.reshape(bsz, t, SWA_Q_HEADS * SWA_HEAD_DIM) @ w_o

def conv_gated_mlp(hn, w_up, conv_w, conv_b, w_down):
    u = causal_dwconv(hn @ w_up, conv_w, conv_b)
    gate, val = jnp.split(u, 2, axis=-1)
    return (jax.nn.silu(gate) * val) @ w_down

def second_inputs(seed: int = 0) -> dict:
    key = jax.random.key(seed)
    ks = jax.random.split(key, 24)
    f32 = jnp.float32

    def nrm(k, shape, scale):
        return jax.random.normal(k, shape, f32) * scale

    def gain(k, shape):
        return 1.0 + 0.02 * jax.random.normal(k, shape, f32)

    dt = jnp.exp(jax.random.uniform(ks[5], (N_A_LAYERS, GDN_V_HEADS), f32,
                                    minval=math.log(1e-3), maxval=math.log(1e-1)))
    return {
        'x': nrm(ks[0], (BATCH, SEQ, D_MODEL), 1.0),
        'a_norm_w': gain(ks[1], (N_A_LAYERS, D_MODEL)),
        'a_w_in': nrm(ks[2], (N_A_LAYERS, D_MODEL, GDN_IN_DIM), D_MODEL ** -0.5),
        'a_conv_w': nrm(ks[3], (N_A_LAYERS, GDN_CONV_WIDTH, GDN_CONV_DIM), GDN_CONV_WIDTH ** -0.5),
        'a_a_log': jnp.log(jax.random.uniform(ks[4], (N_A_LAYERS, GDN_V_HEADS), f32,
                                              minval=1.0, maxval=16.0)),
        'a_dt_bias': dt + jnp.log(-jnp.expm1(-dt)),
        'a_out_norm_w': gain(ks[6], (N_A_LAYERS, GDN_HEAD_DIM)),
        'a_w_out': nrm(ks[7], (N_A_LAYERS, GDN_V_DIM, D_MODEL), GDN_V_DIM ** -0.5),
        'kv_norm_w': gain(ks[8], (D_MODEL,)),
        'w_kv': nrm(ks[9], (D_MODEL, 2 * SWA_KV_HEADS * SWA_HEAD_DIM), D_MODEL ** -0.5),
        'b_norm_w': gain(ks[10], (N_B_LAYERS, D_MODEL)),
        'b_w_q': nrm(ks[11], (N_B_LAYERS, D_MODEL, SWA_Q_HEADS * SWA_HEAD_DIM), D_MODEL ** -0.5),
        'b_sinks': nrm(ks[12], (N_B_LAYERS, SWA_Q_HEADS), 0.5),
        'b_w_o': nrm(ks[13], (N_B_LAYERS, SWA_Q_HEADS * SWA_HEAD_DIM, D_MODEL),
                     (SWA_Q_HEADS * SWA_HEAD_DIM) ** -0.5),
        'rel_bias_table': nrm(ks[14], (REL_BUCKETS, SWA_Q_HEADS), 0.5),
        'ffn_norm_w': gain(ks[15], (DEPTH_2, D_MODEL)),
        'ffn_w_up': nrm(ks[16], (DEPTH_2, D_MODEL, 2 * D_FF), D_MODEL ** -0.5),
        'ffn_conv_w': nrm(ks[17], (DEPTH_2, FFN_CONV_WIDTH, 2 * D_FF), FFN_CONV_WIDTH ** -0.5),
        'ffn_conv_b': nrm(ks[18], (DEPTH_2, 2 * D_FF), 0.02),
        'ffn_w_down': nrm(ks[19], (DEPTH_2, D_FF, D_MODEL), D_FF ** -0.5),
        'final_norm_w': gain(ks[20], (D_MODEL,)),
    }

def second_block(x, a_norm_w, a_w_in, a_conv_w, a_a_log, a_dt_bias, a_out_norm_w, a_w_out,
              kv_norm_w, w_kv, b_norm_w, b_w_q, b_sinks, b_w_o, rel_bias_table,
              ffn_norm_w, ffn_w_up, ffn_conv_w, ffn_conv_b, ffn_w_down, final_norm_w):
    nb = x.shape[1] // SWA_BLOCK
    bias, mask = band_bias_and_mask(rel_bias_table, nb)
    h = x
    k_sh = None
    v_sh = None
    for layer in range(DEPTH_2):
        if layer < N_A_LAYERS:
            i = layer
            h = h + gated_deltanet(rmsnorm_2(h, a_norm_w[i]), a_w_in[i], a_conv_w[i], a_a_log[i],
                                   a_dt_bias[i], a_out_norm_w[i], a_w_out[i])
        else:
            j = layer - N_A_LAYERS
            if j == 0:
                k_sh, v_sh = shared_kv(h, kv_norm_w, w_kv)
            h = h + sliding_window_sink_attention(rmsnorm_2(h, b_norm_w[j]), k_sh, v_sh, b_w_q[j],
                                                  b_sinks[j], b_w_o[j], bias, mask)
        h = h + conv_gated_mlp(rmsnorm_2(h, ffn_norm_w[layer]), ffn_w_up[layer], ffn_conv_w[layer],
                               ffn_conv_b[layer], ffn_w_down[layer])
    return rmsnorm_2(h, final_norm_w)


def setup_inputs(seed=0):
    out = dict(first_inputs(seed))
    for name, value in second_inputs(seed + 1).items():
        if name != "x":
            out[name + "_2"] = value
    return out


def reference(
    x, meta_tokens, norm_gains, ffn_w_in, ffn_w_out, a_w_in, a_conv_w, a_conv_b, a_gate_b,
    a_w_out, b_w_in, b_f_bias, b_lb_raw, b_g_norm, b_w_out, a_norm_w_2, a_w_in_2, a_conv_w_2,
    a_a_log_2, a_dt_bias_2, a_out_norm_w_2, a_w_out_2, kv_norm_w_2, w_kv_2, b_norm_w_2, b_w_q_2,
    b_sinks_2, b_w_o_2, rel_bias_table_2, ffn_norm_w_2, ffn_w_up_2, ffn_conv_w_2, ffn_conv_b_2,
    ffn_w_down_2, final_norm_w_2,
):
    x = first_block(
        x, meta_tokens, norm_gains, ffn_w_in, ffn_w_out, a_w_in, a_conv_w, a_conv_b, a_gate_b,
        a_w_out, b_w_in, b_f_bias, b_lb_raw, b_g_norm, b_w_out,
    )
    return second_block(
        x, a_norm_w_2, a_w_in_2, a_conv_w_2, a_a_log_2, a_dt_bias_2, a_out_norm_w_2, a_w_out_2,
        kv_norm_w_2, w_kv_2, b_norm_w_2, b_w_q_2, b_sinks_2, b_w_o_2, rel_bias_table_2,
        ffn_norm_w_2, ffn_w_up_2, ffn_conv_w_2, ffn_conv_b_2, ffn_w_down_2, final_norm_w_2,
    )


_drawn_inputs = setup_inputs


def setup_inputs(seed=0):
    import zlib

    import numpy as np

    out = dict(_drawn_inputs(seed))
    spreads = {}
    factors = {'a_conv_b': 3.451,
     'a_norm_w_2': 4.205,
     'a_out_norm_w_2': 6.774,
     'kv_norm_w_2': 8.0,
     'b_norm_w_2': 8.0,
     'b_sinks_2': 197.091,
     'ffn_norm_w_2': 4.184,
     'ffn_conv_b_2': 4.063,
     'final_norm_w_2': 22.533,
     'rel_bias_table_2': 3.201}
    for name, (base, spread) in spreads.items():
        noise = np.random.default_rng([zlib.crc32(name.encode()), seed]).standard_normal(out[name].shape)
        drawn = base * np.exp(spread * noise) if base else spread * noise
        out[name] = jnp.asarray(drawn.astype(out[name].dtype))
    for name, factor in factors.items():
        out[name] = (out[name] * factor).astype(out[name].dtype)
    return out
```

```python
from contextlib import ExitStack

import concourse.bass as bass
import numpy as np
from concourse import mybir

F32 = mybir.dt.float32
F32R = mybir.dt.float32r
ALU = mybir.AluOpType
ACT = mybir.ActivationFunctionType
AX = mybir.AxisListType

P = 128
D = 1024
DC = D // P
SEQ = 256
META = 16
TM = SEQ + META
FF = 2816
FC = FF // P
EPS = 1e-6

A_HEADS = 8
A_DK = 64
GDN_QK = 8
GDN_V = 16
SWA_KV = 4
SWA_HD = 64
BUCKETS = 32
MAX_DIST = 128
NEG = -1e30

SLOTS = 4
TILES = 8

VEC = {}
_VEC_SIZES = [("g0", 8), ("g1", 8), ("g2", 8), ("g3", 8), ("g4", 8), ("g5", 8), ("ga", 8), ("gkv", 8), ("gb", 8),
              ("gf0", 8), ("gf1", 8), ("gfin", 8), ("acw", 4 * 8), ("acb", 8), ("dcw", 4 * 32), ("onw", 1),
              ("fcw0", 3 * 44), ("fcb0", 44), ("fcw1", 3 * 44), ("fcb1", 44), ("sink", 16), ("gate", 2), ("dn", 2)]
_at = 0
for _name, _n in _VEC_SIZES:
    VEC[_name] = _at
    _at += _n
VECS = _at

LEVELS = 7
C_ID, C_LE, C_EPS, C_LEVEL = 0, P, 2 * P, 2 * P + 1
CONSTS = C_LEVEL + LEVELS * P


def constants():
    r, c = np.arange(P)[:, None], np.arange(P)[None, :]
    parts = [np.eye(P), r <= c, np.full((P, 1), EPS)]
    for level in range(LEVELS):
        b = 1 << level
        parts.append((r // (2 * b) == c // (2 * b)) & (r // b % 2 == 1) & (c // b % 2 == 0))
    return np.concatenate([np.asarray(x, np.float32) for x in parts], axis=1)


def bucket_rows():
    out = np.zeros((BUCKETS + 1, 3 * P), np.float32)
    for y in range(3 * P):
        n = 2 * P - 1 - y
        if not 0 <= n < P:
            out[BUCKETS, y] = 1.0
            continue
        exact = BUCKETS // 2
        b = n if n < exact else min(exact + int(np.log(n / exact) / np.log(MAX_DIST / exact) * exact), BUCKETS - 1)
        out[b, y] = 1.0
    return out


class Steps:

    def __init__(self, sem, names):
        self.sem, self.names, self.at = sem, list(names), 0

    def prime(self, eng):
        eng.sem_inc(self.sem, len(self.names))

    def done(self, instruction, name):
        assert self.names[self.at % len(self.names)] == name, (self.names[self.at % len(self.names)], name)
        self.at += 1
        instruction.then_inc(self.sem, 1)

    def wait(self, eng, it, name, back=0):
        n = len(self.names)
        eng.wait_ge(self.sem, (it + (1 - back)) * n + self.names.index(name) + 1)


class Stage:

    def __init__(self, name, weights, iters, units, banks, T, rhs, off=0, look=None):
        self.name, self.weights, self.iters, self.units = name, weights, iters, units
        self.banks, self.T, self.rhs, self.off = banks, T, rhs, off
        self.look = look if look is not None else len(banks)
        self.groups = 1 + max(g for u in units for g, _ in u)
        self.first_k = {g: min(k for u in units for q, k in u if q == g) for g in range(self.groups)}
        self.last_k = {g: max(k for u in units for q, k in u if q == g) for g in range(self.groups)}
        self.unit_of = {g: max(n for n, u in enumerate(units) if any(q == g for q, _ in u)) for g in range(self.groups)}
        self.at = [sum(len(u) for u in units[:n]) for n in range(len(units))]


def whole(groups, ks=DC):
    return [[(g, k) for k in range(ks)] for g in range(groups)]


def cut(groups, cuts):
    out = []
    for g in range(groups):
        at = 0
        for n in cuts:
            out.append([(g, at + k) for k in range(n)])
            at += n
    return out


def program(nc, a):
    with ExitStack() as ctx:
        def sem(name):
            return ctx.enter_context(nc.semaphore(name))

        top = [nc.sbuf_base + (-nc.sbuf_base) % 64]

        def region(size):
            at = top[0]
            top[0] += size
            assert top[0] <= nc.sbuf_usable_end, top[0]
            return at

        def carve(at, size, **what):
            out, end = [], at + size
            for name, (shape, dt) in what.items():
                n = int(np.prod(shape[1:])) * 4
                assert at + n <= end, (name, at + n - end)
                out.append(nc.alloc_sbuf_tensor_at(name, shape, dt, offset=at))
                at += -(-n // 32) * 32
            return out

        def sb(name, shape, dt=F32):
            n = -(-int(np.prod(shape[1:])) * 4 // 32) * 32
            return nc.alloc_sbuf_tensor_at(name, shape, dt, offset=region(n))

        def row(name, shape=(P, TM)):
            return sb(name, list(shape))

        H = sb("H", [P, DC, TM])
        xreg_size = 2 * DC * TM * 4
        xreg = region(xreg_size)
        raw = [sb(f"raw{i}", [P, TILES, P]) for i in range(SLOTS)]
        WH = [sb(f"wh{i}", [P, TILES, P], F32R) for i in range(SLOTS)]
        WL = [sb(f"wl{i}", [P, TILES, P], F32R) for i in range(SLOTS)]
        vec = sb("vec", [P, VECS])
        cst = sb("cst", [P, CONSTS])
        ones = sb("ones", [P, P])
        mean = sb("mean", [P, P])
        R = row("R")
        RP = row("RP")
        ACC = row("ACC")
        TP = [row(f"tp{i}", (P, 3 + TM)) for i in range(2)]
        rel = sb("rel", [BUCKETS + 1, 16])
        AC = sb("AC", [P, 3, A_HEADS])
        COLS = sb("COLS", [P, 2, 2, GDN_V])
        big_size, ext_size = 49152, 49152
        big, ext = region(big_size), region(ext_size)
        work_size = nc.sbuf_usable_end - top[0] - 64
        work = region(work_size)
        buf = carve(work, work_size, **{f"{n}{i}": ([P, TM], F32) for n in ("sqb", "cv", "sg", "pr", "sc")
                                        for i in range(2)})
        SQB, CV, SG, PR, SC = (buf[i:i + 2] for i in range(0, 10, 2))
        CONV = CV + SG
        spare = work + 10 * TM * 4 + 64
        spare_size = work + work_size - spare
        XH, XL = carve(xreg, xreg_size, XH=([P, DC, TM], F32R), XL=([P, DC, TM], F32R))
        gains = {n: vec[:, VEC[n]:VEC[n] + DC] for n in ("g0", "g1", "g2", "g3", "g4", "g5", "ga", "gkv", "gb", "gf0",
                                                        "gf1", "gfin")}

        def v(name, i):
            return vec[:, VEC[name] + i:VEC[name] + i + 1] if isinstance(i, int) else vec[:, bass.ds(VEC[name] + i, 1)]

        ident = cst[:, C_ID:C_ID + P]
        causal = cst[:, C_LE:C_LE + P]
        eps = cst[:, C_EPS:C_EPS + 1]
        bank = [ctx.enter_context(nc.psum_tensor(f"bank{i}", [P, 512], F32)) for i in range(8)]

        AH, AL = carve(big, big_size, AH=([P, FC, TM], F32R), AL=([P, FC, TM], F32R))
        YG, SQ = carve(ext, ext_size, YG=([P, DC, TM], F32), SQ=([P, DC, TM], F32))

        mx_d = nc.dram_tensor("mx_d", (2, A_HEADS, TM), F32, kind="Internal").ap()
        gc_d = nc.dram_tensor("gc_d", (GDN_V, SEQ), F32, kind="Internal").ap()
        bias_d = nc.dram_tensor("bias_d", (16, P, 3 * P), F32, kind="Internal").ap()

        X, A = (XH, XL), (AH, AL)
        up_units, down_units = whole(4), cut(2, (6, 6, 5, 5))
        stages = []

        def stage(*args, **kw):
            st = Stage(*args, **kw)
            st.u0 = sum(s.iters * len(s.units) for s in stages)
            st.g0 = sum(s.iters * s.groups for s in stages)
            stages.append(st)
            return st

        up1 = stage("up1", a["w_up1"], 11, up_units, [0, 1, 2, 3], TM, X)
        down1 = stage("down1", a["w_down1"], 4, down_units, [2, 3], TM, A)
        mgate = stage("mgate", a["w_mgate"], 1, cut(1, (2, 2, 2, 2)), [3], TM, X, look=1)
        mqk = stage("mqk", a["w_mqk"], 2, whole(4), [0, 1, 2, 3], TM, X)
        mv = stage("mv", a["w_mv"], 2, whole(4), [0, 1, 2, 3], TM, X)
        mog = stage("mog", a["w_mog"], 2, whole(4), [0, 1, 2, 3], SEQ, X, off=META)
        mout = stage("mout", a["w_mout"], 2, whole(4), [0, 1, 2, 3], SEQ, X)
        up2 = stage("up2", a["w_up2"], 11, up_units, [0, 1, 2, 3], SEQ, X)
        down2 = stage("down2", a["w_down2"], 4, down_units, [2, 3], SEQ, A)
        ggate = stage("ggate", a["w_ggate"], 1, cut(1, (2, 2, 2, 2)), [3], SEQ, X, look=1)
        gqk = stage("gqk", a["w_gqk"], 4, whole(4), [0, 1, 2, 3], SEQ, X)
        gv = stage("gv", a["w_gv"], 4, whole(4), [0, 1, 2, 3], SEQ, X)
        gz = stage("gz", a["w_gz"], 4, whole(4), [0, 1, 2, 3], SEQ, X)
        YH, YL, Z = carve(big, big_size, YH=([P, 16, SEQ], F32R), YL=([P, 16, SEQ], F32R), Z=([P, 16, SEQ], F32))
        gout = stage("gout", a["w_gout"], 4, cut(2, (8, 8)), [2, 3], SEQ, (YH, YL))
        up3 = stage("up3", a["w_up3"], 11, up_units, [0, 1, 2, 3], SEQ, X)
        down3 = stage("down3", a["w_down3"], 4, down_units, [2, 3], SEQ, A)
        skv = stage("skv", a["w_skv"], 1, whole(4), [0, 1, 2, 3], SEQ, X)
        BH, BL, OH, OL = carve(ext, ext_size, BH=([P, DC, SEQ], F32R), BL=([P, DC, SEQ], F32R),
                               OH=([P, DC, SEQ], F32R), OL=([P, DC, SEQ], F32R))
        sq_ = stage("sq", a["w_sq"], 2, whole(4), [0, 1, 2, 3], SEQ, (BH, BL))
        so = stage("so", a["w_so"], 2, whole(4), [0, 1, 2, 3], SEQ, (OH, OL))
        up4 = stage("up4", a["w_up4"], 11, up_units, [0, 1, 2, 3], SEQ, X)
        down4 = stage("down4", a["w_down4"], 4, down_units, [2, 3], SEQ, A)
        for s, t in zip(stages, stages[1:]):
            s.next = t
        stages[-1].next = None

        s_raw = [sem(f"s_raw{i}") for i in range(SLOTS)]
        s_hi = [sem(f"s_hi{i}") for i in range(SLOTS)]
        s_lo = [sem(f"s_lo{i}") for i in range(SLOTS)]
        s_pe = [sem(f"s_pe{i}") for i in range(SLOTS)]
        s_ev = sem("s_ev")
        s_in, s_h0 = sem("s_in"), sem("s_h0")
        s_h, s_xh, s_xl = sem("s_h"), sem("s_xh"), sem("s_xl")
        s_sq, s_ss, s_st, s_r = sem("s_sq"), sem("s_ss"), sem("s_st"), sem("s_r")
        s_ln, s_tmp, s_ms = sem("s_ln"), sem("s_tmp"), sem("s_ms")
        s_rel, s_bias, s_fin = sem("s_rel"), sem("s_bias"), sem("s_fin")
        s_out = sem("s_out")
        LO_POOL = {3}

        def turn(st, it, u):
            return it * (len(st.units) // SLOTS) + (st.u0 + u) // SLOTS

        def unit_done(eng, st, it, u):
            eng.wait_ge(s_pe[u % SLOTS], turn(st, it, u) + 2)

        def group_done(eng, st, it, g):
            unit_done(eng, st, it, st.unit_of[g])

        def group(st, it, g):
            return st.g0 + it * st.groups + g

        def evacuated(eng, st, it, g):
            eng.wait_ge(s_ev, group(st, it, g) + 5)

        def run_dma(eng):
            for st in stages:
                with eng.Fori(0, st.iters) as it:
                    for u, tiles in enumerate(st.units):
                        s, n = u % SLOTS, len(tiles)
                        eng.wait_ge(s_lo[s], turn(st, it, u) + 1)
                        eng.dma_start(raw[s][:, 0:n, :], st.weights[bass.ds(it, 1), :, st.at[u]:st.at[u] + n, :]
                                      .rearrange("i p n m -> p (i n) m")).then_inc(s_raw[s], 16)

        def split_hi(eng, st, it, u):
            s, n = u % SLOTS, len(st.units[u])
            k = turn(st, it, u)
            eng.wait_ge(s_raw[s], (k + 1) * 16)
            eng.wait_ge(s_pe[s], k + 1)
            eng.activation(WH[s][:, 0:n, :], raw[s][:, 0:n, :], ACT.Copy).then_inc(s_hi[s], 1)

        def split_lo(eng, st, it, u):
            s, n = u % SLOTS, len(st.units[u])
            eng.wait_ge(s_hi[s], turn(st, it, u) + 1)
            eng.tensor_tensor(WL[s][:, 0:n, :], raw[s][:, 0:n, :], WH[s][:, 0:n, :].bitcast(F32),
                              ALU.subtract).then_inc(s_lo[s], 1)

        def split(eng, kind, st, it, u):
            if kind == "act":
                split_hi(eng, st, it, u)
            elif (kind == "pool") == (u % SLOTS in LO_POOL):
                split_lo(eng, st, it, u)

        def order(c, kind):
            if hasattr(c, "order"):
                return c.order[kind]
            if kind == "dve":
                return [(0, c.dve), "split"]
            return ["split", (0, c.act if kind == "act" else c.pool)]

        def walk(eng, kind, st, c, hook=None, hook_at=0):
            U = len(st.units)
            todo = order(c, kind)
            lags = [item[0] for item in todo if item != "split"]

            def body(it, last, first):
                for u in range(U):
                    n = u + SLOTS
                    if first and u == hook_at and hook is not None and kind != "act":
                        hook(eng)
                    for item in todo:
                        if item == "split":
                            if n < U:
                                split(eng, kind, st, it, n)
                            elif not last:
                                split(eng, kind, st, it + 1, n - U)
                            elif st.next is not None:
                                split(eng, kind, st.next, 0, n - U)
                            if first and u == hook_at and hook is not None and kind == "act":
                                hook(eng)
                        elif u >= item[0]:
                            item[1](eng, it, u - item[0])
                        elif not first:
                            item[1](eng, it - 1, u - item[0] + U)

            start = 0
            if st.iters > 1 and (hook is not None or max(lags) > 0):
                body(0, False, True)
                start = 1
            if st.iters - 1 > start:
                with eng.Fori(start, st.iters - 1) as it:
                    body(it, False, False)
            body(st.iters - 1, True, st.iters == 1)
            for u in range(U, U + max(lags)):
                for item in todo:
                    if item != "split" and u - item[0] < U:
                        item[1](eng, st.iters - 1, u - item[0])

        def multiply(eng, st, hooks=None, rhs_wait=None):
            hi, lo = st.rhs
            t0, T = st.off, st.T

            def body(it, first):
                for u, tiles in enumerate(st.units):
                    s = u % SLOTS
                    if first and hooks and u in hooks:
                        hooks[u](eng)
                    eng.wait_ge(s_lo[s], turn(st, it, u) + 2)
                    for i, (g, k) in enumerate(tiles):
                        out = bank[st.banks[g % len(st.banks)]][:, 0:T]
                        start, stop = k == st.first_k[g], k == st.last_k[g]
                        if start:
                            eng.wait_ge(s_ev, group(st, it, g) + 5 - st.look)
                        if first and g == 0 and rhs_wait:
                            rhs_wait(k)
                        xh, xl = hi[:, k, t0:t0 + T], lo[:, k, t0:t0 + T]
                        eng.matmul(out, WH[s][:, i, :], xh, start=start, stop=False)
                        eng.matmul(out, WH[s][:, i, :], xl, start=False, stop=False)
                        mm = eng.matmul(out, WL[s][:, i, :], xh, start=False, stop=stop)
                    mm.then_inc(s_pe[s], 1)

            first = bool(hooks or rhs_wait)
            if first:
                body(0, True)
            if st.iters - first:
                with eng.Fori(int(first), st.iters) as it:
                    body(it, False)

        n_x, n_st, n_r, n_h, n_sq, n_ss, n_ln, n_tmp = ([0] for _ in range(8))
        n_ms = [4]

        class Norm:
            pass

        def norm_before(gain, T, h_from):
            o = Norm()
            o.gain, o.T, o.off, o.h = gain, T, TM - T, h_from
            o.x0, n_x[0] = n_x[0], n_x[0] + DC
            o.sq, n_sq[0] = n_sq[0], n_sq[0] + 1
            o.ss, n_ss[0] = n_ss[0], n_ss[0] + 1
            o.st, n_st[0] = n_st[0], n_st[0] + 1
            o.ln, n_ln[0] = n_ln[0], n_ln[0] + 1
            o.r, n_r[0] = n_r[0], n_r[0] + 1

            def act(eng):
                for c in range(DC):
                    o.h(eng, c)
                    eng.activation(XH[:, c, 0:T], H[:, c, o.off:TM], ACT.Identity, bias=0.0,
                                   scale=gains[gain][:, c:c + 1]).then_inc(s_xh, 1)
                eng.activation(SQ[:, :, 0:T], H[:, :, o.off:TM], ACT.Square).then_inc(s_sq, 1)

            def low(eng, c):
                o.h(eng, c)
                eng.wait_ge(s_xh, o.x0 + c + 1)
                eng.scalar_tensor_tensor(XL[:, c, 0:T], H[:, c, o.off:TM], gains[gain][:, c:c + 1],
                                         XH[:, c, 0:T].bitcast(F32), ALU.mult, ALU.subtract).then_inc(s_xl, 1)

            def dve(eng):
                eng.wait_ge(s_sq, o.sq + 1)
                eng.tensor_reduce(ACC[:, 0:T], SQ[:, :, 0:T].rearrange("p c t -> p t c"), AX.X,
                                  ALU.add).then_inc(s_ss, 1)

            def pe(eng):
                eng.wait_ge(s_ss, o.ss + 1)
                eng.matmul(bank[4][:, 0:T], mean[:, :], ACC[:, 0:T], start=True, stop=True).then_inc(s_st, 1)

            def rstd(eng):
                eng.wait_ge(s_st, o.st + 1)
                eng.activation(R[:, 0:T], bank[4][:, 0:T], ACT.Ln, bias=eps, scale=1.0).then_inc(s_ln, 1)
                eng.wait_ge(s_ln, o.ln + 1)
                eng.activation(R[:, 0:T], R[:, 0:T], ACT.Exp, scale=-0.5).then_inc(s_r, 1)

            o.act, o.low, o.dve, o.pe, o.rstd = act, low, dve, pe, rstd
            o.rhs = lambda eng: lambda k: eng.wait_ge(s_xl, o.x0 + k + 1)
            o.ready = lambda eng: eng.wait_ge(s_r, o.r + 1)
            return o

        def norm_streamed(st, which=0):
            o = Norm()
            o.st, n_st[0] = n_st[0], n_st[0] + 1
            o.ln, n_ln[0] = n_ln[0], n_ln[0] + 1
            o.r, n_r[0] = n_r[0], n_r[0] + 1
            T, G = SEQ, st.groups

            def pe(eng):
                st.dv.wait(eng, st.iters - 1, st.acc_last)
                eng.matmul(bank[4][:, 0:T], mean[:, :], ACC[:, 0:T], start=True, stop=True).then_inc(s_st, 1)

            def rstd(eng):
                eng.wait_ge(s_st, o.st + 1)
                eng.activation(R[:, 0:T], bank[4][:, 0:T], ACT.Ln, bias=eps, scale=1.0).then_inc(s_ln, 1)
                eng.wait_ge(s_ln, o.ln + 1)
                eng.activation(R[:, 0:T], R[:, 0:T], ACT.Exp, scale=-0.5).then_inc(s_r, 1)

            o.pe, o.rstd = pe, rstd
            o.rhs = lambda eng, i=which: lambda k: st.dv.wait(eng, k // G, f"low{i}_{k % G}")
            o.ready = lambda eng: eng.wait_ge(s_r, o.r + 1)
            return o

        def norm_after(st, T, h_n):
            o = Norm()
            o.st, n_st[0] = n_st[0], n_st[0] + 1
            o.ln, n_ln[0] = n_ln[0], n_ln[0] + 1
            o.r, n_r[0] = n_r[0], n_r[0] + 1
            o.h0, n_h[0] = n_h[0], n_h[0] + DC
            o.t0, n_tmp[0] = n_tmp[0], n_tmp[0] + DC
            off = TM - T

            def pe(eng):
                st.dv.wait(eng, st.iters - 1, st.acc_last)
                eng.matmul(bank[4][:, 0:T], mean[:, :], ACC[:, 0:T], start=True, stop=True).then_inc(s_st, 1)

            def rstd(eng):
                eng.wait_ge(s_st, o.st + 1)
                eng.activation(RP[:, 0:T], bank[4][:, 0:T], ACT.Ln, bias=eps, scale=1.0).then_inc(s_ln, 1)
                eng.wait_ge(s_ln, o.ln + 1)
                eng.activation(RP[:, 0:T], RP[:, 0:T], ACT.Exp, scale=-0.5).then_inc(s_r, 1)

            def dve(eng, follow):
                eng.wait_ge(s_r, o.r + 1)
                for c in range(DC + 2):
                    if c < DC:
                        eng.tensor_tensor(YG[:, c, 0:T], YG[:, c, 0:T], RP[:, 0:T], ALU.mult).then_inc(s_tmp, 1)
                    if 0 < c <= DC:
                        eng.wait_ge(s_tmp, o.t0 + c)
                        eng.tensor_tensor(H[:, c - 1, off:TM], H[:, c - 1, off:TM], YG[:, c - 1, 0:T],
                                          ALU.add).then_inc(s_h, 1)
                    if c > 1:
                        follow(eng, c - 2)

            o.pe, o.rstd, o.dve = pe, rstd, dve
            o.chunk = lambda eng, c: eng.wait_ge(s_h, o.h0 + c + 1)
            return o

        primed = []

        def steps(kind, name, names):
            s = Steps(sem(f"{kind}_{name}"), names)
            primed.append((kind, s))
            return s

        def leave(st, it, g, ins):
            ins.then_inc(s_ev, 1)

        class UpSteps:

            def __init__(self, st, norm):
                self.st, self.norm = st, norm
                pair = [0, 1]
                self.prods = steps("dve", st.name + "_prod", [f"prod{b}" for b in pair])
                self.lows = steps("dve", st.name + "_low", [f"low{b}" for b in pair])
                self.silus = steps("act", st.name + "_silu", [f"silu{b}" for b in pair])
                self.highs = steps("act", st.name + "_high", [f"high{b}" for b in pair])
                self.order = {"dve": [(0, self.scale), (1, self.prod), "split", (2, self.low)],
                              "act": ["split", (1, self.silu), (2, self.high)],
                              "pool": ["split"] + [(0, lambda eng, it, u: None)]}

            def scale(self, eng, it, u):
                st, T = self.st, self.st.T
                if u == 0:
                    self.norm.ready(eng)
                group_done(eng, st, it, u)
                dst = (CV if u % 2 == 0 else SC)[u // 2][:, 0:T]
                leave(st, it, u, eng.tensor_tensor(dst, bank[st.banks[u]][:, 0:T], R[:, 0:T], ALU.mult))

            def silu(self, eng, it, u):
                b, T = u // 2, self.st.T
                if u % 2 == 0:
                    evacuated(eng, self.st, it, u)
                    self.silus.done(eng.activation(SG[b][:, 0:T], CV[b][:, 0:T], ACT.Silu), f"silu{b}")

            def prod(self, eng, it, u):
                b, T = u // 2, self.st.T
                if u % 2:
                    evacuated(eng, self.st, it, u)
                    self.silus.wait(eng, it, f"silu{b}")
                    self.prods.done(eng.tensor_tensor(PR[b][:, 0:T], SG[b][:, 0:T], SC[b][:, 0:T], ALU.mult),
                                    f"prod{b}")

            def high(self, eng, it, u):
                b, T = u // 2, self.st.T
                if u % 2:
                    self.prods.wait(eng, it, f"prod{b}")
                    self.highs.done(eng.activation(AH[:, bass.ds(it * 2 + b, 1), 0:T], PR[b][:, 0:T].unsqueeze(1),
                                                   ACT.Copy), f"high{b}")

            def low(self, eng, it, u):
                b, T, j = u // 2, self.st.T, it * 2 + u // 2
                if u % 2:
                    self.highs.wait(eng, it, f"high{b}")
                    self.lows.done(eng.tensor_tensor(AL[:, bass.ds(j, 1), 0:T], PR[b][:, 0:T].unsqueeze(1),
                                                     AH[:, bass.ds(j, 1), 0:T].bitcast(F32), ALU.subtract), f"low{b}")

            def rhs_wait(self, eng):
                def wait(k):
                    if k in (0, FC - 2, FC - 1):
                        last = {0: (self.st.iters - 2, "low1"), FC - 2: (self.st.iters - 1, "low0"),
                                FC - 1: (self.st.iters - 1, "low1")}[k]
                        self.lows.wait(eng, *last)
                return wait

        class ConvUpSteps(UpSteps):

            def __init__(self, st, norm, layer):
                self.st, self.norm, self.layer = st, norm, layer
                self.w, self.bias = f"fcw{layer}", f"fcb{layer}"
                pair = [0, 1]
                self.tap2s = steps("act", st.name + "_tap", [f"tap2_{u}" for u in range(4)])
                self.taps = steps("dve", st.name + "_tap", [f"tap{t}_{u}" for u in range(4) for t in (1, 0)])
                self.prods = steps("pool", st.name + "_prod", [f"prod{b}" for b in pair])
                self.lows = steps("pool", st.name + "_low", [f"low{b}" for b in pair])
                self.silus = steps("act", st.name + "_silu", [f"silu{b}" for b in pair])
                self.highs = steps("act", st.name + "_high", [f"high{b}" for b in pair])
                self.order = {"dve": [(0, self.scale), (1, self.tap), "split"],
                              "act": ["split", (0, self.tap2), (2, self.silu), (3, self.high)],
                              "pool": ["split", (2, self.prod), (3, self.low)]}

            def scale(self, eng, it, u):
                st, T = self.st, self.st.T
                if u == 0:
                    self.norm.ready(eng)
                self.taps.wait(eng, it, f"tap0_{(u - 2) % 4}", back=int(u < 2))
                group_done(eng, st, it, u)
                leave(st, it, u, eng.tensor_tensor(TP[u % 2][:, 3:3 + T], bank[st.banks[u]][:, 0:T], R[:, 0:T],
                                                   ALU.mult))

            def dst(self, u):
                return (CV if u % 2 == 0 else SC)[u // 2][:, 0:self.st.T]

            def tap2(self, eng, it, u):
                m, T = it * 4 + u, self.st.T
                evacuated(eng, self.st, it, u)
                if u % 2 == 0:
                    self.silus.wait(eng, it, f"silu{u // 2}", back=1)
                self.tap2s.done(eng.activation(self.dst(u), TP[u % 2][:, 3:3 + T], ACT.Identity,
                                               bias=v(self.bias, m), scale=v(self.w, m + 88)), f"tap2_{u}")

            def tap(self, eng, it, u):
                m, T, dst = it * 4 + u, self.st.T, self.dst(u)
                self.tap2s.wait(eng, it, f"tap2_{u}")
                self.taps.done(eng.scalar_tensor_tensor(dst, TP[u % 2][:, 2:2 + T], v(self.w, m + 44), dst, ALU.mult,
                                                        ALU.add), f"tap1_{u}")
                self.taps.wait(eng, it, f"tap1_{u}")
                self.taps.done(eng.scalar_tensor_tensor(dst, TP[u % 2][:, 1:1 + T], v(self.w, m), dst, ALU.mult,
                                                        ALU.add), f"tap0_{u}")

            def silu(self, eng, it, u):
                b, T = u // 2, self.st.T
                if u % 2 == 0:
                    self.taps.wait(eng, it, f"tap0_{u}")
                    self.silus.done(eng.activation(SG[b][:, 0:T], CV[b][:, 0:T], ACT.Silu), f"silu{b}")

            def prod(self, eng, it, u):
                b, T = u // 2, self.st.T
                if u % 2:
                    self.taps.wait(eng, it, f"tap0_{u}")
                    self.silus.wait(eng, it, f"silu{b}")
                    self.prods.done(eng.tensor_tensor(PR[b][:, 0:T], SG[b][:, 0:T], SC[b][:, 0:T], ALU.mult),
                                    f"prod{b}")

        class NormedSteps:

            def __init__(self, st, gain, factor):
                self.st, self.gain, self.factor = st, gain, factor
                G = st.groups
                self.G = G
                self.dv = steps("dve", st.name, [f"acc{g}" for g in range(G)])
                self.ac = steps("act", st.name, [f"sq{g}" for g in range(G)])
                st.dv, st.acc_last = self.dv, f"acc{G - 1}"

            def before(self, eng):
                eng.memset(ACC[:, :], 0.0).then_inc(s_ms, 1)
                n_ms[0] += 1
                eng.wait_ge(s_ms, n_ms[0])

            def dve(self, eng, it, u):
                st, T = self.st, self.st.T
                for g in range(self.G):
                    if st.unit_of[g] == u:
                        m = it * self.G + g
                        self.ac.wait(eng, it, f"sq{g}")
                        leave(st, it, g, eng.tensor_scalar(YG[:, bass.ds(m, 1), 0:T],
                                                           bank[st.banks[g]][:, 0:T].unsqueeze(1), v(self.gain, m),
                                                           self.factor, ALU.mult, ALU.mult))
                        self.dv.wait(eng, it, f"acc{(g - 1) % self.G}", back=int(g == 0))
                        self.dv.done(eng.tensor_tensor(ACC[:, 0:T], ACC[:, 0:T], SQB[g % 2][:, 0:T], ALU.add),
                                     f"acc{g}")

            def act(self, eng, it, u):
                st, T = self.st, self.st.T
                for g in range(self.G):
                    if st.unit_of[g] == u:
                        group_done(eng, st, it, g)
                        self.dv.wait(eng, it, f"acc{(g - 2) % self.G}", back=int(g < 2))
                        self.ac.done(eng.activation(SQB[g % 2][:, 0:T], bank[st.banks[g]][:, 0:T], ACT.Square),
                                     f"sq{g}")

            def pool(self, eng, it, u):
                pass

        class AddSteps:

            def __init__(self, st, norms):
                self.st, self.norms = st, norms
                G = self.G = st.groups
                n = range(len(norms))
                self.dv = steps("dve", st.name, [x for g in range(G) for x in ([f"low{i}_{g}" for i in n]
                                                                               + [f"acc{g}"])])
                self.ac = steps("act", st.name, [x for g in range(G) for x in ([f"high{i}_{g}" for i in n]
                                                                               + [f"sq{g}"])])
                st.dv, st.acc_last = self.dv, f"acc{G - 1}"

            def before(self, eng):
                eng.memset(ACC[:, :], 0.0).then_inc(s_ms, 1)
                n_ms[0] += 1
                eng.wait_ge(s_ms, n_ms[0])

            def dve(self, eng, it, u):
                st, T = self.st, self.st.T
                for g in range(self.G):
                    if st.unit_of[g] != u:
                        continue
                    m = it * self.G + g
                    h = H[:, bass.ds(m, 1), META:TM]
                    group_done(eng, st, it, g)
                    leave(st, it, g, eng.tensor_tensor(h, bank[st.banks[g]][:, 0:T].unsqueeze(1), h, ALU.add))
                    for i, (gain, hi, lo) in enumerate(self.norms):
                        self.ac.wait(eng, it, f"high{i}_{g}")
                        self.dv.done(eng.scalar_tensor_tensor(lo[:, bass.ds(m, 1), 0:T], h, v(gain, m),
                                                              hi[:, bass.ds(m, 1), 0:T].bitcast(F32), ALU.mult,
                                                              ALU.subtract), f"low{i}_{g}")
                    self.ac.wait(eng, it, f"sq{g}")
                    self.dv.wait(eng, it, f"acc{(g - 1) % self.G}", back=int(g == 0))
                    self.dv.done(eng.tensor_tensor(ACC[:, 0:T], ACC[:, 0:T], SQB[g % 2][:, 0:T], ALU.add), f"acc{g}")

            def act(self, eng, it, u):
                st, T = self.st, self.st.T
                for g in range(self.G):
                    if st.unit_of[g] != u:
                        continue
                    m = it * self.G + g
                    h = H[:, bass.ds(m, 1), META:TM]
                    self.dv.wait(eng, it, f"acc{(g - 2) % self.G}", back=int(g < 2))
                    evacuated(eng, st, it, g)
                    for i, (gain, hi, lo) in enumerate(self.norms):
                        self.ac.done(eng.activation(hi[:, bass.ds(m, 1), 0:T], h, ACT.Identity, bias=0.0,
                                                    scale=v(gain, m)), f"high{i}_{g}")
                    self.ac.done(eng.activation(SQB[g % 2][:, 0:T].unsqueeze(1), h, ACT.Square), f"sq{g}")

            def pool(self, eng, it, u):
                pass

        class ConvSteps:

            def __init__(self, st, norm, w, bias, out, m0, M):
                self.st, self.norm, self.w, self.bias, self.out, self.m0, self.M = st, norm, w, bias, out, m0, M
                self.tap3s = steps("act", st.name + "_tap", [f"tap3_{u}" for u in range(4)])
                self.taps = steps("dve", st.name, [f"tap{t}_{u}" for u in range(4) for t in (2, 1, 0)])
                self.silus = steps("act", st.name, [f"silu{u}" for u in range(4)])
                self.order = {"dve": [(0, self.scale), (1, self.tap), "split"],
                              "act": ["split", (0, self.tap3), (2, self.silu)],
                              "pool": ["split", (0, lambda eng, it, u: None)]}

            def scale(self, eng, it, u):
                st, T = self.st, self.st.T
                if u == 0:
                    self.norm.ready(eng)
                self.taps.wait(eng, it, f"tap0_{(u - 2) % 4}", back=int(u < 2))
                group_done(eng, st, it, u)
                leave(st, it, u, eng.tensor_tensor(TP[u % 2][:, 3:3 + T], bank[st.banks[u]][:, 0:T], R[:, 0:T],
                                                   ALU.mult))

            def tap3(self, eng, it, u):
                m, T = it * 4 + u + self.m0, self.st.T
                evacuated(eng, self.st, it, u)
                self.silus.wait(eng, it, f"silu{u}", back=1)
                self.tap3s.done(eng.activation(CONV[u][:, 0:T], TP[u % 2][:, 3:3 + T], ACT.Identity,
                                               bias=v(self.bias, m) if self.bias else 0.0,
                                               scale=v(self.w, m + 3 * self.M)), f"tap3_{u}")

            def tap(self, eng, it, u):
                m, T, dst = it * 4 + u + self.m0, self.st.T, CONV[u][:, 0:self.st.T]
                self.tap3s.wait(eng, it, f"tap3_{u}")
                for t in (2, 1, 0):
                    self.taps.done(eng.scalar_tensor_tensor(dst, TP[u % 2][:, t:t + T], v(self.w, m + t * self.M), dst,
                                                            ALU.mult, ALU.add), f"tap{t}_{u}")
                    if t:
                        self.taps.wait(eng, it, f"tap{t}_{u}")

            def silu(self, eng, it, u):
                T = self.st.T
                self.taps.wait(eng, it, f"tap0_{u}")
                self.silus.done(eng.activation(self.out(it * 4 + u), CONV[u][:, 0:T].unsqueeze(1), ACT.Silu),
                                f"silu{u}")

        class ScaleSteps:

            def __init__(self, st, norm, out, func=None):
                self.st, self.norm, self.out, self.func = st, norm, out, func
                self.funcs = steps("act", st.name, [f"func{u}" for u in range(4)]) if func else None
                self.order = {"dve": [(0, self.scale), "split"], "act": ["split", (1, self.apply)],
                              "pool": ["split", (0, lambda eng, it, u: None)]}

            def scale(self, eng, it, u):
                st, T = self.st, self.st.T
                if u == 0:
                    self.norm.ready(eng)
                group_done(eng, st, it, u)
                leave(st, it, u, eng.tensor_tensor(self.out(it * 4 + u), bank[st.banks[u]][:, 0:T].unsqueeze(1),
                                                   R[:, TM - T if st.off else 0:][:, 0:T].unsqueeze(1), ALU.mult))

            def apply(self, eng, it, u):
                if self.func:
                    evacuated(eng, self.st, it, u)
                    o = self.out(it * 4 + u)
                    self.funcs.done(eng.activation(o, o, self.func), f"func{u}")

        QK, VT, OG, NMB, ENB = carve(big, big_size, mQK=([P, 8, TM], F32), mVT=([P, 8, TM], F32),
                                     mOG=([P, 8, SEQ], F32), mNMB=([P, 8, SEQ], F32), mENB=([P, 8, SEQ], F32))
        GI, GF, G1, G2, G3, MX = carve(spare, spare_size, **{n: ([A_HEADS, TM], F32) for n in
                                                             ("mGI", "mGF", "mG1", "mG2", "mG3", "mMX")})

        class MGateSteps:

            def __init__(self, st, norm):
                self.st, self.norm = st, norm
                self.dv = steps("dve", st.name, ["one", "gi", "bi", "bf", "neg", "lf", "F", "a", "M", "nm", "negM"])
                self.ac = steps("act", st.name, ["abs", "exp", "ln", "enm"])
                self.ms = sem("dma_mgate_out")
                self.mb = sem("dma_mgate_in")
                self.pe_done = sem("pe_mgate")

            def dve(self, eng, it, u):
                if u != 3:
                    return
                st, d, ac, n = self.st, self.dv, self.ac, A_HEADS
                eng.wait_ge(s_bias, 16)
                d.done(eng.memset(G3[:, :], 1.0), "one")
                self.norm.ready(eng)
                group_done(eng, st, it, 0)
                b = bank[st.banks[0]]
                d.done(eng.tensor_tensor(GI[:, :], b[0:n, 0:TM], R[0:n, :], ALU.mult), "gi")
                leave(st, it, 0, eng.tensor_tensor(GF[:, :], b[32:32 + n, 0:TM], R[32:32 + n, :], ALU.mult))
                d.wait(eng, it, "gi")
                d.done(eng.tensor_scalar(GI[:, :], GI[:, :], vec[0:n, VEC["gate"]:VEC["gate"] + 1], None, ALU.add), "bi")
                evacuated(eng, st, it, 0)
                d.done(eng.tensor_scalar(GF[:, :], GF[:, :], vec[0:n, VEC["gate"] + 1:VEC["gate"] + 2], None,
                                         ALU.add), "bf")
                d.wait(eng, it, "bf")
                d.done(eng.tensor_scalar(MX[:, :], GF[:, :], 0.0, None, ALU.min), "neg")
                ac.wait(eng, it, "ln")
                d.wait(eng, it, "neg")
                d.done(eng.tensor_tensor(G1[:, :], MX[:, :], G2[:, :], ALU.subtract), "lf")
                d.wait(eng, it, "lf")
                d.done(eng.tensor_tensor_scan(GF[:, :], G3[:, :], G1[:, :], 0.0, ALU.mult, ALU.add), "F")
                d.wait(eng, it, "F")
                d.done(eng.tensor_tensor(GI[:, :], GI[:, :], GF[:, :], ALU.subtract), "a")
                d.wait(eng, it, "a")
                d.done(eng.tensor_tensor_scan(MX[:, :], G3[:, :], GI[:, :], 0.0, ALU.mult, ALU.max), "M")
                d.wait(eng, it, "M")
                d.done(eng.tensor_tensor(G1[:, :], GF[:, :], MX[:, :], ALU.add), "nm")
                d.done(eng.tensor_scalar(G2[:, :], MX[:, :], -1.0, None, ALU.mult), "negM")

            def act(self, eng, it, u):
                if u != 3:
                    return
                d, ac = self.dv, self.ac
                d.wait(eng, it, "bf")
                ac.done(eng.activation(G1[:, :], GF[:, :], ACT.Abs), "abs")
                ac.wait(eng, it, "abs")
                ac.done(eng.activation(G2[:, :], G1[:, :], ACT.Exp, scale=-1.0), "exp")
                ac.wait(eng, it, "exp")
                ac.done(eng.activation(G2[:, :], G2[:, :], ACT.Ln, bias=1.0), "ln")
                d.wait(eng, it, "nm")
                ac.done(eng.activation(G1[:, :], G1[:, :], ACT.Exp, scale=-1.0), "enm")

            def pool(self, eng, it, u):
                if u != 3:
                    return
                self.dv.wait(eng, it, "negM")
                eng.dma_start(mx_d[0], G2[:, :]).then_inc(self.ms, 16)
                self.ac.wait(eng, it, "enm")
                eng.dma_start(mx_d[1], G1[:, :]).then_inc(self.ms, 16)
                eng.wait_ge(self.ms, 32)
                for i, dst in enumerate((NMB, ENB)):
                    eng.dma_start(dst[:, :, :], mx_d[i, :, META:TM].partition_broadcast(P)).then_inc(self.mb, 16)

            def pe(self, eng):
                self.dv.wait(eng, 0, "a")
                for s, (t, n) in enumerate(TOKENS):
                    eng.transpose(bank[5][0:n, s * A_HEADS:(s + 1) * A_HEADS], GI[:, t:t + n],
                                  ident[0:A_HEADS, 0:A_HEADS]).then_inc(self.pe_done, 1)

        TOKENS = [(0, META), (META, P), (META + P, P)]
        mc = carve(work, work_size, mQKs=([P, 2, TM], F32), mVs=([P, 2, TM], F32), mVN0=([P, 3, P], F32),
                   mVN1=([P, 3, P], F32), mDB0=([P, 3 * P], F32), mDB1=([P, 3 * P], F32), mDA0=([META, SEQ], F32),
                   mDA1=([META, SEQ], F32), mAD0=([P, SEQ], F32), mAD1=([P, SEQ], F32), mY0=([P, SEQ], F32),
                   mY1=([P, SEQ], F32))
        QKs, Vs, VN, DB, DA, AD, YM = mc[0], mc[1], mc[2:4], mc[4:6], mc[6:8], mc[8:10], mc[10:12]
        two = (0, 1)

        def names(*parts):
            return [f"{n}{i}" for n in parts for i in two]

        class MCore:

            def __init__(self, gate, last_stage, next_stage):
                self.gate, self.prev, self.next = gate, last_stage, next_stage
                self.aT = sem("act_aT")
                self.ac = steps("act", "mcore", ["qk", "v"] + names("vnA", "vnB", "expB", "expA", "abs", "high"))
                self.dv = steps("dve", "mcore", names("dB", "dC", "dA", "wB", "wA", "max", "rec", "og", "y", "low"))
                self.po = steps("pool", "mcore", names("mask"))
                self.pe_ = steps("pe", "mcore", names("vT", "qkB", "num", "den"))

            def act(self, eng):
                a, d, o, p = self.ac, self.dv, self.po, self.pe_
                eng.wait_ge(self.gate.pe_done, 3)
                eng.activation(AC[0:META, 0, :], bank[5][0:META, 0:A_HEADS], ACT.Copy).then_inc(self.aT, 1)
                eng.activation(AC[:, 1:3, :], bank[5][:, A_HEADS:3 * A_HEADS].rearrange("p (s h) -> p s h", s=2),
                               ACT.Copy).then_inc(self.aT, 1)
                evacuated(eng, self.prev, self.prev.iters - 1, 3)
                self.qk_ready(eng)
                with eng.Fori(0, A_HEADS // 2) as it:
                    qk = QK[:, :, :].rearrange("p (x j) t -> p x j t", x=2)
                    p.wait(eng, it, "qkB1", back=1)
                    a.done(eng.activation(QKs[:, :, :].unsqueeze(2), qk[:, :, bass.ds(it, 1), :], ACT.Copy), "qk")
                    a.done(eng.activation(Vs[:, :, :], VT[:, bass.ds(it * 2, 2), :], ACT.Copy), "v")
                    for i in two:
                        p.wait(eng, it, f"vT{i}")
                        p.wait(eng, it, f"num{i}", back=1)
                        a.done(eng.activation(VN[i][0:META, 0, :], bank[i][0:META, 0:P], ACT.Copy), f"vnA{i}")
                    for i in two:
                        a.done(eng.activation(VN[i][:, 1:3, :], bank[i][:, P:3 * P].rearrange("p (s e) -> p s e", s=2),
                                              ACT.Copy), f"vnB{i}")
                    for i in two:
                        d.wait(eng, it, f"dC{i}")
                        a.done(eng.activation(DB[i][:, :], DB[i][:, :], ACT.Exp), f"expB{i}")
                    for i in two:
                        d.wait(eng, it, f"dA{i}")
                        a.done(eng.activation(DA[i][:, :], DA[i][:, :], ACT.Exp), f"expA{i}")
                    for i in two:
                        p.wait(eng, it, f"den{i}")
                        a.done(eng.activation(AD[i][:, :], bank[7 - 3 * i][:, 0:SEQ], ACT.Abs), f"abs{i}")
                    for i in two:
                        d.wait(eng, it, f"y{i}")
                        a.done(eng.activation(XH[:, bass.ds(it * 2 + i, 1), 0:SEQ], YM[i][:, :].unsqueeze(1),
                                              ACT.Copy), f"high{i}")

            def dve(self, eng):
                a, d, o, p = self.ac, self.dv, self.po, self.pe_
                eng.wait_ge(self.gate.mb, 32)
                eng.wait_ge(self.aT, 2)
                self.og_ready(eng)
                with eng.Fori(0, A_HEADS // 2) as it:
                    def m(i, c0, c1):
                        return NMB[:, bass.ds(it * 2 + i, 1), c0:c1]
                    for i in two:
                        p.wait(eng, it, f"den{i}", back=1)
                        d.done(eng.tensor_scalar(DB[i][:, 0:SEQ].unsqueeze(1), m(i, 0, SEQ),
                                                 AC[:, 1, bass.ds(it * 2 + i, 1)], 0.0, ALU.add, ALU.min), f"dB{i}")
                    for i in two:
                        d.done(eng.tensor_scalar(DB[i][:, SEQ:3 * P].unsqueeze(1), m(i, P, SEQ),
                                                 AC[:, 2, bass.ds(it * 2 + i, 1)], 0.0, ALU.add, ALU.min), f"dC{i}")
                    for i in two:
                        d.done(eng.tensor_scalar(DA[i][:, :].unsqueeze(1), NMB[0:META, bass.ds(it * 2 + i, 1), :],
                                                 AC[0:META, 0, bass.ds(it * 2 + i, 1)], 0.0, ALU.add, ALU.min),
                               f"dA{i}")
                    for i in two:
                        p.wait(eng, it, f"qkB{i}")
                        o.wait(eng, it, f"mask{i}")
                        d.done(eng.scalar_tensor_tensor(DB[i][:, :], bank[2 + i][:, 0:3 * P], A_DK ** -0.5, DB[i][:, :],
                                                        ALU.mult, ALU.mult), f"wB{i}")
                    for i in two:
                        a.wait(eng, it, f"expA{i}")
                        d.done(eng.scalar_tensor_tensor(DA[i][:, :], bank[5 + i][0:META, SEQ:2 * SEQ],
                                                        A_DK ** -0.5, DA[i][:, :], ALU.mult, ALU.mult), f"wA{i}")
                    for i in two:
                        a.wait(eng, it, f"abs{i}")
                        d.done(eng.tensor_tensor(AD[i][:, :].unsqueeze(1), AD[i][:, :].unsqueeze(1),
                                                 ENB[:, bass.ds(it * 2 + i, 1), :], ALU.max), f"max{i}")
                    for i in two:
                        d.wait(eng, it, f"max{i}")
                        d.done(eng.reciprocal(AD[i][:, :], AD[i][:, :]), f"rec{i}")
                    for i in two:
                        d.wait(eng, it, f"rec{i}")
                        d.done(eng.tensor_tensor(AD[i][:, :].unsqueeze(1), AD[i][:, :].unsqueeze(1),
                                                 OG[:, bass.ds(it * 2 + i, 1), :], ALU.mult), f"og{i}")
                    for i in two:
                        d.wait(eng, it, f"og{i}")
                        p.wait(eng, it, f"num{i}")
                        a.wait(eng, it, f"high{i}", back=1)
                        d.done(eng.tensor_tensor(YM[i][:, :], bank[5 + i][:, 0:SEQ], AD[i][:, :], ALU.mult), f"y{i}")
                    for i in two:
                        a.wait(eng, it, f"high{i}")
                        d.wait(eng, it, f"y{i}")
                        d.done(eng.tensor_tensor(XL[:, bass.ds(it * 2 + i, 1), 0:SEQ], YM[i][:, :].unsqueeze(1),
                                                 XH[:, bass.ds(it * 2 + i, 1), 0:SEQ].bitcast(F32), ALU.subtract),
                               f"low{i}")

            def pool(self, eng):
                with eng.Fori(0, A_HEADS // 2) as it:
                    for i in two:
                        self.ac.wait(eng, it, f"expB{i}")
                        dd = DB[i][:, :].rearrange("p (s t) -> p s t", t=P)[:, 0:3:2, :]
                        self.po.done(eng.tensor_tensor(dd, dd, causal.unsqueeze(1).to_broadcast([P, 2, P]), ALU.mult),
                                     f"mask{i}")

            def pe(self, eng):
                a, d, p = self.ac, self.dv, self.pe_
                evacuated(eng, self.prev, self.prev.iters - 1, 3)
                eng.wait_ge(self.aT, 2)
                with eng.Fori(0, A_HEADS // 2) as it:
                    a.wait(eng, it, "v")
                    for i in two:
                        a.wait(eng, it, f"vnB{i}", back=1)
                        for s, (t, n) in enumerate(TOKENS):
                            mm = eng.transpose(bank[i][0:n, s * P:(s + 1) * P], Vs[:, i, t:t + n], ident)
                        p.done(mm, f"vT{i}")
                    for i in two:
                        h0 = 64 * i
                        d.wait(eng, it, f"y{i}", back=1)
                        q, k = QKs[h0:h0 + 64, 0, :], QKs[h0:h0 + 64, 1, :]
                        eng.matmul(bank[2 + i][:, 0:SEQ], k[:, META:META + P], q[:, META:TM], start=True, stop=True)
                        eng.matmul(bank[5 + i][0:META, SEQ:2 * SEQ], k[:, 0:META], q[:, META:TM],
                                   start=True, stop=True)
                        p.done(eng.matmul(bank[2 + i][:, SEQ:3 * P], k[:, META + P:TM], q[:, META + P:TM],
                                          start=True, stop=True), f"qkB{i}")
                    for i in two:
                        d.wait(eng, it, f"y{i}", back=1)
                        d.wait(eng, it, f"wA{i}")
                        a.wait(eng, it, f"vnB{i}")
                        out = bank[5 + i]
                        eng.matmul(out[:, 0:SEQ], VN[i][0:META, 0, :], DA[i][:, :], start=True, stop=False)
                        eng.matmul(out[:, 0:SEQ], VN[i][:, 1, :], DB[i][:, 0:SEQ], start=False, stop=False)
                        p.done(eng.matmul(out[:, P:SEQ], VN[i][:, 2, :], DB[i][:, SEQ:3 * P], start=False, stop=True),
                               f"num{i}")
                    for i in two:
                        a.wait(eng, it, f"abs{i}", back=1)
                        den = bank[7 - 3 * i]
                        eng.matmul(den[:, 0:SEQ], ones[0:META, :], DA[i][:, :], start=True, stop=False)
                        eng.matmul(den[:, 0:SEQ], ones[:, :], DB[i][:, 0:SEQ], start=False, stop=False)
                        p.done(eng.matmul(den[:, P:SEQ], ones[:, :], DB[i][:, SEQ:3 * P], start=False,
                                          stop=True), f"den{i}")

            def rhs_wait(self, eng):
                def wait(k):
                    if k % 2 == 0:
                        self.dv.wait(eng, k // 2, "low1")
                return wait

        dQK, dVT, GCB = carve(ext, ext_size, dQK=([P, 16, SEQ], F32), dVT=([P, 16, SEQ], F32), dGCB=([P, 16, SEQ], F32))
        dB, dA, d1, d2, dO, dG, dE = carve(spare, spare_size, **{n: ([GDN_V, SEQ if n != "dE" else 8], F32) for n in
                                                                  ("dB", "dA", "d1", "d2", "dO", "dG", "dE")})
        HG = 4
        four = range(HG)

        class GGateSteps:

            def __init__(self, st, norm):
                self.st, self.norm = st, norm
                self.dv = steps("dve", st.name, ["one", "b", "x", "pos", "b1", "beta", "sp", "g", "gc0", "gc1"])
                self.ac = steps("act", st.name, ["ea", "eb", "abs", "exp", "ln"])
                self.ms, self.mb, self.pe_done = sem("dma_ggate_out"), sem("dma_ggate_in"), sem("pe_ggate")

            def dve(self, eng, it, u):
                if u != 3:
                    return
                st, d, ac, n = self.st, self.dv, self.ac, GDN_V
                d.done(eng.memset(dO[:, :], 1.0), "one")
                self.norm.ready(eng)
                group_done(eng, st, it, 0)
                b = bank[st.banks[0]]
                d.done(eng.tensor_tensor(dB[:, :], b[0:n, 0:SEQ], R[0:n, 0:SEQ], ALU.mult), "b")
                leave(st, it, 0, eng.tensor_tensor(dA[:, :], b[32:32 + n, 0:SEQ], R[32:32 + n, 0:SEQ], ALU.mult))
                evacuated(eng, st, it, 0)
                d.done(eng.tensor_scalar(dA[:, :], dA[:, :], vec[0:n, VEC["dn"] + 1:VEC["dn"] + 2], None, ALU.add), "x")
                d.wait(eng, it, "x")
                d.done(eng.tensor_scalar(dG[:, :], dA[:, :], 0.0, None, ALU.max), "pos")
                ac.wait(eng, it, "eb")
                d.done(eng.tensor_scalar(dB[:, :], dB[:, :], 1.0, None, ALU.add), "b1")
                d.wait(eng, it, "b1")
                d.done(eng.reciprocal(dB[:, :], dB[:, :]), "beta")
                ac.wait(eng, it, "ln")
                d.done(eng.tensor_tensor(dG[:, :], dG[:, :], d2[:, :], ALU.add), "sp")
                d.wait(eng, it, "sp")
                d.done(eng.tensor_scalar(dG[:, :], dG[:, :], dE[:, 0:1], -1.0, ALU.mult, ALU.mult), "g")
                d.wait(eng, it, "g")
                for c in (0, 1):
                    s = slice(c * P, (c + 1) * P)
                    d.done(eng.tensor_tensor_scan(dA[:, s], dO[:, s], dG[:, s], 0.0, ALU.mult, ALU.add), f"gc{c}")

            def act(self, eng, it, u):
                if u != 3:
                    return
                d, ac = self.dv, self.ac
                ac.done(eng.activation(dE[:, 0:1], vec[0:GDN_V, VEC["dn"]:VEC["dn"] + 1], ACT.Exp), "ea")
                d.wait(eng, it, "b")
                ac.done(eng.activation(dB[:, :], dB[:, :], ACT.Exp, scale=-1.0), "eb")
                d.wait(eng, it, "x")
                ac.done(eng.activation(d1[:, :], dA[:, :], ACT.Abs), "abs")
                ac.wait(eng, it, "abs")
                ac.done(eng.activation(d2[:, :], d1[:, :], ACT.Exp, scale=-1.0), "exp")
                ac.wait(eng, it, "exp")
                ac.done(eng.activation(d2[:, :], d2[:, :], ACT.Ln, bias=1.0), "ln")

            def pool(self, eng, it, u):
                if u != 3:
                    return
                self.dv.wait(eng, it, "gc1")
                eng.dma_start(gc_d, dA[:, :]).then_inc(self.ms, 16)
                eng.wait_ge(self.ms, 16)
                eng.dma_start(GCB[:, :, :], gc_d.partition_broadcast(P)).then_inc(self.mb, 16)

            def pe(self, eng):
                self.dv.wait(eng, 0, "gc1")
                for c in (0, 1):
                    for q, src in enumerate((dA, dB)):
                        o = (2 * c + q) * GDN_V
                        eng.transpose(bank[5][:, o:o + GDN_V], src[:, c * P:(c + 1) * P],
                                      ident[0:GDN_V, 0:GDN_V]).then_inc(self.pe_done, 1)

        t4 = ([P, HG, P], F32)
        KN, RT, VG, VB0, VB1, CG, KC, NB, EGC = carve(xreg, xreg_size, gKN=([P, 2, 2, SEQ], F32), gRT=([P, 2, 2, SEQ], F32),
                                     gVG=([P, HG, SEQ], F32), gVB0=t4, gVB1=t4,
                                     gCG=([P, 2, 2, HG], F32), gKC=([P, HG], F32), gNB=([P, HG], F32),
                                     gEGC=([P, HG], F32))
        _, Lm0, Lm1, OT = carve(xreg, xreg_size, gx0=([P, 2, 2, SEQ], F32), gL0=t4, gL1=t4, gOT=([P, HG, SEQ], F32))
        _, SQ2 = carve(xreg, xreg_size, gx1=([P, 2, 2, SEQ], F32), gSQ2=([P, HG, SEQ], F32))
        E0, E1, EA0, EA1, T0, T1, U0, U1, Y0, Y1, KD, QD, _ = carve(
            work, work_size, gE0=t4, gE1=t4, gEA0=t4, gEA1=t4, gT0=t4, gT1=t4, gU0=t4, gU1=t4, gY0=t4, gY1=t4,
            gKD=t4, gQD=t4, gEnd=([P, 8], F32))
        RO, = carve(work, work_size, gRO=([P, HG, SEQ], F32))
        _, _, _, _, S0, R1 = carve(work, work_size, gy0=t4, gy1=t4, gy2=t4, gy3=t4, gS0=t4, gR1=t4)
        VB, L, E, EA, T_, U_, Y_ = (VB0, VB1), (Lm0, Lm1), (E0, E1), (EA0, EA1), (T0, T1), (U0, U1), (Y0, Y1)

        def heads(ap, n):
            return ap.rearrange("p (h c) -> p h c", h=n)

        def nn(*parts):
            return [f"{x}{n}" for x in parts for n in (0, 1)]

        class GCore:

            def __init__(self, gate, prev):
                self.gate, self.prev, self.cols = gate, prev, sem("act_cols")
                lv = range(1, LEVELS)
                self.ac = steps("act", "gcore", ["sq", "ln0", "ln1", "rs", "vg", "kce", "egc"] + nn("ex", "exa") + ["eg"]
                                + nn("u") + [f"yc{l}_{n}" for l in lv for n in (0, 1)]
                                + ["vnc0", "sc", "ot0", "vnc1", "ot1", "sq2", "ln2_0", "ln2_1", "ro", "high"])
                self.dv = steps("dve", "gcore", ["cg", "kc"] + nn("e", "ea") + ["kn", "qn", "nb", "vb0", "vb1", "kd"]
                                + nn("m") + nn("t") + nn("at")
                                + [f"{x}{l}_{n}" for l in lv for n in (0, 1) for x in (("dt", "du") if l < LEVELS - 1
                                                                                     else ("du",))]
                                + ["r1", "yo", "yz", "low"])
                self.po = steps("pool", "gcore", nn("em") + [f"l0_{n}" for n in (0, 1)] + ["l1_0", "l1_1", "qd"]
                                + [f"l{l}_{n}" for l in lv if l > 1 for n in (0, 1)])
                self.pe_ = steps("pe", "gcore", ["ss0", "ss1", "vt0", "vt1", "kt", "gr0", "gr1", "tt0", "tt1"]
                                 + [f"{x}{l}_{n}" for l in lv for x, n in ((("y", 0), ("y", 1), ("pp", 0), ("pp", 1)))]
                                 + ["vn0", "s", "o0", "ks", "vn1", "o1", "oss0", "oss1"])

            def act(self, eng):
                a, d, o, p = self.ac, self.dv, self.po, self.pe_
                eng.wait_ge(self.gate.pe_done, 4)
                eng.activation(COLS[:, :, :, :], bank[5][:, 0:4 * GDN_V].rearrange("p (c q h) -> p c q h", c=2, q=2),
                               ACT.Copy).then_inc(self.cols, 1)
                evacuated(eng, self.prev, self.prev.iters - 1, 3)
                self.qkv_ready(eng)
                with eng.Fori(0, GDN_V // HG) as it:
                    p.wait(eng, it, "oss1", back=1)
                    a.done(eng.activation(RT[:, :, :, :].rearrange("p a b t -> p (a b) t"),
                                          dQK[:, bass.ds(it * 4, 4), :], ACT.Square), "sq")
                    for i in two:
                        p.wait(eng, it, f"ss{i}")
                        a.done(eng.activation(RT[:, i, :, :], bank[i][:, :].rearrange("p (b t) -> p b t", b=2), ACT.Ln,
                                              bias=eps), f"ln{i}")
                    a.wait(eng, it, "ln1")
                    a.done(eng.activation(RT[:, :, :, :], RT[:, :, :, :], ACT.Exp, scale=-0.5), "rs")
                    d.wait(eng, it, "low", back=1)
                    a.done(eng.activation(VG[:, :, :], dVT[:, bass.ds(it * HG, HG), :], ACT.Copy), "vg")
                    d.wait(eng, it, "kc")
                    a.done(eng.activation(KC[:, :], KC[:, :], ACT.Exp), "kce")
                    a.done(eng.activation(EGC[:, :], CG[:, 1, 0, :], ACT.Exp), "egc")
                    for n in two:
                        d.wait(eng, it, f"e{n}")
                        a.done(eng.activation(E[n][:, :, :], E[n][:, :, :], ACT.Exp, scale=-1.0), f"ex{n}")
                    for n in two:
                        d.wait(eng, it, f"ea{n}")
                        a.done(eng.activation(EA[n][:, :, :], EA[n][:, :, :], ACT.Exp), f"exa{n}")
                    a.done(eng.activation(QD[:, :, :], GCB[:, bass.ds(it * HG, HG), P:SEQ], ACT.Exp), "eg")
                    for n in two:
                        p.wait(eng, it, f"tt{n}")
                        a.done(eng.activation(U_[n][:, :, :], heads(bank[n][:, :], HG), ACT.Copy), f"u{n}")
                    for l in range(1, LEVELS):
                        for n in two:
                            p.wait(eng, it, f"y{l}_{n}")
                            a.done(eng.activation(Y_[n][:, :, :], heads(bank[n][:, :], HG), ACT.Copy), f"yc{l}_{n}")
                    p.wait(eng, it, "vn0")
                    a.done(eng.activation(Y_[0][:, :, :], heads(bank[5][:, :], HG), ACT.Copy), "vnc0")
                    p.wait(eng, it, "s")
                    a.done(eng.activation(S0[:, :, :], heads(bank[1][:, :], HG), ACT.Copy), "sc")
                    p.wait(eng, it, "o0")
                    a.done(eng.activation(OT[:, :, 0:P], heads(bank[6][:, :], HG), ACT.Copy), "ot0")
                    p.wait(eng, it, "vn1")
                    a.done(eng.activation(Y_[1][:, :, :], heads(bank[2][:, :], HG), ACT.Copy), "vnc1")
                    p.wait(eng, it, "o1")
                    a.done(eng.activation(OT[:, :, P:SEQ], heads(bank[3][:, :], HG), ACT.Copy), "ot1")
                    a.wait(eng, it, "ot1")
                    a.done(eng.activation(SQ2[:, :, :], OT[:, :, :], ACT.Square), "sq2")
                    for i in two:
                        p.wait(eng, it, f"oss{i}")
                        a.done(eng.activation(RO[:, 2 * i:2 * i + 2, :], bank[5 + i][:, :].rearrange(
                            "p (h t) -> p h t", h=2), ACT.Ln, bias=eps, scale=1.0 / P), f"ln2_{i}")
                    a.wait(eng, it, "ln2_1")
                    a.done(eng.activation(RO[:, :, :], RO[:, :, :], ACT.Exp, scale=-0.5), "ro")
                    d.wait(eng, it, "yz")
                    a.done(eng.activation(YH[:, bass.ds(it * HG, HG), :], OT[:, :, :], ACT.Copy), "high")

            def dve(self, eng):
                a, d, o, p = self.ac, self.dv, self.po, self.pe_
                eng.wait_ge(self.gate.mb, 16)
                eng.wait_ge(self.cols, 1)
                self.z_ready(eng)
                with eng.Fori(0, GDN_V // HG) as it:
                    g = [GCB[:, bass.ds(it * HG + h, 1), :] for h in four]
                    d.done(eng.tensor_copy(CG[:, :, :, :], COLS[:, :, :, bass.ds(it * HG, HG)]), "cg")
                    d.wait(eng, it, "cg")
                    d.done(eng.tensor_tensor(KC[:, :].unsqueeze(2), GCB[:, bass.ds(it * HG, HG), P - 1:P],
                                             CG[:, 0, 0, :].unsqueeze(2), ALU.subtract), "kc")
                    for n in two:
                        for h in four:
                            ins = eng.tensor_scalar(E[n][:, h:h + 1, :], g[h][:, :, n * P:(n + 1) * P],
                                                    CG[:, n, 0, h:h + 1], 0.0, ALU.subtract, ALU.max)
                        d.done(ins, f"e{n}")
                    for n in two:
                        for h in four:
                            ins = eng.tensor_scalar(EA[n][:, h:h + 1, :], g[h][:, :, n * P:(n + 1) * P],
                                                    CG[:, n, 0, h:h + 1], 0.0, ALU.subtract, ALU.min)
                        d.done(ins, f"ea{n}")
                    qk = dQK[:, bass.ds(it * 4, 4), :]
                    a.wait(eng, it, "rs")
                    o.wait(eng, it, "qd", back=1)
                    kn4 = KN[:, :, :, :].rearrange("p a b t -> p (a b) t")
                    rt4 = RT[:, :, :, :].rearrange("p a b t -> p (a b) t")
                    d.done(eng.tensor_tensor(kn4[:, 0:4:2, :], qk[:, 0:4:2, :], rt4[:, 0:4:2, :], ALU.mult), "kn")
                    d.done(eng.scalar_tensor_tensor(kn4[:, 1:4:2, :], qk[:, 1:4:2, :], float(P) ** -0.5,
                                                    rt4[:, 1:4:2, :], ALU.mult, ALU.mult), "qn")
                    a.wait(eng, it, "egc")
                    d.done(eng.scalar_tensor_tensor(NB[:, :], EGC[:, :], -1.0, CG[:, 1, 1, :], ALU.mult, ALU.mult), "nb")
                    for n in two:
                        p.wait(eng, it, f"vt{n}")
                        d.done(eng.tensor_tensor(VB[n][:, :, :], heads(bank[2 + n][:, :], HG),
                                                 CG[:, n, 1, :].unsqueeze(2).to_broadcast([P, HG, P]), ALU.mult), f"vb{n}")
                    p.wait(eng, it, "kt")
                    a.wait(eng, it, "kce")
                    for i in two:
                        ins = eng.tensor_tensor(KD[:, 2 * i:2 * i + 2, :],
                                                bank[4][:, i * P:(i + 1) * P].unsqueeze(1).to_broadcast([P, 2, P]),
                                                KC[:, 2 * i:2 * i + 2].unsqueeze(2).to_broadcast([P, 2, P]), ALU.mult)
                    d.done(ins, "kd")
                    for n in two:
                        gram = bank[5 + n][:, :].rearrange("p (i x c) -> p i x c", i=2, x=2)
                        p.wait(eng, it, f"gr{n}")
                        a.wait(eng, it, f"ex{n}")
                        for h in four:
                            ins = eng.scalar_tensor_tensor(E[n][:, h, :], gram[:, h // 2, 0, :], CG[:, n, 1, h:h + 1],
                                                           E[n][:, h, :], ALU.mult, ALU.mult)
                        d.done(ins, f"m{n}")
                    for n in two:
                        o.wait(eng, it, f"l0_{n}")
                        d.done(eng.tensor_tensor(T_[n][:, :, :], ident.unsqueeze(1).to_broadcast([P, HG, P]),
                                                 L[n][:, :, :], ALU.subtract), f"t{n}")
                    for n in two:
                        gram = bank[5 + n][:, :].rearrange("p (i x c) -> p i x c", i=2, x=2)
                        o.wait(eng, it, f"em{n}")
                        for i in two:
                            ins = eng.tensor_tensor(EA[n][:, 2 * i:2 * i + 2, :],
                                                    gram[:, i, 1, :].unsqueeze(1).to_broadcast([P, 2, P]),
                                                    EA[n][:, 2 * i:2 * i + 2, :], ALU.mult)
                        d.done(ins, f"at{n}")
                    for l in range(1, LEVELS):
                        for n in two:
                            p.wait(eng, it, f"pp{l}_{n}")
                            if l < LEVELS - 1:
                                d.wait(eng, it, f"t{n}" if l == 1 else f"dt{l - 1}_{n}")
                                d.done(eng.tensor_tensor(T_[n][:, :, :], T_[n][:, :, :],
                                                         heads(bank[4 + 3 * n][:, :], HG), ALU.subtract), f"dt{l}_{n}")
                            if l > 1:
                                d.wait(eng, it, f"du{l - 1}_{n}")
                            d.done(eng.tensor_tensor(U_[n][:, :, :], U_[n][:, :, :], heads(bank[2 + n][:, :], HG),
                                                     ALU.subtract), f"du{l}_{n}")
                    p.wait(eng, it, "ks")
                    for h in four:
                        ins = eng.scalar_tensor_tensor(R1[:, h, :], bank[0][:, h * P:(h + 1) * P], NB[:, h:h + 1],
                                                       VB[1][:, h, :], ALU.mult, ALU.add)
                    d.done(ins, "r1")
                    a.wait(eng, it, "ro")
                    d.done(eng.scalar_tensor_tensor(OT[:, :, :], OT[:, :, :], v("onw", 0), RO[:, :, :], ALU.mult,
                                                    ALU.mult), "yo")
                    d.wait(eng, it, "yo")
                    d.done(eng.tensor_tensor(OT[:, :, :], OT[:, :, :], Z[:, bass.ds(it * HG, HG), :], ALU.mult), "yz")
                    a.wait(eng, it, "high")
                    d.wait(eng, it, "yz")
                    d.done(eng.tensor_tensor(YL[:, bass.ds(it * HG, HG), :], OT[:, :, :],
                                             YH[:, bass.ds(it * HG, HG), :].bitcast(F32), ALU.subtract), "low")

            def pool(self, eng):
                a, d, o, p = self.ac, self.dv, self.po, self.pe_
                with eng.Fori(0, GDN_V // HG) as it:
                    for n in two:
                        a.wait(eng, it, f"exa{n}")
                        o.done(eng.tensor_tensor(EA[n][:, :, :], EA[n][:, :, :],
                                                 causal.unsqueeze(1).to_broadcast([P, HG, P]), ALU.mult), f"em{n}")

                    def level(l, n):
                        m = cst[:, C_LEVEL + l * P:C_LEVEL + (l + 1) * P]
                        if l == 0:
                            d.wait(eng, it, f"m{n}")
                        elif l == 1:
                            d.wait(eng, it, f"t{n}")
                        else:
                            p.wait(eng, it, f"y{l - 1}_{n}")
                        o.done(eng.tensor_tensor(L[n][:, :, :], E[n][:, :, :],
                                                 m.unsqueeze(1).to_broadcast([P, HG, P]), ALU.mult), f"l{l}_{n}")
                    for n in two:
                        level(0, n)
                    for n in two:
                        level(1, n)
                    a.wait(eng, it, "eg")
                    for i in two:
                        ins = eng.tensor_tensor(QD[:, 2 * i:2 * i + 2, :], QD[:, 2 * i:2 * i + 2, :],
                                                KN[:, i, 1, P:SEQ].unsqueeze(1).to_broadcast([P, 2, P]), ALU.mult)
                    o.done(ins, "qd")
                    for l in range(2, LEVELS):
                        for n in two:
                            level(l, n)

            def pe(self, eng):
                a, d, o, p = self.ac, self.dv, self.po, self.pe_
                evacuated(eng, self.prev, self.prev.iters - 1, 3)
                eng.wait_ge(self.cols, 1)

                def each(out, lhs, rhs, start=True, stop=True):
                    for h in four:
                        mm = eng.matmul(out[:, h * P:(h + 1) * P], lhs[:, h, :], rhs[:, h, :], start=start, stop=stop)
                    return mm

                with eng.Fori(0, GDN_V // HG) as it:
                    a.wait(eng, it, "sq")
                    d.wait(eng, it, "r1", back=1)
                    for i in two:
                        p.done(eng.matmul(bank[i][:, :], ones[:, :], RT[:, i, :, :].rearrange("p b t -> p (b t)"),
                                          start=True, stop=True), f"ss{i}")
                    a.wait(eng, it, "vg")
                    for n in two:
                        for h in four:
                            mm = eng.transpose(bank[2 + n][:, h * P:(h + 1) * P], VG[:, h, n * P:(n + 1) * P], ident)
                        p.done(mm, f"vt{n}")
                    d.wait(eng, it, "kn")
                    for i in two:
                        mm = eng.transpose(bank[4][:, i * P:(i + 1) * P], KN[:, i, 0, 0:P], ident)
                    p.done(mm, "kt")
                    d.wait(eng, it, "qn")
                    for n in two:
                        for i in two:
                            mm = eng.matmul(bank[5 + n][:, i * 2 * P:(i + 1) * 2 * P].rearrange("p (x c) -> p x c", x=2),
                                            KN[:, i, 0, n * P:(n + 1) * P], KN[:, i, :, n * P:(n + 1) * P],
                                            start=True, stop=True)
                        p.done(mm, f"gr{n}")
                    for n in two:
                        d.wait(eng, it, f"t{n}")
                        a.wait(eng, it, f"ln{n}")
                        for h in four:
                            mm = eng.transpose(bank[n][:, h * P:(h + 1) * P], T_[n][:, h, :], ident)
                        p.done(mm, f"tt{n}")
                    for l in range(1, LEVELS):
                        for n in two:
                            a.wait(eng, it, f"u{n}" if l == 1 else f"yc{l - 1}_{n}")
                            if l > 1:
                                d.wait(eng, it, f"du{l - 1}_{n}")
                            o.wait(eng, it, f"l{l}_{n}")
                            p.done(each(bank[n], L[n], U_[n]), f"y{l}_{n}")
                        for n in two:
                            a.wait(eng, it, f"yc{l}_{n}")
                            if l == 1:
                                d.wait(eng, it, "kd")
                            mm = each(bank[2 + n], T_[n], Y_[n])
                            if l < LEVELS - 1:
                                mm = each(bank[4 + 3 * n], Y_[n], T_[n])
                            p.done(mm, f"pp{l}_{n}")
                    d.wait(eng, it, f"du{LEVELS - 1}_0")
                    p.done(each(bank[5], U_[0], VB[0]), "vn0")
                    a.wait(eng, it, "vnc0")
                    p.done(each(bank[1], KD, Y_[0]), "s")
                    p.done(each(bank[6], Y_[0], EA[0]), "o0")
                    a.wait(eng, it, "sc")
                    for i in two:
                        mm = eng.matmul(bank[0][:, i * 2 * P:(i + 1) * 2 * P], KN[:, i, 0, P:SEQ],
                                        S0[:, 2 * i:2 * i + 2, :].rearrange("p h e -> p (h e)"), start=True, stop=True)
                    p.done(mm, "ks")
                    d.wait(eng, it, "r1")
                    p.done(each(bank[2], U_[1], R1), "vn1")
                    a.wait(eng, it, "vnc1")
                    o.wait(eng, it, "qd")
                    for h in four:
                        eng.matmul(bank[3][:, h * P:(h + 1) * P], Y_[1][:, h, :], EA[1][:, h, :], start=True, stop=False)
                        mm = eng.matmul(bank[3][:, h * P:(h + 1) * P], S0[:, h, :], QD[:, h, :], start=False, stop=True)
                    p.done(mm, "o1")
                    a.wait(eng, it, "sq2")
                    for i in two:
                        p.done(eng.matmul(bank[5 + i][:, :], ones[:, :],
                                          SQ2[:, 2 * i:2 * i + 2, :].rearrange("p h t -> p (h t)"), start=True,
                                          stop=True), f"oss{i}")

            def rhs_wait(self, eng):
                def wait(k):
                    if k % HG == 0:
                        self.dv.wait(eng, k // HG, "low")
                return wait

        BT, sQ, sKD, sVT, sVN = carve(big, big_size, sBT=([P, 16, 3 * P], F32), sQ=([P, 8, SEQ], F32),
                                      sKD=([P, SWA_KV, SEQ], F32), sVT=([P, 2, SEQ], F32), sVN=([P, 2, 2, P], F32))
        sc_ = carve(work, work_size, sQS=([P, 2, SEQ], F32), sKS=([P, SEQ], F32), sVG=([P, 2, SWA_HD], F32),
                    sMX=([P, 4, 2], F32), sNM=([P, 4, 2], F32), sSM=([P, 4, 2], F32), sES=([P, 4, 2], F32),
                    **{f"{n}{i}": ([P, 3 * P], F32) for n in ("sSB", "sPT") for i in range(4)})
        QS, KS, VGs, sMX, sNM, sSM, sES = sc_[:7]
        SB, PT = sc_[7:11], sc_[11:15]
        onehot, bias_s = carve(spare, spare_size, onehot=([BUCKETS + 1, 3 * P], F32), bias_s=([16, 3 * P], F32))

        class KVSteps:

            def __init__(self, st, norm):
                self.st, self.norm = st, norm
                self.mb = sem("dma_bias_in")

            def dve(self, eng, it, u):
                st = self.st
                if u == 0:
                    self.norm.ready(eng)
                group_done(eng, st, it, u)
                b = bank[st.banks[u]]
                if u < 2:
                    for g in two:
                        for half in two:
                            ins = eng.tensor_tensor(sKD[64 * half:64 * half + 64, 2 * u + g, :],
                                                    b[64 * g:64 * g + 64, 0:SEQ], R[64 * g:64 * g + 64, 0:SEQ], ALU.mult)
                    leave(st, it, u, ins)
                else:
                    leave(st, it, u, eng.tensor_tensor(sVT[:, u - 2, :], b[:, 0:SEQ], R[:, 0:SEQ], ALU.mult))

            def act(self, eng, it, u):
                pass

            def pool(self, eng, it, u):
                if u:
                    return
                unit_done(eng, down3, down3.iters - 1, 7)
                eng.wait_ge(s_bias, 16)
                t = bias_d
                for c0, k0, n in ((0, P, P), (P, 0, 2 * P)):
                    src = bass.AP(tensor=t.tensor, offset=P - 1 + k0, ap=[[3 * P - 1, P], [3 * P * P, 16], [1, n]])
                    eng.dma_start(BT[:, :, c0:c0 + n], src).then_inc(self.mb, 16)

        def pe_bias(eng):
            eng.wait_ge(s_rel, 48)
            eng.matmul(bank[7][0:16, 0:3 * P], rel[:, :], onehot[:, :], start=True, stop=True).then_inc(s_rel, 1)

        def dve_bias(eng):
            eng.wait_ge(s_rel, 49)
            eng.tensor_copy(bias_s[:, :], bank[7][0:16, 0:3 * P]).then_inc(s_rel, 1)

        class SCore:

            def __init__(self, kv, prev):
                self.kv, self.prev = kv, prev
                self.vt, self.vn = sem("pe_swa_v"), sem("act_swa_v")
                f = lambda *xs: [f"{x}{i}" for x in xs for i in four]
                self.ac = steps("act", "score", ["qs", "ks", "vg"] + [f"{x}{i}" for i in four for x in ("e", "es")]
                                + f("ptc") + ["oh0", "oh1"])
                self.dv = steps("dve", "score", [f"{x}{i}" for i in four for x in ("b", "x", "nm")]
                                + [f"{x}{i}" for i in four for x in ("dn", "rc", "p")] + ["ol0", "ol1"])
                self.pe_ = steps("pe", "score", f("s") + f("pt") + f("o"))

            def act(self, eng):
                a, d, p = self.ac, self.dv, self.pe_
                eng.wait_ge(self.vt, 1)
                eng.activation(sVN[:, :, :, :].rearrange("p b c e -> p c b e"),
                               bank[5][:, :].rearrange("p (c b e) -> p c b e", c=2, b=2), ACT.Copy).then_inc(self.vn, 1)
                evacuated(eng, self.prev, self.prev.iters - 1, 3)
                eng.wait_ge(self.vn, 1)
                with eng.Fori(0, SWA_KV) as it:
                    p.wait(eng, it, "o3", back=1)
                    a.done(eng.activation(QS[:, :, :], sQ[:, bass.ds(it * 2, 2), :], ACT.Copy), "qs")
                    a.done(eng.activation(KS[:, :].unsqueeze(1), sKD[:, bass.ds(it, 1), :], ACT.Copy), "ks")
                    vn = sVN[:, :, :, :].rearrange("p b c (x e) -> p b (c x) e", x=2)
                    a.done(eng.activation(VGs[:, :, :].unsqueeze(2), vn[:, :, bass.ds(it, 1), :], ACT.Copy), "vg")
                    for i in four:
                        d.wait(eng, it, f"nm{i}")
                        for n, (c0, c1) in enumerate(((0, P), (P, 3 * P))):
                            ins = eng.activation(SB[i][:, c0:c1], SB[i][:, c0:c1], ACT.Exp, bias=sNM[:, i, n:n + 1],
                                                 accum_out=sSM[:, i, n:n + 1])
                        a.done(ins, f"e{i}")
                        a.done(eng.activation(sES[:, i, :], sNM[:, i, :], ACT.Exp, bias=v("sink", it * 4 + i)), f"es{i}")
                    for i in four:
                        p.wait(eng, it, f"pt{i}")
                        a.done(eng.activation(PT[i][:, :], bank[i][:, 0:3 * P], ACT.Copy), f"ptc{i}")
                    for j in two:
                        p.wait(eng, it, f"o{2 * j + 1}")
                        a.done(eng.activation(OH[:, bass.ds(it * 2 + j, 1), :], bank[6 + j][:, 0:SEQ].unsqueeze(1),
                                              ACT.Copy), f"oh{j}")

            def dve(self, eng):
                a, d, p = self.ac, self.dv, self.pe_
                eng.wait_ge(self.kv.mb, 32)
                with eng.Fori(0, SWA_KV) as it:
                    for i in four:
                        p.wait(eng, it, f"s{i}")
                        d.done(eng.scalar_tensor_tensor(SB[i][:, :].unsqueeze(1), bank[i][:, 0:3 * P].unsqueeze(1),
                                                        SWA_HD ** -0.5, BT[:, bass.ds(it * 4 + i, 1), :], ALU.mult,
                                                        ALU.add), f"b{i}")
                        d.wait(eng, it, f"b{i}")
                        for n, (c0, c1) in enumerate(((0, P), (P, 3 * P))):
                            ins = eng.tensor_reduce(sMX[:, i, n:n + 1], SB[i][:, c0:c1], AX.X, ALU.max)
                        d.done(ins, f"x{i}")
                        d.wait(eng, it, f"x{i}")
                        d.done(eng.tensor_scalar(sNM[:, i, :], sMX[:, i, :], v("sink", it * 4 + i), -1.0, ALU.max,
                                                 ALU.mult), f"nm{i}")
                    for i in four:
                        a.wait(eng, it, f"es{i}")
                        d.done(eng.tensor_tensor(sSM[:, i, :], sSM[:, i, :], sES[:, i, :], ALU.add), f"dn{i}")
                        d.wait(eng, it, f"dn{i}")
                        d.done(eng.reciprocal(sSM[:, i, :], sSM[:, i, :]), f"rc{i}")
                        d.wait(eng, it, f"rc{i}")
                        for n, (c0, c1) in enumerate(((0, P), (P, 3 * P))):
                            ins = eng.tensor_scalar(SB[i][:, c0:c1], SB[i][:, c0:c1], sSM[:, i, n:n + 1], None, ALU.mult)
                        d.done(ins, f"p{i}")
                    for j in two:
                        a.wait(eng, it, f"oh{j}")
                        d.done(eng.tensor_tensor(OL[:, bass.ds(it * 2 + j, 1), :], bank[6 + j][:, 0:SEQ].unsqueeze(1),
                                                 OH[:, bass.ds(it * 2 + j, 1), :].bitcast(F32), ALU.subtract), f"ol{j}")

            def pool(self, eng):
                pass

            def pe_v(self, eng):
                evacuated(eng, self.kv.st, 0, 3)
                for c in two:
                    for b in two:
                        o = (2 * c + b) * P
                        mm = eng.transpose(bank[5][:, o:o + P], sVT[:, c, b * P:(b + 1) * P], ident)
                mm.then_inc(self.vt, 1)

            def pe(self, eng):
                a, d, p = self.ac, self.dv, self.pe_
                evacuated(eng, self.prev, self.prev.iters - 1, 3)
                with eng.Fori(0, SWA_KV) as it:
                    a.wait(eng, it, "vg")
                    for i in four:
                        q, k = QS[64 * (i % 2):64 * (i % 2) + 64, i // 2, :], KS[64 * (i % 2):64 * (i % 2) + 64, :]
                        a.wait(eng, it, f"ptc{i}", back=1)
                        eng.matmul(bank[i][:, 0:P], q[:, 0:P], k[:, 0:P], start=True, stop=True)
                        p.done(eng.matmul(bank[i][:, P:3 * P], q[:, P:SEQ], k[:, :], start=True, stop=True), f"s{i}")
                    for i in four:
                        d.wait(eng, it, f"p{i}")
                        for t in range(3):
                            mm = eng.transpose(bank[i][:, t * P:(t + 1) * P], SB[i][:, t * P:(t + 1) * P], ident)
                        p.done(mm, f"pt{i}")
                    for i in four:
                        a.wait(eng, it, f"ptc{i}")
                        d.wait(eng, it, f"ol{i // 2}", back=1)
                        out = bank[6 + i // 2][64 * (i % 2):64 * (i % 2) + 64, :]
                        eng.matmul(out[:, 0:P], VGs[:, 0, :], PT[i][:, 0:P], start=True, stop=True)
                        eng.matmul(out[:, P:SEQ], VGs[:, 0, :], PT[i][:, P:2 * P], start=True, stop=False)
                        p.done(eng.matmul(out[:, P:SEQ], VGs[:, 1, :], PT[i][:, 2 * P:3 * P], start=False, stop=True),
                               f"o{i}")

            def rhs_wait(self, eng):
                def wait(k):
                    if k % 2 == 0:
                        self.dv.wait(eng, k // 2, "ol1")
                return wait

        def loaded(eng, c=None):
            eng.wait_ge(s_h0, 16)

        def sq_free(eng, c=None):
            pass

        n1 = norm_before("g0", TM, loaded)
        c_up1 = UpSteps(up1, n1)
        c_down1 = NormedSteps(down1, "g1", 0.5)
        a1 = norm_after(down1, TM, None)
        n2 = norm_before("g2", TM, a1.chunk)
        c_mg = MGateSteps(mgate, n2)
        c_mqk = ConvSteps(mqk, n2, "acw", "acb", lambda m: QK[:, bass.ds(m, 1), :], 0, 8)
        c_mv = ScaleSteps(mv, n2, lambda m: VT[:, bass.ds(m, 1), :])
        c_mog = ScaleSteps(mog, n2, lambda m: OG[:, bass.ds(m, 1), :], ACT.Sigmoid)
        core1 = MCore(c_mg, mog, mout)
        core1.og_ready = lambda eng: c_mog.funcs.wait(eng, mog.iters - 1, "func3")
        core1.qk_ready = lambda eng: c_mqk.silus.wait(eng, mqk.iters - 1, "silu3")
        c_mout = NormedSteps(mout, "g3", 1.0)
        a3 = norm_after(mout, SEQ, None)
        n4 = norm_before("g4", SEQ, a3.chunk)
        c_up2 = UpSteps(up2, n4)
        c_down2 = NormedSteps(down2, "g5", 0.5)
        a5 = norm_after(down2, SEQ, None)
        n6 = norm_before("ga", SEQ, a5.chunk)
        c_gg = GGateSteps(ggate, n6)
        c_gqk = ConvSteps(gqk, n6, "dcw", None, lambda m: dQK[:, bass.ds(m, 1), :], 0, 32)
        c_gv = ConvSteps(gv, n6, "dcw", None, lambda m: dVT[:, bass.ds(m, 1), :], 16, 32)
        c_gz = ScaleSteps(gz, n6, lambda m: Z[:, bass.ds(m, 1), :], ACT.Silu)
        core2 = GCore(c_gg, gz)
        core2.z_ready = lambda eng: c_gz.funcs.wait(eng, gz.iters - 1, "func3")
        core2.qkv_ready = lambda eng: c_gv.silus.wait(eng, gv.iters - 1, "silu3")
        c_gout = AddSteps(gout, [("gf0", XH, XL)])
        n7 = norm_streamed(gout)
        c_up3 = ConvUpSteps(up3, n7, 0)
        c_down3 = AddSteps(down3, [("gkv", XH, XL), ("gb", BH, BL)])
        n8 = norm_streamed(down3)
        c_kv = KVSteps(skv, n8)
        c_sq = ScaleSteps(sq_, n8, lambda m: sQ[:, bass.ds(m, 1), :])
        core3 = SCore(c_kv, sq_)
        c_so = AddSteps(so, [("gf1", XH, XL)])
        n9 = norm_streamed(so)
        c_up4 = ConvUpSteps(up4, n9, 1)
        c_down4 = AddSteps(down4, [])
        n10 = norm_streamed(down4)


        def prime(eng, kind):
            for k, s in primed:
                if k == kind:
                    s.prime(eng)

        def first_splits(eng, kind):
            for u in range(SLOTS):
                split(eng, kind, stages[0], 0, u)

        def walk_all(eng, kind):
            def go(st, c, hook=None, hook_at=0):
                walk(eng, kind, st, c, hook if kind == "act" else None, hook_at)

            def normed(st, c, after, before):
                if kind == "dve":
                    c.before(eng)
                go(st, c)
                if kind == "act":
                    after.rstd(eng)
                    if before:
                        before.act(eng)
                if kind == "dve":
                    after.dve(eng, before.low if before else lambda eng, c: None)
                    if before:
                        before.dve(eng)

            first_splits(eng, kind)
            if kind == "act":
                n1.act(eng)
            if kind == "dve":
                for c in range(DC):
                    n1.low(eng, c)
                n1.dve(eng)
            go(up1, c_up1, n1.rstd)
            normed(down1, c_down1, a1, n2)
            go(mgate, c_mg, n2.rstd, 3)
            go(mqk, c_mqk)
            go(mv, c_mv)
            go(mog, c_mog)
            core_part(core1, kind)(eng)
            normed(mout, c_mout, a3, n4)
            go(up2, c_up2, n4.rstd)
            normed(down2, c_down2, a5, n6)

            def added(st, c):
                if kind == "dve":
                    c.before(eng)
                go(st, c)

            go(ggate, c_gg, n6.rstd, 3)
            go(gqk, c_gqk)
            go(gv, c_gv)
            go(gz, c_gz)
            core_part(core2, kind)(eng)
            added(gout, c_gout)
            go(up3, c_up3, n7.rstd)
            added(down3, c_down3)
            go(skv, c_kv, n8.rstd)
            go(sq_, c_sq)
            core_part(core3, kind)(eng)
            added(so, c_so)
            go(up4, c_up4, n9.rstd)
            added(down4, c_down4)
            if kind == "act":
                n10.rstd(eng)
            if kind == "dve":
                n10.ready(eng)
                for c in range(DC):
                    eng.scalar_tensor_tensor(H[:, c, META:TM], H[:, c, META:TM], gains["gfin"][:, c:c + 1],
                                             R[:, 0:SEQ], ALU.mult, ALU.mult).then_inc(s_fin, 1)


        def core_part(core, kind):
            return {"act": core.act, "dve": core.dve, "pool": core.pool}[kind]

        block = ctx.enter_context(nc.Block())

        @block.sync
        def _(eng):
            eng.dma_start(vec[:, :], a["vecs"]).then_inc(s_in, 16)
            eng.dma_start(cst[:, :], a["consts"]).then_inc(s_in, 16)
            eng.dma_start(H[:, :, :], a["h0"]).then_inc(s_h0, 16)
            eng.dma_start(onehot[:, :], a["buckets"]).then_inc(s_rel, 16)
            eng.dma_start(rel[0:BUCKETS, :], a["rel_table"]).then_inc(s_rel, 16)
            run_dma(eng)
            for c in range(0, DC, 2):
                eng.wait_ge(s_fin, c + 2)
                eng.dma_start(a["out"][:, c:c + 2, :], H[:, c:c + 2, META:TM]).then_inc(s_out, 16)
            eng.wait_ge(s_out, 16 * DC // 2)


        @block.gpsimd
        def _(eng):
            prime(eng, "pool")
            eng.wait_ge(s_rel, 50)
            eng.dma_start(bias_d, bias_s[:, :].unsqueeze(1).to_broadcast([16, P, 3 * P])).then_inc(s_bias, 16)
            for s in LO_POOL:
                eng.sem_inc(s_lo[s], 1)
            walk_all(eng, "pool")

        @block.scalar
        def _(eng):
            prime(eng, "act")
            eng.wait_ge(s_in, 32)
            walk_all(eng, "act")

        @block.vector
        def _(eng):
            prime(eng, "dve")
            for s in set(range(SLOTS)) - LO_POOL:
                eng.sem_inc(s_lo[s], 1)
            eng.sem_inc(s_ev, 4)
            eng.memset(ones[:, :], 1.0).then_inc(s_ms, 1)
            eng.memset(mean[:, :], 1.0 / D).then_inc(s_ms, 1)
            for t in TP:
                eng.memset(t[:, 0:3], 0.0).then_inc(s_ms, 1)
            eng.memset(rel[BUCKETS:BUCKETS + 1, :], NEG).then_inc(s_rel, 16)
            eng.wait_ge(s_in, 32)
            dve_bias(eng)
            walk_all(eng, "dve")

        @block.tensor
        def _(eng):
            prime(eng, "pe")
            for s in range(SLOTS):
                eng.sem_inc(s_pe[s], 1)
            eng.wait_ge(s_in, 32)
            eng.wait_ge(s_ms, 4)
            pe_bias(eng)
            multiply(eng, up1, {2: n1.pe}, n1.rhs(eng))
            multiply(eng, down1, None, c_up1.rhs_wait(eng))
            a1.pe(eng)
            multiply(eng, mgate, None, n2.rhs(eng))
            multiply(eng, mqk, {1: n2.pe})
            multiply(eng, mv, {0: c_mg.pe})
            multiply(eng, mog)
            core1.pe(eng)
            multiply(eng, mout, None, core1.rhs_wait(eng))
            a3.pe(eng)
            multiply(eng, up2, {2: n4.pe}, n4.rhs(eng))
            multiply(eng, down2, None, c_up2.rhs_wait(eng))
            a5.pe(eng)
            multiply(eng, ggate, None, n6.rhs(eng))
            multiply(eng, gqk, {1: n6.pe})
            multiply(eng, gv, {0: c_gg.pe})
            multiply(eng, gz)
            core2.pe(eng)
            multiply(eng, gout, None, core2.rhs_wait(eng))
            multiply(eng, up3, {2: n7.pe}, n7.rhs(eng))
            multiply(eng, down3, None, c_up3.rhs_wait(eng))
            multiply(eng, skv, {2: n8.pe}, n8.rhs(eng))
            multiply(eng, sq_, {0: core3.pe_v}, lambda k: down3.dv.wait(eng, k // 2, f"low1_{k % 2}"))
            core3.pe(eng)
            multiply(eng, so, None, core3.rhs_wait(eng))
            multiply(eng, up4, {2: n9.pe}, n9.rhs(eng))
            multiply(eng, down4, None, c_up4.rhs_wait(eng))
            n10.pe(eng)



def _tiles(w, pad=0):
    k, m = w.shape
    return w.reshape(k // P, P, m // P, P).transpose(2, 1, 0, 3)


def _bodies(tiles, groups):
    m, p, k, f = tiles.shape
    return np.ascontiguousarray(tiles.reshape(m // groups, groups, p, k, f).transpose(0, 2, 1, 3, 4)
                                .reshape(m // groups, p, groups * k, f))


def _pairs(w):
    t = _tiles(w)
    return _bodies(t.reshape(2, FC, *t.shape[1:]).transpose(1, 0, 2, 3, 4).reshape(t.shape), 4)


def _gates(w, n):
    out = np.zeros((D, P), w.dtype)
    out[:, 0:n] = w[:, 0:n]
    out[:, 32:32 + n] = w[:, n:2 * n]
    return _bodies(_tiles(out), 1)


def _col(x):
    return np.ascontiguousarray(x.reshape(-1, P).T)


def _pair_cols(x):
    c = x.reshape(-1, 2, FC, P).transpose(0, 2, 1, 3)
    return _col(c)


def _pad(x, n):
    out = np.zeros((P, n), np.float32)
    out[0:x.shape[0], 0:x.shape[1]] = x
    return out


def kernel(**inputs):
    from concourse import bacc
    from concourse.bass_utils import run_bass_kernel_spmd

    i = {k: np.asarray(x) for k, x in inputs.items()}
    ng = i["norm_gains"][0]
    qk_cols = GDN_QK * P
    w2 = i["a_w_in_2"][0]
    kq = w2[:, 0:2 * qk_cols].reshape(D, 2, GDN_QK, P)[:, ::-1].transpose(0, 2, 1, 3).reshape(D, 2 * qk_cols)
    cw = i["a_conv_w_2"][0]
    cw_kq = cw[:, 0:2 * qk_cols].reshape(4, 2, GDN_QK, P)[:, ::-1].transpose(0, 2, 1, 3).reshape(4, 2 * qk_cols)
    gdn_cw = np.concatenate([cw_kq, cw[:, 2 * qk_cols:]], axis=1)
    vecs = {"acw": _col(i["a_conv_w"][0]), "acb": _col(i["a_conv_b"][0]), "dcw": _col(gdn_cw),
            "onw": _col(i["a_out_norm_w_2"]), "sink": np.repeat(i["b_sinks_2"], P, axis=0),
            "gate": _pad(i["a_gate_b"][0].reshape(2, A_HEADS).T, 2),
            "dn": _pad(np.stack([i["a_a_log_2"][0], i["a_dt_bias_2"][0]], axis=1), 2),
            "ga": _col(i["a_norm_w_2"]), "gkv": _col(i["kv_norm_w_2"]), "gb": _col(i["b_norm_w_2"]),
            "gf0": _col(i["ffn_norm_w_2"][0]), "gf1": _col(i["ffn_norm_w_2"][1]), "gfin": _col(i["final_norm_w_2"])}
    for n in range(6):
        vecs[f"g{n}"] = _col(ng[n])
    for n in range(2):
        vecs[f"fcw{n}"] = _pair_cols(i["ffn_conv_w_2"][n])
        vecs[f"fcb{n}"] = _pair_cols(i["ffn_conv_b_2"][n])
    for n, size in _VEC_SIZES:
        assert vecs[n].shape == (P, size), (n, vecs[n].shape)
    aw = i["a_w_in"][0]
    h0 = np.concatenate([i["meta_tokens"], i["x"][0]], axis=0).T.reshape(DC, P, TM).transpose(1, 0, 2)
    arrays = {
        "vecs": np.concatenate([vecs[n] for n, _ in _VEC_SIZES], axis=1),
        "consts": constants(), "buckets": bucket_rows(), "h0": np.ascontiguousarray(h0),
        "rel_table": i["rel_bias_table_2"],
        "w_up1": _pairs(i["ffn_w_in"][0, 0]), "w_down1": _bodies(_tiles(i["ffn_w_out"][0, 0]), 2),
        "w_up2": _pairs(i["ffn_w_in"][0, 1]), "w_down2": _bodies(_tiles(i["ffn_w_out"][0, 1]), 2),
        "w_mgate": _gates(aw[:, 3072:], A_HEADS), "w_mqk": _bodies(_tiles(aw[:, 0:1024]), 4),
        "w_mv": _bodies(_tiles(aw[:, 1024:2048]), 4), "w_mog": _bodies(_tiles(aw[:, 2048:3072]), 4),
        "w_mout": _bodies(_tiles(i["a_w_out"][0]), 4),
        "w_ggate": _gates(w2[:, 6144:], GDN_V), "w_gqk": _bodies(_tiles(kq), 4),
        "w_gv": _bodies(_tiles(w2[:, 2048:4096]), 4), "w_gz": _bodies(_tiles(w2[:, 4096:6144]), 4),
        "w_gout": _bodies(_tiles(i["a_w_out_2"][0]), 2),
        "w_up3": _pairs(i["ffn_w_up_2"][0]), "w_down3": _bodies(_tiles(i["ffn_w_down_2"][0]), 2),
        "w_skv": _bodies(_tiles(i["w_kv_2"]), 4), "w_sq": _bodies(_tiles(i["b_w_q_2"][0]), 4),
        "w_so": _bodies(_tiles(i["b_w_o_2"][0]), 4),
        "w_up4": _pairs(i["ffn_w_up_2"][1]), "w_down4": _bodies(_tiles(i["ffn_w_down_2"][1]), 2),
    }
    nc = bacc.Bacc("TRN2", target_bir_lowering=False, num_devices=1)
    a = {n: nc.dram_tensor(f"in_{n}", x.shape, F32, kind="ExternalInput").ap() for n, x in arrays.items()}
    a["out"] = nc.dram_tensor("out", (P, DC, SEQ), F32, kind="ExternalOutput").ap()
    program(nc, a)
    r = run_bass_kernel_spmd(nc, [{f"in_{n}": x for n, x in arrays.items()}], core_ids=[0])
    y = r.results[0]["out"]
    return np.ascontiguousarray(y.transpose(2, 1, 0).reshape(1, SEQ, D))
```

```python
from contextlib import ExitStack

import concourse.bass as bass
import numpy as np
from concourse import mybir

F32 = mybir.dt.float32
F32R = mybir.dt.float32r
ALU = mybir.AluOpType
ACT = mybir.ActivationFunctionType
AX = mybir.AxisListType

P = 128
D = 1024
DC = D // P
SEQ = 256
META = 16
TM = SEQ + META
FF = 2816
FC = FF // P
EPS = 1e-6

A_HEADS = 8
A_DK = 64
GDN_QK = 8
GDN_V = 16
SWA_KV = 4
SWA_HD = 64
BUCKETS = 32
MAX_DIST = 128
NEG = -1e30

SLOTS = 4
TILES = 8
MEMSETS = 6

VEC = {}
_VEC_SIZES = [("g0", 8), ("g1", 8), ("g2", 8), ("g3", 8), ("g4", 8), ("g5", 8), ("ga", 8), ("gkv", 8), ("gb", 8),
              ("gf0", 8), ("gf1", 8), ("gfin", 8), ("acw", 4 * 8), ("acb", 8), ("dcw", 4 * 32), ("onw", 1),
              ("fcw0", 3 * 44), ("fcb0", 44), ("fcw1", 3 * 44), ("fcb1", 44), ("sink", 16), ("gate", 2), ("dn", 2)]
_at = 0
for _name, _n in _VEC_SIZES:
    VEC[_name] = _at
    _at += _n
VECS = _at

LEVELS = 7
C_ID, C_LE, C_LEVEL = 0, P, 2 * P
CONSTS = C_LEVEL + LEVELS * P


def constants():
    r, c = np.arange(P)[:, None], np.arange(P)[None, :]
    parts = [np.eye(P), r <= c]
    for level in range(LEVELS):
        b = 1 << level
        parts.append((r // (2 * b) == c // (2 * b)) & (r // b % 2 == 1) & (c // b % 2 == 0))
    return np.concatenate([np.asarray(x, np.float32) for x in parts], axis=1)


def bucket_rows():
    out = np.zeros((BUCKETS + 1, 3 * P), np.float32)
    for y in range(3 * P):
        n = 2 * P - 1 - y
        if not 0 <= n < P:
            out[BUCKETS, y] = 1.0
            continue
        exact = BUCKETS // 2
        b = n if n < exact else min(exact + int(np.log(n / exact) / np.log(MAX_DIST / exact) * exact), BUCKETS - 1)
        out[b, y] = 1.0
    return out


class Steps:

    def __init__(self, sem, names):
        self.sem, self.names, self.at = sem, list(names), 0

    def prime(self, eng):
        eng.sem_inc(self.sem, len(self.names))

    def done(self, instruction, name):
        assert self.names[self.at % len(self.names)] == name, (self.names[self.at % len(self.names)], name)
        self.at += 1
        instruction.then_inc(self.sem, 1)

    def wait(self, eng, it, name, back=0):
        n = len(self.names)
        eng.wait_ge(self.sem, (it + (1 - back)) * n + self.names.index(name) + 1)


class Stage:

    def __init__(self, name, weights, iters, units, banks, T, rhs, off=0, look=None):
        self.name, self.weights, self.iters, self.units = name, weights, iters, units
        self.banks, self.T, self.rhs, self.off = banks, T, rhs, off
        self.look = look if look is not None else len(banks)
        self.groups = 1 + max(g for u in units for g, _ in u)
        self.first_k = {g: min(k for u in units for q, k in u if q == g) for g in range(self.groups)}
        self.last_k = {g: max(k for u in units for q, k in u if q == g) for g in range(self.groups)}
        self.unit_of = {g: max(n for n, u in enumerate(units) if any(q == g for q, _ in u)) for g in range(self.groups)}
        self.at = [sum(len(u) for u in units[:n]) for n in range(len(units))]


def whole(groups, ks=DC):
    return [[(g, k) for k in range(ks)] for g in range(groups)]


def cut(groups, cuts):
    out = []
    for g in range(groups):
        at = 0
        for n in cuts:
            out.append([(g, at + k) for k in range(n)])
            at += n
    return out


def program(nc, a):
    with ExitStack() as ctx:
        def sem(name):
            return ctx.enter_context(nc.semaphore(name))

        top = [nc.sbuf_base + (-nc.sbuf_base) % 64]

        def region(size):
            at = top[0]
            top[0] += size
            assert top[0] <= nc.sbuf_usable_end, top[0]
            return at

        def carve(at, size, **what):
            out, end = [], at + size
            for name, (shape, dt) in what.items():
                n = int(np.prod(shape[1:])) * 4
                assert at + n <= end, (name, at + n - end)
                out.append(nc.alloc_sbuf_tensor_at(name, shape, dt, offset=at))
                at += -(-n // 32) * 32
            return out

        def sb(name, shape, dt=F32):
            n = -(-int(np.prod(shape[1:])) * 4 // 32) * 32
            return nc.alloc_sbuf_tensor_at(name, shape, dt, offset=region(n))

        def row(name, shape=(P, TM)):
            return sb(name, list(shape))

        H = sb("H", [P, DC, TM])
        xreg_size = 2 * DC * TM * 4
        xreg = region(xreg_size)
        raw = [sb(f"raw{i}", [P, TILES, P]) for i in range(SLOTS)]
        WH = [sb(f"wh{i}", [P, TILES, P], F32R) for i in range(SLOTS)]
        WL = [sb(f"wl{i}", [P, TILES, P], F32R) for i in range(SLOTS)]
        vec = sb("vec", [P, VECS])
        cst = sb("cst", [P, CONSTS])
        ones = sb("ones", [P, P])
        mean = sb("mean", [P, P])
        R = row("R")
        RP = row("RP")
        ACC = row("ACC")
        TP = [row(f"tp{i}", (P, 3 + TM)) for i in range(2)]
        scratch = sb("scratch", [P, 2])
        rel = sb("rel", [BUCKETS + 1, 16])
        AC = sb("AC", [P, 3, A_HEADS])
        COLS = sb("COLS", [P, 2, 2, GDN_V])
        big_size, ext_size = 49152, 49152
        big, ext = region(big_size), region(ext_size)
        work_size = nc.sbuf_usable_end - top[0] - 64
        work = region(work_size)
        buf = carve(work, work_size, **{f"{n}{i}": ([P, TM], F32) for n in ("sqb", "cv", "sg", "pr", "sc")
                                        for i in range(2)})
        SQB, CV, SG, PR, SC = (buf[i:i + 2] for i in range(0, 10, 2))
        CONV = CV + SG
        spare = work + 10 * TM * 4 + 64
        spare_size = work + work_size - spare
        XH, XL = carve(xreg, xreg_size, XH=([P, DC, TM], F32R), XL=([P, DC, TM], F32R))
        gains = {n: vec[:, VEC[n]:VEC[n] + DC] for n in ("g0", "g1", "g2", "g3", "g4", "g5", "ga", "gkv", "gb", "gf0",
                                                        "gf1", "gfin")}

        def v(name, i):
            return vec[:, VEC[name] + i:VEC[name] + i + 1] if isinstance(i, int) else vec[:, bass.ds(VEC[name] + i, 1)]

        ident = cst[:, C_ID:C_ID + P]
        causal = cst[:, C_LE:C_LE + P]
        eps = scratch[:, 0:1]
        bank = [ctx.enter_context(nc.psum_tensor(f"bank{i}", [P, 512], F32)) for i in range(8)]

        AH, AL = carve(big, big_size, AH=([P, FC, TM], F32R), AL=([P, FC, TM], F32R))
        YG, SQ = carve(ext, ext_size, YG=([P, DC, TM], F32), SQ=([P, DC, TM], F32))

        mx_d = nc.dram_tensor("mx_d", (2, A_HEADS, TM), F32, kind="Internal").ap()
        gc_d = nc.dram_tensor("gc_d", (GDN_V, SEQ), F32, kind="Internal").ap()
        bias_d = nc.dram_tensor("bias_d", (16, P, 3 * P), F32, kind="Internal").ap()

        X, A = (XH, XL), (AH, AL)
        up_units, down_units = whole(4), cut(2, (6, 6, 5, 5))
        stages = []

        def stage(*args, **kw):
            st = Stage(*args, **kw)
            st.u0 = sum(s.iters * len(s.units) for s in stages)
            st.g0 = sum(s.iters * s.groups for s in stages)
            stages.append(st)
            return st

        up1 = stage("up1", a["w_up1"], 11, up_units, [0, 1, 2, 3], TM, X)
        down1 = stage("down1", a["w_down1"], 4, down_units, [2, 3], TM, A)
        mgate = stage("mgate", a["w_mgate"], 1, cut(1, (2, 2, 2, 2)), [3], TM, X, look=1)
        mqk = stage("mqk", a["w_mqk"], 2, whole(4), [0, 1, 2, 3], TM, X)
        mv = stage("mv", a["w_mv"], 2, whole(4), [0, 1, 2, 3], TM, X)
        mog = stage("mog", a["w_mog"], 2, whole(4), [0, 1, 2, 3], SEQ, X, off=META)
        mout = stage("mout", a["w_mout"], 2, whole(4), [0, 1, 2, 3], SEQ, X)
        up2 = stage("up2", a["w_up2"], 11, up_units, [0, 1, 2, 3], SEQ, X)
        down2 = stage("down2", a["w_down2"], 4, down_units, [2, 3], SEQ, A)
        ggate = stage("ggate", a["w_ggate"], 1, cut(1, (2, 2, 2, 2)), [3], SEQ, X, look=1)
        gqk = stage("gqk", a["w_gqk"], 4, whole(4), [0, 1, 2, 3], SEQ, X)
        gvz0 = stage("gvz0", a["w_gvz"][0:1], 1, whole(8), [0, 1, 2, 3], SEQ, X)
        gvz = stage("gvz", a["w_gvz"][1:4], 3, whole(8), [7, 4], SEQ, X)
        YL, Z = carve(big, big_size, YL=([P, 16, SEQ], F32R), Z=([P, 16, SEQ], F32))
        core_at, core_size = big + 2 * 16 * SEQ * 4, 16 * SEQ * 4
        YH, = carve(ext + 16 * SEQ * 4, 16 * SEQ * 4, YH=([P, 16, SEQ], F32R))
        gout = stage("gout", a["w_gout"], 4, cut(2, (8, 8)), [2, 3], SEQ, (YH, YL))
        up3 = stage("up3", a["w_up3"], 11, up_units, [0, 1, 2, 3], SEQ, X)
        down3 = stage("down3", a["w_down3"], 4, down_units, [2, 3], SEQ, A)
        skv = stage("skv", a["w_skv"], 1, whole(4), [0, 1, 2, 3], SEQ, X)
        BH, BL, OH, OL = carve(ext, ext_size, BH=([P, DC, SEQ], F32R), BL=([P, DC, SEQ], F32R),
                               OH=([P, DC, SEQ], F32R), OL=([P, DC, SEQ], F32R))
        sq_ = stage("sq", a["w_sq"], 2, whole(4), [0, 1, 2, 3], SEQ, (BH, BL))
        so = stage("so", a["w_so"], 2, whole(4), [0, 1, 2, 3], SEQ, (OH, OL))
        up4 = stage("up4", a["w_up4"], 11, up_units, [0, 1, 2, 3], SEQ, X)
        down4 = stage("down4", a["w_down4"], 4, down_units, [2, 3], SEQ, A)
        for s, t in zip(stages, stages[1:]):
            s.next = t
        stages[-1].next = None

        s_raw = [sem(f"s_raw{i}") for i in range(SLOTS)]
        s_hi = [sem(f"s_hi{i}") for i in range(SLOTS)]
        s_lo = [sem(f"s_lo{i}") for i in range(SLOTS)]
        s_pe = [sem(f"s_pe{i}") for i in range(SLOTS)]
        s_ev = sem("s_ev")
        s_in, s_cst = sem("s_in"), sem("s_cst")
        s_h0 = [sem("s_h0_0"), sem("s_h0_1")]
        s_ms = sem("s_ms")
        s_rel, s_bias = sem("s_rel"), sem("s_bias")
        s_bias_pe, s_bias_dve = sem("s_bias_pe"), sem("s_bias_dve")
        s_h = sem("s_h")
        s_xh, s_xl = sem("s_xh"), sem("s_xl")
        s_sq, s_ss = sem("s_sq"), sem("s_ss")
        s_st = sem("s_st")
        s_ln, s_r = sem("s_ln"), sem("s_r")
        s_tmp = sem("s_tmp")
        s_fin, s_out = sem("s_fin"), sem("s_out")
        LO_POOL = {3}

        def turn(st, it, u):
            return it * (len(st.units) // SLOTS) + (st.u0 + u) // SLOTS

        def unit_done(eng, st, it, u):
            eng.wait_ge(s_pe[u % SLOTS], turn(st, it, u) + 2)

        def group_done(eng, st, it, g):
            unit_done(eng, st, it, st.unit_of[g])

        def group(st, it, g):
            return st.g0 + it * st.groups + g

        def evacuated(eng, st, it, g):
            eng.wait_ge(s_ev, group(st, it, g) + 5)

        def warm(eng, func):
            eng.activation(scratch[:, 1:2], scratch[:, 0:1], func)

        def run_dma(eng):
            for st in stages:
                with eng.Fori(0, st.iters) as it:
                    for u, tiles in enumerate(st.units):
                        s, n = u % SLOTS, len(tiles)
                        eng.wait_ge(s_lo[s], turn(st, it, u) + 1)
                        eng.dma_start(raw[s][:, 0:n, :], st.weights[bass.ds(it, 1), :, st.at[u]:st.at[u] + n, :]
                                      .rearrange("i p n m -> p (i n) m")).then_inc(s_raw[s], 16)

        def split_hi(eng, st, it, u):
            s, n = u % SLOTS, len(st.units[u])
            k = turn(st, it, u)
            eng.wait_ge(s_raw[s], (k + 1) * 16)
            eng.wait_ge(s_pe[s], k + 1)
            eng.activation(WH[s][:, 0:n, :], raw[s][:, 0:n, :], ACT.Copy).then_inc(s_hi[s], 1)

        def split_lo(eng, st, it, u):
            s, n = u % SLOTS, len(st.units[u])
            eng.wait_ge(s_hi[s], turn(st, it, u) + 1)
            eng.tensor_tensor(WL[s][:, 0:n, :], raw[s][:, 0:n, :], WH[s][:, 0:n, :].bitcast(F32),
                              ALU.subtract).then_inc(s_lo[s], 1)

        def split(eng, kind, st, it, u):
            if kind == "act":
                split_hi(eng, st, it, u)
            elif (kind == "pool") == (u % SLOTS in LO_POOL):
                split_lo(eng, st, it, u)

        def order(c, kind):
            if hasattr(c, "order"):
                return c.order[kind]
            if kind == "dve":
                return [(0, c.dve), "split"]
            return ["split", (0, c.act if kind == "act" else c.pool)]

        def walk(eng, kind, st, c, hooks):
            U = len(st.units)
            todo = order(c, kind)
            lags = [item[0] for item in todo if item != "split"]

            def body(it, last, first):
                for u in range(U):
                    n = u + SLOTS
                    if first and kind == "dve" and u in hooks:
                        hooks[u](eng)
                    for item in todo:
                        if item == "split":
                            if n < U:
                                split(eng, kind, st, it, n)
                            elif not last:
                                split(eng, kind, st, it + 1, n - U)
                            elif st.next is not None:
                                split(eng, kind, st.next, 0, n - U)
                            if first and kind == "act" and u in hooks:
                                hooks[u](eng)
                        elif u >= item[0]:
                            item[1](eng, it, u - item[0])
                        elif not first:
                            item[1](eng, it - 1, u - item[0] + U)

            start = 0
            if st.iters > 1 and (hooks or max(lags) > 0):
                body(0, False, True)
                start = 1
            if st.iters - 1 > start:
                with eng.Fori(start, st.iters - 1) as it:
                    body(it, False, False)
            body(st.iters - 1, True, st.iters == 1)
            for u in range(U, U + max(lags)):
                for item in todo:
                    if item != "split" and u - item[0] < U:
                        item[1](eng, st.iters - 1, u - item[0])

        def multiply_unit(eng, st, it, u, rhs_wait=None):
            (hi, lo), t0, T, s = st.rhs, st.off, st.T, u % SLOTS
            eng.wait_ge(s_lo[s], turn(st, it, u) + 2)
            for i, (g, k) in enumerate(st.units[u]):
                out = bank[st.banks[g % len(st.banks)]][:, 0:T]
                start, stop = k == st.first_k[g], k == st.last_k[g]
                if start:
                    eng.wait_ge(s_ev, group(st, it, g) + 5 - st.look)
                if g == 0 and rhs_wait:
                    rhs_wait(k)
                xh, xl = hi[:, k, t0:t0 + T], lo[:, k, t0:t0 + T]
                eng.matmul(out, WH[s][:, i, :], xh, start=start, stop=False)
                eng.matmul(out, WH[s][:, i, :], xl, start=False, stop=False)
                mm = eng.matmul(out, WL[s][:, i, :], xh, start=False, stop=stop)
            mm.then_inc(s_pe[s], 1)

        def multiply(eng, st, hooks=None, rhs_wait=None):
            def body(it, first):
                for u in range(len(st.units)):
                    if first and hooks and u in hooks:
                        hooks[u](eng)
                    multiply_unit(eng, st, it, u, rhs_wait if first else None)

            first = bool(hooks or rhs_wait)
            if first:
                body(0, True)
            if st.iters - first:
                with eng.Fori(int(first), st.iters) as it:
                    body(it, False)

        n_x, n_st, n_r, n_h, n_sq, n_ss, n_ln, n_tmp = ([0] for _ in range(8))
        n_ms = [MEMSETS]

        class Norm:
            pass

        def norm_before(gain, T, h_from):
            o = Norm()
            o.gain, o.T, o.off, o.h = gain, T, TM - T, h_from
            o.x0, n_x[0] = n_x[0], n_x[0] + DC
            o.sq, n_sq[0] = n_sq[0], n_sq[0] + 1
            o.ss, n_ss[0] = n_ss[0], n_ss[0] + 1
            o.st, n_st[0] = n_st[0], n_st[0] + 1
            o.ln, n_ln[0] = n_ln[0], n_ln[0] + 1
            o.r, n_r[0] = n_r[0], n_r[0] + 1

            def act(eng):
                for c in range(DC):
                    o.h(eng, c)
                    eng.activation(XH[:, c, 0:T], H[:, c, o.off:TM], ACT.Identity, bias=0.0,
                                   scale=gains[gain][:, c:c + 1]).then_inc(s_xh, 1)

            def square(eng):
                eng.activation(SQ[:, :, 0:T], H[:, :, o.off:TM], ACT.Square).then_inc(s_sq, 1)

            def low(eng, c):
                o.h(eng, c)
                eng.wait_ge(s_xh, o.x0 + c + 1)
                eng.scalar_tensor_tensor(XL[:, c, 0:T], H[:, c, o.off:TM], gains[gain][:, c:c + 1],
                                         XH[:, c, 0:T].bitcast(F32), ALU.mult, ALU.subtract).then_inc(s_xl, 1)

            def dve(eng):
                eng.wait_ge(s_sq, o.sq + 1)
                eng.tensor_reduce(ACC[:, 0:T], SQ[:, :, 0:T].rearrange("p c t -> p t c"), AX.X,
                                  ALU.add).then_inc(s_ss, 1)

            def pe(eng):
                eng.wait_ge(s_ss, o.ss + 1)
                eng.matmul(bank[4][:, 0:T], mean[:, :], ACC[:, 0:T], start=True, stop=True).then_inc(s_st, 1)

            def rstd(eng):
                eng.wait_ge(s_st, o.st + 1)
                eng.activation(R[:, 0:T], bank[4][:, 0:T], ACT.Ln, bias=eps, scale=1.0).then_inc(s_ln, 1)
                eng.wait_ge(s_ln, o.ln + 1)
                eng.activation(R[:, 0:T], R[:, 0:T], ACT.Exp, scale=-0.5).then_inc(s_r, 1)

            o.act, o.square, o.low, o.dve, o.pe, o.rstd = act, square, low, dve, pe, rstd
            o.rhs = lambda eng: lambda k: eng.wait_ge(s_xl, o.x0 + k + 1)
            o.ready = lambda eng: eng.wait_ge(s_r, o.r + 1)
            return o

        def norm_streamed(st, which=0):
            o = Norm()
            o.st, n_st[0] = n_st[0], n_st[0] + 1
            o.ln, n_ln[0] = n_ln[0], n_ln[0] + 1
            o.r, n_r[0] = n_r[0], n_r[0] + 1
            T, G = SEQ, st.groups

            def pe(eng):
                st.dv.wait(eng, st.iters - 1, st.acc_last)
                eng.matmul(bank[4][:, 0:T], mean[:, :], ACC[:, 0:T], start=True, stop=True).then_inc(s_st, 1)

            def rstd(eng):
                eng.wait_ge(s_st, o.st + 1)
                eng.activation(R[:, 0:T], bank[4][:, 0:T], ACT.Ln, bias=eps, scale=1.0).then_inc(s_ln, 1)
                eng.wait_ge(s_ln, o.ln + 1)
                eng.activation(R[:, 0:T], R[:, 0:T], ACT.Exp, scale=-0.5).then_inc(s_r, 1)

            o.pe, o.rstd = pe, rstd
            o.rhs = lambda eng, i=which: lambda k: st.dv.wait(eng, k // G, f"low{i}_{k % G}")
            o.ready = lambda eng: eng.wait_ge(s_r, o.r + 1)
            return o

        def norm_after(st, T):
            o = Norm()
            o.st, n_st[0] = n_st[0], n_st[0] + 1
            o.ln, n_ln[0] = n_ln[0], n_ln[0] + 1
            o.r, n_r[0] = n_r[0], n_r[0] + 1
            o.h0, n_h[0] = n_h[0], n_h[0] + DC
            o.t0, n_tmp[0] = n_tmp[0], n_tmp[0] + DC
            off = TM - T

            def pe(eng):
                st.dv.wait(eng, st.iters - 1, st.acc_last)
                eng.matmul(bank[4][:, 0:T], mean[:, :], ACC[:, 0:T], start=True, stop=True).then_inc(s_st, 1)

            def rstd(eng):
                eng.wait_ge(s_st, o.st + 1)
                eng.activation(RP[:, 0:T], bank[4][:, 0:T], ACT.Ln, bias=eps, scale=1.0).then_inc(s_ln, 1)
                eng.wait_ge(s_ln, o.ln + 1)
                eng.activation(RP[:, 0:T], RP[:, 0:T], ACT.Exp, scale=-0.5).then_inc(s_r, 1)

            def dve(eng, follow):
                eng.wait_ge(s_r, o.r + 1)
                for c in range(DC + 2):
                    if c < DC:
                        eng.tensor_tensor(YG[:, c, 0:T], YG[:, c, 0:T], RP[:, 0:T], ALU.mult).then_inc(s_tmp, 1)
                    if 0 < c <= DC:
                        eng.wait_ge(s_tmp, o.t0 + c)
                        eng.tensor_tensor(H[:, c - 1, off:TM], H[:, c - 1, off:TM], YG[:, c - 1, 0:T],
                                          ALU.add).then_inc(s_h, 1)
                    if c > 1:
                        follow(eng, c - 2)

            o.pe, o.rstd, o.dve = pe, rstd, dve
            o.chunk = lambda eng, c: eng.wait_ge(s_h, o.h0 + c + 1)
            return o

        primed = []

        def steps(kind, name, names):
            s = Steps(sem(f"{kind}_{name}"), names)
            primed.append((kind, s))
            return s

        def leave(st, it, g, ins):
            ins.then_inc(s_ev, 1)

        class UpSteps:

            def __init__(self, st, norm):
                self.st, self.norm = st, norm
                pair = [0, 1]
                self.prods = steps("dve", st.name + "_prod", [f"prod{b}" for b in pair])
                self.lows = steps("dve", st.name + "_low", [f"low{b}" for b in pair])
                self.silus = steps("act", st.name + "_silu", [f"silu{b}" for b in pair])
                self.highs = steps("act", st.name + "_high", [f"high{b}" for b in pair])
                self.order = {"dve": [(0, self.scale), (1, self.prod), "split", (2, self.low)],
                              "act": ["split", (1, self.silu), (2, self.high)],
                              "pool": ["split"] + [(0, lambda eng, it, u: None)]}

            def scale(self, eng, it, u):
                st, T = self.st, self.st.T
                if u == 0:
                    self.norm.ready(eng)
                group_done(eng, st, it, u)
                dst = (CV if u % 2 == 0 else SC)[u // 2][:, 0:T]
                leave(st, it, u, eng.tensor_tensor(dst, bank[st.banks[u]][:, 0:T], R[:, 0:T], ALU.mult))

            def silu(self, eng, it, u):
                b, T = u // 2, self.st.T
                if u % 2 == 0:
                    evacuated(eng, self.st, it, u)
                    self.silus.done(eng.activation(SG[b][:, 0:T], CV[b][:, 0:T], ACT.Silu), f"silu{b}")

            def prod(self, eng, it, u):
                b, T = u // 2, self.st.T
                if u % 2:
                    evacuated(eng, self.st, it, u)
                    self.silus.wait(eng, it, f"silu{b}")
                    self.prods.done(eng.tensor_tensor(PR[b][:, 0:T], SG[b][:, 0:T], SC[b][:, 0:T], ALU.mult),
                                    f"prod{b}")

            def high(self, eng, it, u):
                b, T = u // 2, self.st.T
                if u % 2:
                    self.prods.wait(eng, it, f"prod{b}")
                    self.highs.done(eng.activation(AH[:, bass.ds(it * 2 + b, 1), 0:T], PR[b][:, 0:T].unsqueeze(1),
                                                   ACT.Copy), f"high{b}")

            def low(self, eng, it, u):
                b, T, j = u // 2, self.st.T, it * 2 + u // 2
                if u % 2:
                    self.highs.wait(eng, it, f"high{b}")
                    self.lows.done(eng.tensor_tensor(AL[:, bass.ds(j, 1), 0:T], PR[b][:, 0:T].unsqueeze(1),
                                                     AH[:, bass.ds(j, 1), 0:T].bitcast(F32), ALU.subtract), f"low{b}")

            def rhs_wait(self, eng):
                def wait(k):
                    if k in (0, FC - 2, FC - 1):
                        last = {0: (self.st.iters - 2, "low1"), FC - 2: (self.st.iters - 1, "low0"),
                                FC - 1: (self.st.iters - 1, "low1")}[k]
                        self.lows.wait(eng, *last)
                return wait

        class ConvUpSteps(UpSteps):

            def __init__(self, st, norm, layer):
                self.st, self.norm, self.layer = st, norm, layer
                self.w, self.bias = f"fcw{layer}", f"fcb{layer}"
                pair = [0, 1]
                self.tap2s = steps("act", st.name + "_tap", [f"tap2_{u}" for u in range(4)])
                self.taps = steps("dve", st.name + "_tap", [f"tap{t}_{u}" for u in range(4) for t in (1, 0)])
                self.prods = steps("pool", st.name + "_prod", [f"prod{b}" for b in pair])
                self.lows = steps("pool", st.name + "_low", [f"low{b}" for b in pair])
                self.silus = steps("act", st.name + "_silu", [f"silu{b}" for b in pair])
                self.highs = steps("act", st.name + "_high", [f"high{b}" for b in pair])
                self.order = {"dve": [(0, self.scale), (1, self.tap), "split"],
                              "act": ["split", (0, self.tap2), (2, self.silu), (3, self.high)],
                              "pool": ["split", (2, self.prod), (3, self.low)]}

            def scale(self, eng, it, u):
                st, T = self.st, self.st.T
                if u == 0:
                    self.norm.ready(eng)
                self.taps.wait(eng, it, f"tap0_{(u - 2) % 4}", back=int(u < 2))
                group_done(eng, st, it, u)
                leave(st, it, u, eng.tensor_tensor(TP[u % 2][:, 3:3 + T], bank[st.banks[u]][:, 0:T], R[:, 0:T],
                                                   ALU.mult))

            def dst(self, u):
                return (CV if u % 2 == 0 else SC)[u // 2][:, 0:self.st.T]

            def tap2(self, eng, it, u):
                m, T = it * 4 + u, self.st.T
                evacuated(eng, self.st, it, u)
                if u % 2 == 0:
                    self.silus.wait(eng, it, f"silu{u // 2}", back=1)
                self.tap2s.done(eng.activation(self.dst(u), TP[u % 2][:, 3:3 + T], ACT.Identity,
                                               bias=v(self.bias, m), scale=v(self.w, m + 88)), f"tap2_{u}")

            def tap(self, eng, it, u):
                m, T, dst = it * 4 + u, self.st.T, self.dst(u)
                self.tap2s.wait(eng, it, f"tap2_{u}")
                self.taps.done(eng.scalar_tensor_tensor(dst, TP[u % 2][:, 2:2 + T], v(self.w, m + 44), dst, ALU.mult,
                                                        ALU.add), f"tap1_{u}")
                self.taps.wait(eng, it, f"tap1_{u}")
                self.taps.done(eng.scalar_tensor_tensor(dst, TP[u % 2][:, 1:1 + T], v(self.w, m), dst, ALU.mult,
                                                        ALU.add), f"tap0_{u}")

            def silu(self, eng, it, u):
                b, T = u // 2, self.st.T
                if u % 2 == 0:
                    self.taps.wait(eng, it, f"tap0_{u}")
                    self.silus.done(eng.activation(SG[b][:, 0:T], CV[b][:, 0:T], ACT.Silu), f"silu{b}")

            def prod(self, eng, it, u):
                b, T = u // 2, self.st.T
                if u % 2:
                    self.taps.wait(eng, it, f"tap0_{u}")
                    self.silus.wait(eng, it, f"silu{b}")
                    self.prods.done(eng.tensor_tensor(PR[b][:, 0:T], SG[b][:, 0:T], SC[b][:, 0:T], ALU.mult),
                                    f"prod{b}")

        class NormedSteps:

            def __init__(self, st, gain, factor):
                self.st, self.gain, self.factor = st, gain, factor
                G = st.groups
                self.G = G
                self.dv = steps("dve", st.name, [f"acc{g}" for g in range(G)])
                self.ac = steps("act", st.name, [f"sq{g}" for g in range(G)])
                st.dv, st.acc_last = self.dv, f"acc{G - 1}"

            def before(self, eng):
                eng.memset(ACC[:, :], 0.0).then_inc(s_ms, 1)
                n_ms[0] += 1
                eng.wait_ge(s_ms, n_ms[0])

            def dve(self, eng, it, u):
                st, T = self.st, self.st.T
                for g in range(self.G):
                    if st.unit_of[g] == u:
                        m = it * self.G + g
                        self.ac.wait(eng, it, f"sq{g}")
                        leave(st, it, g, eng.tensor_scalar(YG[:, bass.ds(m, 1), 0:T],
                                                           bank[st.banks[g]][:, 0:T].unsqueeze(1), v(self.gain, m),
                                                           self.factor, ALU.mult, ALU.mult))
                        self.dv.wait(eng, it, f"acc{(g - 1) % self.G}", back=int(g == 0))
                        self.dv.done(eng.tensor_tensor(ACC[:, 0:T], ACC[:, 0:T], SQB[g % 2][:, 0:T], ALU.add),
                                     f"acc{g}")

            def act(self, eng, it, u):
                st, T = self.st, self.st.T
                for g in range(self.G):
                    if st.unit_of[g] == u:
                        group_done(eng, st, it, g)
                        self.dv.wait(eng, it, f"acc{(g - 2) % self.G}", back=int(g < 2))
                        self.ac.done(eng.activation(SQB[g % 2][:, 0:T], bank[st.banks[g]][:, 0:T], ACT.Square),
                                     f"sq{g}")

            def pool(self, eng, it, u):
                pass

        class AddSteps:

            def __init__(self, st, norms):
                self.st, self.norms = st, norms
                G = self.G = st.groups
                n = range(len(norms))
                self.dv = steps("dve", st.name, [x for g in range(G) for x in ([f"low{i}_{g}" for i in n]
                                                                               + [f"acc{g}"])])
                self.ac = steps("act", st.name, [x for g in range(G) for x in ([f"high{i}_{g}" for i in n]
                                                                               + [f"sq{g}"])])
                st.dv, st.acc_last = self.dv, f"acc{G - 1}"

            def before(self, eng):
                eng.memset(ACC[:, :], 0.0).then_inc(s_ms, 1)
                n_ms[0] += 1
                eng.wait_ge(s_ms, n_ms[0])

            def dve(self, eng, it, u):
                st, T = self.st, self.st.T
                for g in range(self.G):
                    if st.unit_of[g] != u:
                        continue
                    m = it * self.G + g
                    h = H[:, bass.ds(m, 1), META:TM]
                    group_done(eng, st, it, g)
                    leave(st, it, g, eng.tensor_tensor(h, bank[st.banks[g]][:, 0:T].unsqueeze(1), h, ALU.add))
                    for i, (gain, hi, lo) in enumerate(self.norms):
                        self.ac.wait(eng, it, f"high{i}_{g}")
                        self.dv.done(eng.scalar_tensor_tensor(lo[:, bass.ds(m, 1), 0:T], h, v(gain, m),
                                                              hi[:, bass.ds(m, 1), 0:T].bitcast(F32), ALU.mult,
                                                              ALU.subtract), f"low{i}_{g}")
                    self.ac.wait(eng, it, f"sq{g}")
                    self.dv.wait(eng, it, f"acc{(g - 1) % self.G}", back=int(g == 0))
                    self.dv.done(eng.tensor_tensor(ACC[:, 0:T], ACC[:, 0:T], SQB[g % 2][:, 0:T], ALU.add), f"acc{g}")

            def act(self, eng, it, u):
                st, T = self.st, self.st.T
                for g in range(self.G):
                    if st.unit_of[g] != u:
                        continue
                    m = it * self.G + g
                    h = H[:, bass.ds(m, 1), META:TM]
                    self.dv.wait(eng, it, f"acc{(g - 2) % self.G}", back=int(g < 2))
                    evacuated(eng, st, it, g)
                    for i, (gain, hi, lo) in enumerate(self.norms):
                        self.ac.done(eng.activation(hi[:, bass.ds(m, 1), 0:T], h, ACT.Identity, bias=0.0,
                                                    scale=v(gain, m)), f"high{i}_{g}")
                    self.ac.done(eng.activation(SQB[g % 2][:, 0:T].unsqueeze(1), h, ACT.Square), f"sq{g}")

            def pool(self, eng, it, u):
                pass

        class ConvSteps:

            def __init__(self, st, norm, w, bias, out, m0, M):
                self.st, self.norm, self.w, self.bias, self.out, self.m0, self.M = st, norm, w, bias, out, m0, M
                self.tap3s = steps("act", st.name + "_tap", [f"tap3_{u}" for u in range(4)])
                self.taps = steps("dve", st.name, [f"tap{t}_{u}" for u in range(4) for t in (2, 1, 0)])
                self.silus = steps("act", st.name, [f"silu{u}" for u in range(4)])
                self.order = {"dve": [(0, self.scale), (1, self.tap), "split"],
                              "act": ["split", (0, self.tap3), (2, self.silu)],
                              "pool": ["split", (0, lambda eng, it, u: None)]}

            def scale(self, eng, it, u):
                st, T = self.st, self.st.T
                if u == 0:
                    self.norm.ready(eng)
                self.taps.wait(eng, it, f"tap0_{(u - 2) % 4}", back=int(u < 2))
                group_done(eng, st, it, u)
                leave(st, it, u, eng.tensor_tensor(TP[u % 2][:, 3:3 + T], bank[st.banks[u]][:, 0:T], R[:, 0:T],
                                                   ALU.mult))

            def tap3(self, eng, it, u):
                m, T = it * 4 + u + self.m0, self.st.T
                evacuated(eng, self.st, it, u)
                self.silus.wait(eng, it, f"silu{u}", back=1)
                self.tap3s.done(eng.activation(CONV[u][:, 0:T], TP[u % 2][:, 3:3 + T], ACT.Identity,
                                               bias=v(self.bias, m) if self.bias else 0.0,
                                               scale=v(self.w, m + 3 * self.M)), f"tap3_{u}")

            def tap(self, eng, it, u):
                m, T, dst = it * 4 + u + self.m0, self.st.T, CONV[u][:, 0:self.st.T]
                self.tap3s.wait(eng, it, f"tap3_{u}")
                for t in (2, 1, 0):
                    self.taps.done(eng.scalar_tensor_tensor(dst, TP[u % 2][:, t:t + T], v(self.w, m + t * self.M), dst,
                                                            ALU.mult, ALU.add), f"tap{t}_{u}")
                    if t:
                        self.taps.wait(eng, it, f"tap{t}_{u}")

            def silu(self, eng, it, u):
                T = self.st.T
                self.taps.wait(eng, it, f"tap0_{u}")
                self.silus.done(eng.activation(self.out(it * 4 + u), CONV[u][:, 0:T].unsqueeze(1), ACT.Silu),
                                f"silu{u}")

        class ScaleSteps:

            def __init__(self, st, norm, out, func=None):
                self.st, self.norm, self.out, self.func = st, norm, out, func
                self.funcs = steps("act", st.name, [f"func{u}" for u in range(4)]) if func else None
                self.order = {"dve": [(0, self.scale), "split"], "act": ["split", (1, self.apply)],
                              "pool": ["split", (0, lambda eng, it, u: None)]}

            def scale(self, eng, it, u):
                st, T = self.st, self.st.T
                if u == 0:
                    self.norm.ready(eng)
                group_done(eng, st, it, u)
                leave(st, it, u, eng.tensor_tensor(self.out(it * 4 + u), bank[st.banks[u]][:, 0:T].unsqueeze(1),
                                                   R[:, TM - T if st.off else 0:][:, 0:T].unsqueeze(1), ALU.mult))

            def apply(self, eng, it, u):
                if self.func:
                    evacuated(eng, self.st, it, u)
                    o = self.out(it * 4 + u)
                    self.funcs.done(eng.activation(o, o, self.func), f"func{u}")

        QK, VT, OG, NMB, ENB = carve(big, big_size, mQK=([P, 8, TM], F32), mVT=([P, 8, TM], F32),
                                     mOG=([P, 8, SEQ], F32), mNMB=([P, 8, SEQ], F32), mENB=([P, 8, SEQ], F32))
        GI, GF, G1, G2, G3, MX = carve(spare, spare_size, **{n: ([A_HEADS, TM], F32) for n in
                                                             ("mGI", "mGF", "mG1", "mG2", "mG3", "mMX")})

        class MGateSteps:

            def __init__(self, st, norm):
                self.st, self.norm = st, norm
                self.dv = steps("dve", st.name, ["one", "gi", "bi", "bf", "neg", "lf", "F", "a", "M", "nm", "negM"])
                self.ac = steps("act", st.name, ["abs", "exp", "ln", "enm"])
                self.ms = sem("dma_mgate_out")
                self.mb = sem("dma_mgate_in")
                self.pe_done = sem("pe_mgate")

            def dve(self, eng, it, u):
                if u != 3:
                    return
                st, d, ac, n = self.st, self.dv, self.ac, A_HEADS
                eng.wait_ge(s_bias, 16)
                d.done(eng.memset(G3[:, :], 1.0), "one")
                self.norm.ready(eng)
                group_done(eng, st, it, 0)
                b = bank[st.banks[0]]
                d.done(eng.tensor_tensor(GI[:, :], b[0:n, 0:TM], R[0:n, :], ALU.mult), "gi")
                leave(st, it, 0, eng.tensor_tensor(GF[:, :], b[32:32 + n, 0:TM], R[32:32 + n, :], ALU.mult))
                d.wait(eng, it, "gi")
                d.done(eng.tensor_scalar(GI[:, :], GI[:, :], vec[0:n, VEC["gate"]:VEC["gate"] + 1], None, ALU.add), "bi")
                evacuated(eng, st, it, 0)
                d.done(eng.tensor_scalar(GF[:, :], GF[:, :], vec[0:n, VEC["gate"] + 1:VEC["gate"] + 2], None,
                                         ALU.add), "bf")
                d.wait(eng, it, "bf")
                d.done(eng.tensor_scalar(MX[:, :], GF[:, :], 0.0, None, ALU.min), "neg")
                ac.wait(eng, it, "ln")
                d.wait(eng, it, "neg")
                d.done(eng.tensor_tensor(G1[:, :], MX[:, :], G2[:, :], ALU.subtract), "lf")
                d.wait(eng, it, "lf")
                d.done(eng.tensor_tensor_scan(GF[:, :], G3[:, :], G1[:, :], 0.0, ALU.mult, ALU.add), "F")
                d.wait(eng, it, "F")
                d.done(eng.tensor_tensor(GI[:, :], GI[:, :], GF[:, :], ALU.subtract), "a")
                d.wait(eng, it, "a")
                d.done(eng.tensor_tensor_scan(MX[:, :], G3[:, :], GI[:, :], 0.0, ALU.mult, ALU.max), "M")
                d.wait(eng, it, "M")
                d.done(eng.tensor_tensor(G1[:, :], GF[:, :], MX[:, :], ALU.add), "nm")
                d.done(eng.tensor_scalar(G2[:, :], MX[:, :], -1.0, None, ALU.mult), "negM")

            def act(self, eng, it, u):
                if u != 3:
                    return
                d, ac = self.dv, self.ac
                d.wait(eng, it, "bf")
                ac.done(eng.activation(G1[:, :], GF[:, :], ACT.Abs), "abs")
                ac.wait(eng, it, "abs")
                ac.done(eng.activation(G2[:, :], G1[:, :], ACT.Exp, scale=-1.0), "exp")
                ac.wait(eng, it, "exp")
                ac.done(eng.activation(G2[:, :], G2[:, :], ACT.Ln, bias=1.0), "ln")
                d.wait(eng, it, "nm")
                ac.done(eng.activation(G1[:, :], G1[:, :], ACT.Exp, scale=-1.0), "enm")

            def pool(self, eng, it, u):
                if u != 3:
                    return
                self.dv.wait(eng, it, "negM")
                eng.dma_start(mx_d[0], G2[:, :]).then_inc(self.ms, 16)
                self.ac.wait(eng, it, "enm")
                eng.dma_start(mx_d[1], G1[:, :]).then_inc(self.ms, 16)
                eng.wait_ge(self.ms, 32)
                for i, dst in enumerate((NMB, ENB)):
                    eng.dma_start(dst[:, :, :], mx_d[i, :, META:TM].partition_broadcast(P)).then_inc(self.mb, 16)

            def pe(self, eng):
                eng.wait_ge(s_cst, 16)
                self.dv.wait(eng, 0, "a")
                for s, (t, n) in enumerate(TOKENS):
                    eng.transpose(bank[5][0:n, s * A_HEADS:(s + 1) * A_HEADS], GI[:, t:t + n],
                                  ident[0:A_HEADS, 0:A_HEADS]).then_inc(self.pe_done, 1)

        TOKENS = [(0, META), (META, P), (META + P, P)]
        mc = carve(work, work_size, mQKs=([P, 2, TM], F32), mVs=([P, 2, TM], F32), mVN0=([P, 3, P], F32),
                   mVN1=([P, 3, P], F32), mDB0=([P, 3 * P], F32), mDB1=([P, 3 * P], F32), mDA0=([META, SEQ], F32),
                   mDA1=([META, SEQ], F32), mAD0=([P, SEQ], F32), mAD1=([P, SEQ], F32), mY0=([P, SEQ], F32),
                   mY1=([P, SEQ], F32))
        QKs, Vs, VN, DB, DA, AD, YM = mc[0], mc[1], mc[2:4], mc[4:6], mc[6:8], mc[8:10], mc[10:12]
        two = (0, 1)

        def names(*parts):
            return [f"{n}{i}" for n in parts for i in two]

        class MCore:

            def __init__(self, gate, prev):
                self.gate, self.prev = gate, prev
                self.aT = sem("act_aT")
                self.ac = steps("act", "mcore", ["qk", "v"] + names("vnA", "vnB", "expB", "expA"))
                self.dv = steps("dve", "mcore", names("dB", "dC", "dA", "wB", "wA"))
                self.po = steps("pool", "mcore", names("mask"))
                self.pe_ = steps("pe", "mcore", names("vT", "qkB", "num", "den"))
                self.ac_end = steps("act", "mcore_end", names("abs", "high"))
                self.dv_end = steps("dve", "mcore_end", names("max", "rec", "og", "y", "low"))

            def run(self, eng, body, end):
                for part in body:
                    part(eng, 0)
                with eng.Fori(1, A_HEADS // 2) as it:
                    body[0](eng, it)
                    end[0](eng, it - 1)
                    body[1](eng, it)
                    end[1](eng, it - 1)
                for part in end:
                    part(eng, A_HEADS // 2 - 1)

            def act(self, eng):
                a, d, o, p = self.ac, self.dv, self.po, self.pe_
                eng.wait_ge(self.gate.pe_done, 3)
                eng.activation(AC[0:META, 0, :], bank[5][0:META, 0:A_HEADS], ACT.Copy).then_inc(self.aT, 1)
                eng.activation(AC[:, 1:3, :], bank[5][:, A_HEADS:3 * A_HEADS].rearrange("p (s h) -> p s h", s=2),
                               ACT.Copy).then_inc(self.aT, 1)
                evacuated(eng, self.prev, self.prev.iters - 1, 3)
                self.qk_ready(eng)

                def copies(eng, it):
                    qk = QK[:, :, :].rearrange("p (x j) t -> p x j t", x=2)
                    p.wait(eng, it, "qkB1", back=1)
                    a.done(eng.activation(QKs[:, :, :].unsqueeze(2), qk[:, :, bass.ds(it, 1), :], ACT.Copy), "qk")
                    a.done(eng.activation(Vs[:, :, :], VT[:, bass.ds(it * 2, 2), :], ACT.Copy), "v")

                def weights(eng, it):
                    for i in two:
                        p.wait(eng, it, f"vT{i}")
                        a.done(eng.activation(VN[i][0:META, 0, :], bank[i][0:META, 0:P], ACT.Copy), f"vnA{i}")
                    for i in two:
                        a.done(eng.activation(VN[i][:, 1:3, :], bank[i][:, P:3 * P].rearrange("p (s e) -> p s e", s=2),
                                              ACT.Copy), f"vnB{i}")
                    for i in two:
                        d.wait(eng, it, f"dC{i}")
                        a.done(eng.activation(DB[i][:, :], DB[i][:, :], ACT.Exp), f"expB{i}")
                    for i in two:
                        d.wait(eng, it, f"dA{i}")
                        a.done(eng.activation(DA[i][:, :], DA[i][:, :], ACT.Exp), f"expA{i}")

                def absolute(eng, it):
                    for i in two:
                        p.wait(eng, it, f"den{i}")
                        self.ac_end.done(eng.activation(AD[i][:, :], bank[7 - 3 * i][:, 0:SEQ], ACT.Abs), f"abs{i}")

                def high(eng, it):
                    for i in two:
                        self.dv_end.wait(eng, it, f"y{i}")
                        self.ac_end.done(eng.activation(XH[:, bass.ds(it * 2 + i, 1), 0:SEQ], YM[i][:, :].unsqueeze(1),
                                                        ACT.Copy), f"high{i}")
                warm(eng, ACT.Exp)
                self.run(eng, (copies, weights), (absolute, high))

            def dve(self, eng):
                a, d, o, p, e = self.ac, self.dv, self.po, self.pe_, self.dv_end
                eng.wait_ge(self.gate.mb, 32)
                eng.wait_ge(self.aT, 2)
                self.og_ready(eng)

                def exponents(eng, it):
                    def m(i, c0, c1):
                        return NMB[:, bass.ds(it * 2 + i, 1), c0:c1]
                    for i in two:
                        p.wait(eng, it, f"den{i}", back=1)
                        d.done(eng.tensor_scalar(DB[i][:, 0:SEQ].unsqueeze(1), m(i, 0, SEQ),
                                                 AC[:, 1, bass.ds(it * 2 + i, 1)], 0.0, ALU.add, ALU.min), f"dB{i}")
                    for i in two:
                        d.done(eng.tensor_scalar(DB[i][:, SEQ:3 * P].unsqueeze(1), m(i, P, SEQ),
                                                 AC[:, 2, bass.ds(it * 2 + i, 1)], 0.0, ALU.add, ALU.min), f"dC{i}")
                    for i in two:
                        d.done(eng.tensor_scalar(DA[i][:, :].unsqueeze(1), NMB[0:META, bass.ds(it * 2 + i, 1), :],
                                                 AC[0:META, 0, bass.ds(it * 2 + i, 1)], 0.0, ALU.add, ALU.min),
                               f"dA{i}")

                def weights(eng, it):
                    for i in two:
                        p.wait(eng, it, f"qkB{i}")
                        o.wait(eng, it, f"mask{i}")
                        d.done(eng.scalar_tensor_tensor(DB[i][:, :], bank[2 + i][:, 0:3 * P], A_DK ** -0.5, DB[i][:, :],
                                                        ALU.mult, ALU.mult), f"wB{i}")
                    for i in two:
                        a.wait(eng, it, f"expA{i}")
                        d.done(eng.scalar_tensor_tensor(DA[i][:, :], bank[7 - 3 * i][0:META, SEQ:2 * SEQ],
                                                        A_DK ** -0.5, DA[i][:, :], ALU.mult, ALU.mult), f"wA{i}")

                def output(eng, it):
                    for i in two:
                        self.ac_end.wait(eng, it, f"abs{i}")
                        e.done(eng.tensor_tensor(AD[i][:, :].unsqueeze(1), AD[i][:, :].unsqueeze(1),
                                                 ENB[:, bass.ds(it * 2 + i, 1), :], ALU.max), f"max{i}")
                    for i in two:
                        e.wait(eng, it, f"max{i}")
                        e.done(eng.reciprocal(AD[i][:, :], AD[i][:, :]), f"rec{i}")
                    for i in two:
                        e.wait(eng, it, f"rec{i}")
                        e.done(eng.tensor_tensor(AD[i][:, :].unsqueeze(1), AD[i][:, :].unsqueeze(1),
                                                 OG[:, bass.ds(it * 2 + i, 1), :], ALU.mult), f"og{i}")
                    for i in two:
                        e.wait(eng, it, f"og{i}")
                        p.wait(eng, it, f"num{i}")
                        self.ac_end.wait(eng, it, f"high{i}", back=1)
                        e.done(eng.tensor_tensor(YM[i][:, :], bank[5 + i][:, 0:SEQ], AD[i][:, :], ALU.mult), f"y{i}")
                def low(eng, it):
                    for i in two:
                        self.ac_end.wait(eng, it, f"high{i}")
                        e.wait(eng, it, f"y{i}")
                        e.done(eng.tensor_tensor(XL[:, bass.ds(it * 2 + i, 1), 0:SEQ], YM[i][:, :].unsqueeze(1),
                                                 XH[:, bass.ds(it * 2 + i, 1), 0:SEQ].bitcast(F32), ALU.subtract),
                               f"low{i}")
                self.run(eng, (exponents, weights), (output, low))

            def pool(self, eng):
                eng.wait_ge(s_cst, 16)
                with eng.Fori(0, A_HEADS // 2) as it:
                    for i in two:
                        self.ac.wait(eng, it, f"expB{i}")
                        dd = DB[i][:, :].rearrange("p (s t) -> p s t", t=P)[:, 0:3:2, :]
                        self.po.done(eng.tensor_tensor(dd, dd, causal.unsqueeze(1).to_broadcast([P, 2, P]), ALU.mult),
                                     f"mask{i}")

            def pe(self, eng):
                a, d, p = self.ac, self.dv, self.pe_
                evacuated(eng, self.prev, self.prev.iters - 1, 3)
                eng.wait_ge(self.aT, 2)
                with eng.Fori(0, A_HEADS // 2) as it:
                    a.wait(eng, it, "v")
                    for i in two:
                        a.wait(eng, it, f"vnB{i}", back=1)
                        for s, (t, n) in enumerate(TOKENS):
                            mm = eng.transpose(bank[i][0:n, s * P:(s + 1) * P], Vs[:, i, t:t + n], ident)
                        p.done(mm, f"vT{i}")
                    for i in two:
                        h0 = 64 * i
                        self.ac_end.wait(eng, it, f"abs{i}", back=1)
                        q, k = QKs[h0:h0 + 64, 0, :], QKs[h0:h0 + 64, 1, :]
                        eng.matmul(bank[2 + i][:, 0:SEQ], k[:, META:META + P], q[:, META:TM], start=True, stop=True)
                        eng.matmul(bank[7 - 3 * i][0:META, SEQ:2 * SEQ], k[:, 0:META], q[:, META:TM],
                                   start=True, stop=True)
                        p.done(eng.matmul(bank[2 + i][:, SEQ:3 * P], k[:, META + P:TM], q[:, META + P:TM],
                                          start=True, stop=True), f"qkB{i}")
                    for i in two:
                        self.dv_end.wait(eng, it, f"y{i}", back=1)
                        d.wait(eng, it, f"wA{i}")
                        a.wait(eng, it, f"vnB{i}")
                        out = bank[5 + i]
                        eng.matmul(out[:, 0:SEQ], VN[i][0:META, 0, :], DA[i][:, :], start=True, stop=False)
                        eng.matmul(out[:, 0:SEQ], VN[i][:, 1, :], DB[i][:, 0:SEQ], start=False, stop=False)
                        p.done(eng.matmul(out[:, P:SEQ], VN[i][:, 2, :], DB[i][:, SEQ:3 * P], start=False, stop=True),
                               f"num{i}")
                    for i in two:
                        den = bank[7 - 3 * i]
                        eng.matmul(den[:, 0:SEQ], ones[0:META, :], DA[i][:, :], start=True, stop=False)
                        eng.matmul(den[:, 0:SEQ], ones[:, :], DB[i][:, 0:SEQ], start=False, stop=False)
                        p.done(eng.matmul(den[:, P:SEQ], ones[:, :], DB[i][:, SEQ:3 * P], start=False,
                                          stop=True), f"den{i}")

            def rhs_wait(self, eng):
                def wait(k):
                    if k % 2 == 0:
                        self.dv_end.wait(eng, k // 2, "low1")
                return wait

        dQK, dVT, GCB = carve(ext, ext_size, dQK=([P, 16, SEQ], F32), dVT=([P, 16, SEQ], F32), dGCB=([P, 16, SEQ], F32))
        dB, dA, d1, d2, dO, dG, dE = carve(spare, spare_size, **{n: ([GDN_V, SEQ if n != "dE" else 8], F32) for n in
                                                                  ("dB", "dA", "d1", "d2", "dO", "dG", "dE")})
        HG = 4
        four = range(HG)

        class GGateSteps:

            def __init__(self, st, norm):
                self.st, self.norm = st, norm
                self.dv = steps("dve", st.name, ["one", "b", "x", "pos", "b1", "beta", "sp", "g", "gc0", "gc1"])
                self.ac = steps("act", st.name, ["ea", "eb", "abs", "exp", "ln"])
                self.ms, self.mb, self.pe_done = sem("dma_ggate_out"), sem("dma_ggate_in"), sem("pe_ggate")

            def dve(self, eng, it, u):
                if u != 3:
                    return
                st, d, ac, n = self.st, self.dv, self.ac, GDN_V
                d.done(eng.memset(dO[:, :], 1.0), "one")
                self.norm.ready(eng)
                group_done(eng, st, it, 0)
                b = bank[st.banks[0]]
                d.done(eng.tensor_tensor(dB[:, :], b[0:n, 0:SEQ], R[0:n, 0:SEQ], ALU.mult), "b")
                leave(st, it, 0, eng.tensor_tensor(dA[:, :], b[32:32 + n, 0:SEQ], R[32:32 + n, 0:SEQ], ALU.mult))
                evacuated(eng, st, it, 0)
                d.done(eng.tensor_scalar(dA[:, :], dA[:, :], vec[0:n, VEC["dn"] + 1:VEC["dn"] + 2], None, ALU.add), "x")
                d.wait(eng, it, "x")
                d.done(eng.tensor_scalar(dG[:, :], dA[:, :], 0.0, None, ALU.max), "pos")
                ac.wait(eng, it, "eb")
                d.done(eng.tensor_scalar(dB[:, :], dB[:, :], 1.0, None, ALU.add), "b1")
                d.wait(eng, it, "b1")
                d.done(eng.reciprocal(dB[:, :], dB[:, :]), "beta")
                ac.wait(eng, it, "ln")
                d.done(eng.tensor_tensor(dG[:, :], dG[:, :], d2[:, :], ALU.add), "sp")
                d.wait(eng, it, "sp")
                d.done(eng.tensor_scalar(dG[:, :], dG[:, :], dE[:, 0:1], -1.0, ALU.mult, ALU.mult), "g")
                d.wait(eng, it, "g")
                for c in (0, 1):
                    s = slice(c * P, (c + 1) * P)
                    d.done(eng.tensor_tensor_scan(dA[:, s], dO[:, s], dG[:, s], 0.0, ALU.mult, ALU.add), f"gc{c}")

            def act(self, eng, it, u):
                if u != 3:
                    return
                d, ac = self.dv, self.ac
                ac.done(eng.activation(dE[:, 0:1], vec[0:GDN_V, VEC["dn"]:VEC["dn"] + 1], ACT.Exp), "ea")
                d.wait(eng, it, "b")
                ac.done(eng.activation(dB[:, :], dB[:, :], ACT.Exp, scale=-1.0), "eb")
                d.wait(eng, it, "x")
                ac.done(eng.activation(d1[:, :], dA[:, :], ACT.Abs), "abs")
                ac.wait(eng, it, "abs")
                ac.done(eng.activation(d2[:, :], d1[:, :], ACT.Exp, scale=-1.0), "exp")
                ac.wait(eng, it, "exp")
                ac.done(eng.activation(d2[:, :], d2[:, :], ACT.Ln, bias=1.0), "ln")

            def pool(self, eng, it, u):
                if u != 3:
                    return
                self.dv.wait(eng, it, "gc1")
                eng.dma_start(gc_d, dA[:, :]).then_inc(self.ms, 16)
                eng.wait_ge(self.ms, 16)
                eng.dma_start(GCB[:, :, :], gc_d.partition_broadcast(P)).then_inc(self.mb, 16)

            def pe(self, eng):
                self.dv.wait(eng, 0, "gc1")
                for c in (0, 1):
                    for q, src in enumerate((dA, dB)):
                        o = (2 * c + q) * GDN_V
                        eng.transpose(bank[5][:, o:o + GDN_V], src[:, c * P:(c + 1) * P],
                                      ident[0:GDN_V, 0:GDN_V]).then_inc(self.pe_done, 1)

        class VZSteps:

            def __init__(self, st, norm, g0):
                self.st, self.norm, self.g0 = st, norm, g0
                self.tap3s = steps("act", st.name + "_tap", [f"tap3_{u}" for u in range(HG)])
                self.taps = steps("dve", st.name, [f"tap{t}_{u}" for u in range(HG) for t in (2, 1, 0)])
                self.silus = steps("act", st.name, [f"silu{u}" for u in range(2 * HG)])
                self.order = {"dve": [(0, self.scale), (1, self.tap), "split"],
                              "act": ["split", (0, self.tap3), (2, self.silu)],
                              "pool": ["split", (0, lambda eng, it, u: None)]}

            def out(self, it, u):
                m = it * HG + self.g0 * HG + u % HG
                return (dVT if u < HG else Z)[:, bass.ds(m, 1), :]

            def scale(self, eng, it, u):
                st, T = self.st, self.st.T
                if u == 0:
                    self.norm.ready(eng)
                if u < HG:
                    self.taps.wait(eng, it, f"tap0_{(u - 2) % HG}", back=int(u < 2))
                group_done(eng, st, it, u)
                src = bank[st.banks[u % len(st.banks)]][:, 0:T]
                if u < HG:
                    leave(st, it, u, eng.tensor_tensor(TP[u % 2][:, 3:3 + T], src, R[:, 0:T], ALU.mult))
                else:
                    leave(st, it, u, eng.tensor_tensor(self.out(it, u), src.unsqueeze(1), R[:, 0:T].unsqueeze(1),
                                                       ALU.mult))

            def tap3(self, eng, it, u):
                if u >= HG:
                    return
                m, T = it * HG + self.g0 * HG + 16 + u, self.st.T
                evacuated(eng, self.st, it, u)
                self.tap3s.done(eng.activation(self.out(it, u), TP[u % 2][:, 3:3 + T].unsqueeze(1), ACT.Identity,
                                               bias=0.0, scale=v("dcw", m + 3 * 32)), f"tap3_{u}")

            def tap(self, eng, it, u):
                if u >= HG:
                    return
                m, T = it * HG + self.g0 * HG + 16 + u, self.st.T
                self.tap3s.wait(eng, it, f"tap3_{u}")
                for t in (2, 1, 0):
                    self.taps.done(eng.scalar_tensor_tensor(self.out(it, u), TP[u % 2][:, t:t + T].unsqueeze(1),
                                                            v("dcw", m + t * 32), self.out(it, u), ALU.mult, ALU.add),
                                   f"tap{t}_{u}")
                    if t:
                        self.taps.wait(eng, it, f"tap{t}_{u}")

            def silu(self, eng, it, u):
                if u < HG:
                    self.taps.wait(eng, it, f"tap0_{u}")
                else:
                    evacuated(eng, self.st, it, u)
                self.silus.done(eng.activation(self.out(it, u), self.out(it, u), ACT.Silu), f"silu{u}")

        t4 = ([P, HG, P], F32)
        KN, RT, VG, VB0, VB1 = carve(core_at, core_size, gKN=([P, 2, 2, SEQ], F32), gRT=([P, 2, 2, SEQ], F32),
                                     gVG=([P, HG, SEQ], F32), gVB0=t4, gVB1=t4)
        _, Lm0, Lm1, OT = carve(core_at, core_size, gx0=([P, 2, 2, SEQ], F32), gL0=t4, gL1=t4, gOT=([P, HG, SEQ], F32))
        _, SQ2 = carve(core_at, core_size, gx1=([P, 2, 2, SEQ], F32), gSQ2=([P, HG, SEQ], F32))
        E0, E1, EA0, EA1, T0, T1, U0, U1, Y0, Y1, KD, QD, CG, KC, NB, EGC = carve(
            work, work_size, gE0=t4, gE1=t4, gEA0=t4, gEA1=t4, gT0=t4, gT1=t4, gU0=t4, gU1=t4, gY0=t4, gY1=t4,
            gKD=t4, gQD=t4, gCG=([P, 2, 2, HG], F32), gKC=([P, HG], F32), gNB=([P, HG], F32), gEGC=([P, HG], F32))
        RO, = carve(work, work_size, gRO=([P, HG, SEQ], F32))
        _, _, _, _, S0, R1 = carve(work, work_size, gy0=t4, gy1=t4, gy2=t4, gy3=t4, gS0=t4, gR1=t4)
        VB, L, E, EA, T_, U_, Y_ = (VB0, VB1), (Lm0, Lm1), (E0, E1), (EA0, EA1), (T0, T1), (U0, U1), (Y0, Y1)

        def heads(ap, n):
            return ap.rearrange("p (h c) -> p h c", h=n)

        def nn(*parts):
            return [f"{x}{n}" for x in parts for n in (0, 1)]

        class GCore:

            def __init__(self, gate, prev, fill):
                self.gate, self.prev, self.cols = gate, prev, sem("act_cols")
                self.fill, self.last = fill, GDN_V // HG - 1
                self.silu_v = steps("act", "gcore_v", ["v"])
                self.silu_z = steps("act", "gcore_z", ["z"])
                lv = range(1, LEVELS)
                self.ac = steps("act", "gcore", ["sq", "ln0", "ln1", "rs", "vg", "kce", "egc"] + nn("ex", "exa") + ["eg"]
                                + nn("u") + [f"yc{l}_{n}" for l in lv for n in (0, 1)]
                                + ["vnc0", "sc", "ot0", "vnc1", "ot1", "sq2", "ln2_0", "ln2_1", "ro", "high"])
                self.dv = steps("dve", "gcore", ["cg", "kc"] + nn("e", "ea") + ["kn", "qn", "nb", "vb0", "vb1", "kd"]
                                + nn("m") + nn("t") + nn("at")
                                + [f"{x}{l}_{n}" for l in lv for n in (0, 1) for x in (("du", "dt") if l < LEVELS - 1
                                                                                     else ("du",))]
                                + ["r1", "yo", "yz", "low"])
                self.po = steps("pool", "gcore", nn("em") + [f"l0_{n}" for n in (0, 1)] + ["l1_0", "l1_1", "qd"]
                                + [f"l{l}_{n}" for l in lv if l > 1 for n in (0, 1)])
                self.pe_ = steps("pe", "gcore", ["ss0", "ss1", "vt0", "vt1", "kt", "gr0", "gr1", "tt0", "tt1"]
                                 + [f"{x}{l}_{n}" for l in lv
                                    for x, n in (("y", 0), ("y", 1), ("pu", 0), ("pt", 0), ("pu", 1), ("pt", 1))
                                    if x != "pt" or l < LEVELS - 1]
                                 + ["vn0", "s", "o0", "ks", "vn1", "o1", "oss0", "oss1"])

            def run(self, eng, body):
                with eng.Fori(0, self.last) as it:
                    body(it, True)
                body(self.last, False)

            def split_for(self, eng, kind, it, u):
                st = self.fill.st
                n = u + SLOTS
                split(eng, kind, st, it if n < len(st.units) else it + 1, n % len(st.units))

            def act(self, eng):
                a, d, o, p = self.ac, self.dv, self.po, self.pe_
                eng.wait_ge(self.gate.pe_done, 4)
                eng.activation(COLS[:, :, :, :], bank[5][:, 0:4 * GDN_V].rearrange("p (c q h) -> p c q h", c=2, q=2),
                               ACT.Copy).then_inc(self.cols, 1)
                evacuated(eng, self.prev, self.prev.iters - 1, self.prev.groups - 1)
                self.qkv_ready(eng)
                f = self.fill

                def body(it, filled):
                    def hi(*units):
                        for u in units:
                            if filled:
                                self.split_for(eng, "act", it, u)

                    p.wait(eng, it, "oss1", back=1)
                    a.done(eng.activation(RT[:, :, :, :].rearrange("p a b t -> p (a b) t"),
                                          dQK[:, bass.ds(it * 4, 4), :], ACT.Square), "sq")
                    hi(0)
                    for i in two:
                        p.wait(eng, it, f"ss{i}")
                        a.done(eng.activation(RT[:, i, :, :], bank[i][:, :].rearrange("p (b t) -> p b t", b=2), ACT.Ln,
                                              bias=eps), f"ln{i}")
                    a.wait(eng, it, "ln1")
                    a.done(eng.activation(RT[:, :, :, :], RT[:, :, :, :], ACT.Exp, scale=-0.5), "rs")
                    if filled:
                        f.tap3(eng, it, 0)
                    self.silu_v.wait(eng, it, "v", back=1)
                    d.wait(eng, it, "low", back=1)
                    a.done(eng.activation(VG[:, :, :], dVT[:, bass.ds(it * HG, HG), :], ACT.Copy), "vg")
                    hi(1)
                    if filled:
                        f.tap3(eng, it, 1)
                    d.wait(eng, it, "kc")
                    a.done(eng.activation(KC[:, :], KC[:, :], ACT.Exp), "kce")
                    a.done(eng.activation(EGC[:, :], CG[:, 1, 0, :], ACT.Exp), "egc")
                    for n in two:
                        d.wait(eng, it, f"e{n}")
                        a.done(eng.activation(E[n][:, :, :], E[n][:, :, :], ACT.Exp, scale=-1.0), f"ex{n}")
                    for n in two:
                        d.wait(eng, it, f"ea{n}")
                        a.done(eng.activation(EA[n][:, :, :], EA[n][:, :, :], ACT.Exp), f"exa{n}")
                    a.done(eng.activation(QD[:, :, :], GCB[:, bass.ds(it * HG, HG), P:SEQ], ACT.Exp), "eg")
                    hi(2)
                    if filled:
                        f.tap3(eng, it, 2)
                    hi(3)
                    for n in two:
                        p.wait(eng, it, f"tt{n}")
                        a.done(eng.activation(U_[n][:, :, :], heads(bank[n][:, :], HG), ACT.Copy), f"u{n}")
                    if filled:
                        f.tap3(eng, it, 3)
                    for l in range(1, LEVELS):
                        for n in two:
                            p.wait(eng, it, f"y{l}_{n}")
                            a.done(eng.activation(Y_[n][:, :, :], heads(bank[n][:, :], HG), ACT.Copy), f"yc{l}_{n}")
                    p.wait(eng, it, "vn0")
                    a.done(eng.activation(Y_[0][:, :, :], heads(bank[5][:, :], HG), ACT.Copy), "vnc0")
                    p.wait(eng, it, "s")
                    a.done(eng.activation(S0[:, :, :], heads(bank[1][:, :], HG), ACT.Copy), "sc")
                    p.wait(eng, it, "o0")
                    a.done(eng.activation(OT[:, :, 0:P], heads(bank[6][:, :], HG), ACT.Copy), "ot0")
                    hi(4, 5)
                    p.wait(eng, it, "vn1")
                    a.done(eng.activation(Y_[1][:, :, :], heads(bank[2][:, :], HG), ACT.Copy), "vnc1")
                    p.wait(eng, it, "o1")
                    a.done(eng.activation(OT[:, :, P:SEQ], heads(bank[3][:, :], HG), ACT.Copy), "ot1")
                    a.wait(eng, it, "ot1")
                    a.done(eng.activation(SQ2[:, :, :], OT[:, :, :], ACT.Square), "sq2")
                    for i in two:
                        p.wait(eng, it, f"oss{i}")
                        a.done(eng.activation(RO[:, 2 * i:2 * i + 2, :], bank[5 + i][:, :].rearrange(
                            "p (h t) -> p h t", h=2), ACT.Ln, bias=eps, scale=1.0 / P), f"ln2_{i}")
                    a.wait(eng, it, "ln2_1")
                    a.done(eng.activation(RO[:, :, :], RO[:, :, :], ACT.Exp, scale=-0.5), "ro")
                    if filled:
                        f.taps.wait(eng, it, "tap0_3")
                    hi(6, 7)
                    d.wait(eng, it, "yz")
                    for h in (2, 0):
                        ins = eng.activation(YH[:, bass.ds(it * HG + h, 2), :], OT[:, h:h + 2, :], ACT.Copy)
                    a.done(ins, "high")
                    if not filled:
                        return
                    vs, zs = (t[:, bass.ds(it * HG + HG, HG), :] for t in (dVT, Z))
                    self.silu_v.done(eng.activation(vs, vs, ACT.Silu), "v")
                    evacuated(eng, f.st, it, 7)
                    self.silu_z.done(eng.activation(zs, zs, ACT.Silu), "z")

                self.run(eng, body)

            def dve(self, eng):
                a, d, o, p = self.ac, self.dv, self.po, self.pe_
                eng.wait_ge(s_cst, 16)
                eng.wait_ge(self.gate.mb, 16)
                eng.wait_ge(self.cols, 1)
                self.z_ready(eng)
                f = self.fill

                def body(it, filled):
                    def scale(u):
                        if filled:
                            f.scale(eng, it, u)
                            self.split_for(eng, "dve", it, u)

                    def tap(u):
                        if filled:
                            f.tap(eng, it, u)

                    g = [GCB[:, bass.ds(it * HG + h, 1), :] for h in four]
                    d.done(eng.tensor_copy(CG[:, :, :, :], COLS[:, :, :, bass.ds(it * HG, HG)]), "cg")
                    d.wait(eng, it, "cg")
                    d.done(eng.tensor_tensor(KC[:, :].unsqueeze(2), GCB[:, bass.ds(it * HG, HG), P - 1:P],
                                             CG[:, 0, 0, :].unsqueeze(2), ALU.subtract), "kc")
                    for n in two:
                        for h in four:
                            ins = eng.tensor_scalar(E[n][:, h:h + 1, :], g[h][:, :, n * P:(n + 1) * P],
                                                    CG[:, n, 0, h:h + 1], 0.0, ALU.subtract, ALU.max)
                        d.done(ins, f"e{n}")
                    scale(0)
                    for n in two:
                        for h in four:
                            ins = eng.tensor_scalar(EA[n][:, h:h + 1, :], g[h][:, :, n * P:(n + 1) * P],
                                                    CG[:, n, 0, h:h + 1], 0.0, ALU.subtract, ALU.min)
                        d.done(ins, f"ea{n}")
                    qk = dQK[:, bass.ds(it * 4, 4), :]
                    a.wait(eng, it, "rs")
                    o.wait(eng, it, "qd", back=1)
                    kn4 = KN[:, :, :, :].rearrange("p a b t -> p (a b) t")
                    rt4 = RT[:, :, :, :].rearrange("p a b t -> p (a b) t")
                    d.done(eng.tensor_tensor(kn4[:, 0:4:2, :], qk[:, 0:4:2, :], rt4[:, 0:4:2, :], ALU.mult), "kn")
                    d.done(eng.scalar_tensor_tensor(kn4[:, 1:4:2, :], qk[:, 1:4:2, :], float(P) ** -0.5,
                                                    rt4[:, 1:4:2, :], ALU.mult, ALU.mult), "qn")
                    scale(1)
                    a.wait(eng, it, "egc")
                    d.done(eng.scalar_tensor_tensor(NB[:, :], EGC[:, :], -1.0, CG[:, 1, 1, :], ALU.mult, ALU.mult), "nb")
                    for n in two:
                        p.wait(eng, it, f"vt{n}")
                        d.done(eng.tensor_tensor(VB[n][:, :, :], heads(bank[2 + n][:, :], HG),
                                                 CG[:, n, 1, :].unsqueeze(2).to_broadcast([P, HG, P]), ALU.mult), f"vb{n}")
                    p.wait(eng, it, "kt")
                    a.wait(eng, it, "kce")
                    for i in two:
                        ins = eng.tensor_tensor(KD[:, 2 * i:2 * i + 2, :],
                                                bank[4][:, i * P:(i + 1) * P].unsqueeze(1).to_broadcast([P, 2, P]),
                                                KC[:, 2 * i:2 * i + 2].unsqueeze(2).to_broadcast([P, 2, P]), ALU.mult)
                    d.done(ins, "kd")
                    tap(0)
                    scale(2)
                    for n in two:
                        gram = bank[5 + n][:, :].rearrange("p (i x c) -> p i x c", i=2, x=2)
                        p.wait(eng, it, f"gr{n}")
                        a.wait(eng, it, f"ex{n}")
                        for h in four:
                            ins = eng.scalar_tensor_tensor(E[n][:, h, :], gram[:, h // 2, 0, :], CG[:, n, 1, h:h + 1],
                                                           E[n][:, h, :], ALU.mult, ALU.mult)
                        d.done(ins, f"m{n}")
                    for n in two:
                        o.wait(eng, it, f"l0_{n}")
                        d.done(eng.tensor_tensor(T_[n][:, :, :], ident.unsqueeze(1).to_broadcast([P, HG, P]),
                                                 L[n][:, :, :], ALU.subtract), f"t{n}")
                    tap(1)
                    scale(3)
                    for n in two:
                        gram = bank[5 + n][:, :].rearrange("p (i x c) -> p i x c", i=2, x=2)
                        o.wait(eng, it, f"em{n}")
                        for i in two:
                            ins = eng.tensor_tensor(EA[n][:, 2 * i:2 * i + 2, :],
                                                    gram[:, i, 1, :].unsqueeze(1).to_broadcast([P, 2, P]),
                                                    EA[n][:, 2 * i:2 * i + 2, :], ALU.mult)
                        d.done(ins, f"at{n}")
                    for l in range(1, LEVELS):
                        if l in (2, 3):
                            tap(l)
                        for n in two:
                            p.wait(eng, it, f"pu{l}_{n}")
                            if l > 1:
                                d.wait(eng, it, f"du{l - 1}_{n}")
                            d.done(eng.tensor_tensor(U_[n][:, :, :], U_[n][:, :, :], heads(bank[2 + n][:, :], HG),
                                                     ALU.subtract), f"du{l}_{n}")
                            if l < LEVELS - 1:
                                p.wait(eng, it, f"pt{l}_{n}")
                                d.wait(eng, it, f"t{n}" if l == 1 else f"dt{l - 1}_{n}")
                                d.done(eng.tensor_tensor(T_[n][:, :, :], T_[n][:, :, :],
                                                         heads(bank[4 + 3 * n][:, :], HG), ALU.subtract), f"dt{l}_{n}")
                    scale(4)
                    p.wait(eng, it, "ks")
                    for h in four:
                        ins = eng.scalar_tensor_tensor(R1[:, h, :], bank[0][:, h * P:(h + 1) * P], NB[:, h:h + 1],
                                                       VB[1][:, h, :], ALU.mult, ALU.add)
                    d.done(ins, "r1")
                    scale(5)
                    a.wait(eng, it, "ro")
                    d.done(eng.scalar_tensor_tensor(OT[:, :, :], OT[:, :, :], v("onw", 0), RO[:, :, :], ALU.mult,
                                                    ALU.mult), "yo")
                    d.wait(eng, it, "yo")
                    self.silu_z.wait(eng, it, "z", back=1)
                    d.done(eng.tensor_tensor(OT[:, :, :], OT[:, :, :], Z[:, bass.ds(it * HG, HG), :], ALU.mult), "yz")
                    scale(6)
                    scale(7)
                    a.wait(eng, it, "high")
                    d.wait(eng, it, "yz")
                    d.done(eng.tensor_tensor(YL[:, bass.ds(it * HG, HG), :], OT[:, :, :],
                                             YH[:, bass.ds(it * HG, HG), :].bitcast(F32), ALU.subtract), "low")

                self.run(eng, body)

            def pool(self, eng):
                a, d, o, p = self.ac, self.dv, self.po, self.pe_

                def body(it, filled):
                    def lo(u):
                        if filled:
                            self.split_for(eng, "pool", it, u)

                    for n in two:
                        a.wait(eng, it, f"exa{n}")
                        o.done(eng.tensor_tensor(EA[n][:, :, :], EA[n][:, :, :],
                                                 causal.unsqueeze(1).to_broadcast([P, HG, P]), ALU.mult), f"em{n}")

                    def level(l, n):
                        m = cst[:, C_LEVEL + l * P:C_LEVEL + (l + 1) * P]
                        if l == 0:
                            d.wait(eng, it, f"m{n}")
                        elif l == 1:
                            d.wait(eng, it, f"t{n}")
                        else:
                            p.wait(eng, it, f"y{l - 1}_{n}")
                        o.done(eng.tensor_tensor(L[n][:, :, :], E[n][:, :, :],
                                                 m.unsqueeze(1).to_broadcast([P, HG, P]), ALU.mult), f"l{l}_{n}")
                    for n in two:
                        level(0, n)
                    for n in two:
                        level(1, n)
                    a.wait(eng, it, "eg")
                    for i in two:
                        ins = eng.tensor_tensor(QD[:, 2 * i:2 * i + 2, :], QD[:, 2 * i:2 * i + 2, :],
                                                KN[:, i, 1, P:SEQ].unsqueeze(1).to_broadcast([P, 2, P]), ALU.mult)
                    o.done(ins, "qd")
                    for u in range(4):
                        lo(u)
                    for l in range(2, LEVELS):
                        for n in two:
                            level(l, n)
                    for u in range(4, 8):
                        lo(u)

                self.run(eng, body)

            def pe(self, eng):
                a, d, o, p = self.ac, self.dv, self.po, self.pe_
                evacuated(eng, self.prev, self.prev.iters - 1, self.prev.groups - 1)
                eng.wait_ge(self.cols, 1)

                def each(out, lhs, rhs, start=True, stop=True):
                    for h in four:
                        mm = eng.matmul(out[:, h * P:(h + 1) * P], lhs[:, h, :], rhs[:, h, :], start=start, stop=stop)
                    return mm

                f = self.fill

                def body(it, filled):
                    def other(u):
                        if filled:
                            multiply_unit(eng, f.st, it, u)

                    other(0)
                    a.wait(eng, it, "sq")
                    d.wait(eng, it, "r1", back=1)
                    for i in two:
                        p.done(eng.matmul(bank[i][:, :], ones[:, :], RT[:, i, :, :].rearrange("p b t -> p (b t)"),
                                          start=True, stop=True), f"ss{i}")
                    other(1)
                    a.wait(eng, it, "vg")
                    for n in two:
                        for h in four:
                            mm = eng.transpose(bank[2 + n][:, h * P:(h + 1) * P], VG[:, h, n * P:(n + 1) * P], ident)
                        p.done(mm, f"vt{n}")
                    if filled:
                        evacuated(eng, f.st, it, 1)
                    d.wait(eng, it, "kn")
                    for i in two:
                        mm = eng.transpose(bank[4][:, i * P:(i + 1) * P], KN[:, i, 0, 0:P], ident)
                    p.done(mm, "kt")
                    other(2)
                    d.wait(eng, it, "qn")
                    for n in two:
                        for i in two:
                            mm = eng.matmul(bank[5 + n][:, i * 2 * P:(i + 1) * 2 * P].rearrange("p (x c) -> p x c", x=2),
                                            KN[:, i, 0, n * P:(n + 1) * P], KN[:, i, :, n * P:(n + 1) * P],
                                            start=True, stop=True)
                        p.done(mm, f"gr{n}")
                    if filled:
                        d.wait(eng, it, "kd")
                        other(3)
                    for n in two:
                        d.wait(eng, it, f"t{n}")
                        a.wait(eng, it, f"ln{n}")
                        for h in four:
                            mm = eng.transpose(bank[n][:, h * P:(h + 1) * P], T_[n][:, h, :], ident)
                        p.done(mm, f"tt{n}")
                    for l in range(1, LEVELS):
                        for n in two:
                            a.wait(eng, it, f"u{n}" if l == 1 else f"yc{l - 1}_{n}")
                            if l > 1:
                                d.wait(eng, it, f"du{l - 1}_{n}")
                            o.wait(eng, it, f"l{l}_{n}")
                            p.done(each(bank[n], L[n], U_[n]), f"y{l}_{n}")
                        for n in two:
                            a.wait(eng, it, f"yc{l}_{n}")
                            if l == 1:
                                d.wait(eng, it, "kd")
                                if filled:
                                    evacuated(eng, f.st, it, 3)
                            else:
                                d.wait(eng, it, f"dt{l - 1}_{n}")
                            p.done(each(bank[2 + n], T_[n], Y_[n]), f"pu{l}_{n}")
                            if l < LEVELS - 1:
                                p.done(each(bank[4 + 3 * n], Y_[n], T_[n]), f"pt{l}_{n}")
                    d.wait(eng, it, f"du{LEVELS - 1}_0")
                    p.done(each(bank[5], U_[0], VB[0]), "vn0")
                    a.wait(eng, it, "vnc0")
                    p.done(each(bank[1], KD, Y_[0]), "s")
                    p.done(each(bank[6], Y_[0], EA[0]), "o0")
                    other(4)
                    a.wait(eng, it, "sc")
                    for i in two:
                        mm = eng.matmul(bank[0][:, i * 2 * P:(i + 1) * 2 * P], KN[:, i, 0, P:SEQ],
                                        S0[:, 2 * i:2 * i + 2, :].rearrange("p h e -> p (h e)"), start=True, stop=True)
                    p.done(mm, "ks")
                    other(5)
                    d.wait(eng, it, "r1")
                    p.done(each(bank[2], U_[1], R1), "vn1")
                    a.wait(eng, it, "vnc1")
                    o.wait(eng, it, "qd")
                    for h in four:
                        eng.matmul(bank[3][:, h * P:(h + 1) * P], Y_[1][:, h, :], EA[1][:, h, :], start=True, stop=False)
                        mm = eng.matmul(bank[3][:, h * P:(h + 1) * P], S0[:, h, :], QD[:, h, :], start=False, stop=True)
                    p.done(mm, "o1")
                    a.wait(eng, it, "sq2")
                    for i in two:
                        p.done(eng.matmul(bank[5 + i][:, :], ones[:, :],
                                          SQ2[:, 2 * i:2 * i + 2, :].rearrange("p h t -> p (h t)"), start=True,
                                          stop=True), f"oss{i}")
                    other(6)
                    other(7)

                self.run(eng, body)

            def rhs_wait(self, eng):
                def wait(k):
                    if k % HG == 0:
                        self.dv.wait(eng, k // HG, "low")
                return wait

        BT, sQ, sKD, sVT, sVN = carve(big, big_size, sBT=([P, 16, 3 * P], F32), sQ=([P, 8, SEQ], F32),
                                      sKD=([P, SWA_KV, SEQ], F32), sVT=([P, 2, SEQ], F32), sVN=([P, 2, 2, P], F32))
        sc_ = carve(work, work_size, sQS=([P, 2, SEQ], F32), sKS=([P, SEQ], F32), sVG=([P, 2, SWA_HD], F32),
                    sMX=([P, 4, 2], F32), sNM=([P, 4, 2], F32), sSM=([P, 4, 2], F32), sES=([P, 4, 2], F32),
                    **{f"{n}{i}": ([P, 3 * P], F32) for n in ("sSB", "sPT") for i in range(4)})
        QS, KS, VGs, sMX, sNM, sSM, sES = sc_[:7]
        SB, PT = sc_[7:11], sc_[11:15]
        onehot, bias_s = carve(spare, spare_size, onehot=([BUCKETS + 1, 3 * P], F32), bias_s=([16, 3 * P], F32))

        class KVSteps:

            def __init__(self, st, norm):
                self.st, self.norm = st, norm
                self.mb = sem("dma_bias_in")

            def dve(self, eng, it, u):
                st = self.st
                if u == 0:
                    self.norm.ready(eng)
                group_done(eng, st, it, u)
                b = bank[st.banks[u]]
                if u < 2:
                    for g in two:
                        for half in two:
                            ins = eng.tensor_tensor(sKD[64 * half:64 * half + 64, 2 * u + g, :],
                                                    b[64 * g:64 * g + 64, 0:SEQ], R[64 * g:64 * g + 64, 0:SEQ], ALU.mult)
                    leave(st, it, u, ins)
                else:
                    leave(st, it, u, eng.tensor_tensor(sVT[:, u - 2, :], b[:, 0:SEQ], R[:, 0:SEQ], ALU.mult))

            def act(self, eng, it, u):
                pass

            def pool(self, eng, it, u):
                if u:
                    return
                unit_done(eng, down3, down3.iters - 1, 7)
                eng.wait_ge(s_bias, 16)
                t = bias_d
                for c0, k0, n in ((0, P, P), (P, 0, 2 * P)):
                    src = bass.AP(tensor=t.tensor, offset=P - 1 + k0, ap=[[3 * P - 1, P], [3 * P * P, 16], [1, n]])
                    eng.dma_start(BT[:, :, c0:c0 + n], src).then_inc(self.mb, 16)

        def pe_bias(eng):
            eng.wait_ge(s_rel, 32)
            eng.matmul(bank[7][0:16, 0:3 * P], rel[:, :], onehot[:, :], start=True, stop=True).then_inc(s_bias_pe, 1)

        def dve_bias(eng):
            eng.wait_ge(s_bias_pe, 1)
            eng.tensor_copy(bias_s[:, :], bank[7][0:16, 0:3 * P]).then_inc(s_bias_dve, 1)

        def pool_bias(eng):
            eng.wait_ge(s_bias_dve, 1)
            eng.dma_start(bias_d, bias_s[:, :].unsqueeze(1).to_broadcast([16, P, 3 * P])).then_inc(s_bias, 16)

        class SCore:

            def __init__(self, kv, prev):
                self.kv, self.prev = kv, prev
                self.vt, self.vn = sem("pe_swa_v"), sem("act_swa_v")
                f = lambda *xs: [f"{x}{i}" for x in xs for i in four]
                self.ac = steps("act", "score", ["qs", "ks"] + [f"{x}{i}" for i in four for x in ("e", "es")] + ["vg"]
                                + f("ptc"))
                self.dv = steps("dve", "score", [f"{x}{i}" for i in four for x in ("b", "x", "nm")]
                                + [f"{x}{i}" for i in four for x in ("dn", "rc", "p")])
                self.pe_ = steps("pe", "score", f("s") + f("pt"))
                self.ac_end = steps("act", "score_end", ["oh0", "oh1"])
                self.dv_end = steps("dve", "score_end", ["ol0", "ol1"])
                self.pe_end = steps("pe", "score_end", f("o"))

            def run(self, eng, first, end, second):
                first(eng, 0)
                second(eng, 0)
                with eng.Fori(1, SWA_KV) as it:
                    first(eng, it)
                    end(eng, it - 1)
                    second(eng, it)
                end(eng, SWA_KV - 1)

            def act(self, eng):
                a, d, p = self.ac, self.dv, self.pe_
                eng.wait_ge(self.vt, 1)
                eng.activation(sVN[:, :, :, :].rearrange("p b c e -> p c b e"),
                               bank[5][:, :].rearrange("p (c b e) -> p c b e", c=2, b=2), ACT.Copy).then_inc(self.vn, 1)
                evacuated(eng, self.prev, self.prev.iters - 1, self.prev.groups - 1)
                eng.wait_ge(self.vn, 1)
                warm(eng, ACT.Exp)

                def softmax(eng, it):
                    p.wait(eng, it, "s3", back=1)
                    a.done(eng.activation(QS[:, :, :], sQ[:, bass.ds(it * 2, 2), :], ACT.Copy), "qs")
                    a.done(eng.activation(KS[:, :].unsqueeze(1), sKD[:, bass.ds(it, 1), :], ACT.Copy), "ks")
                    for i in four:
                        d.wait(eng, it, f"nm{i}")
                        for n, (c0, c1) in enumerate(((0, P), (P, 3 * P))):
                            ins = eng.activation(SB[i][:, c0:c1], SB[i][:, c0:c1], ACT.Exp, bias=sNM[:, i, n:n + 1],
                                                 accum_out=sSM[:, i, n:n + 1])
                        a.done(ins, f"e{i}")
                        a.done(eng.activation(sES[:, i, :], sNM[:, i, :], ACT.Exp, bias=v("sink", it * 4 + i)), f"es{i}")

                def output(eng, it):
                    for j in two:
                        self.pe_end.wait(eng, it, f"o{2 * j + 1}")
                        self.ac_end.done(eng.activation(OH[:, bass.ds(it * 2 + j, 1), :],
                                                        bank[6 + j][:, 0:SEQ].unsqueeze(1), ACT.Copy), f"oh{j}")

                def copies(eng, it):
                    self.pe_end.wait(eng, it, "o3", back=1)
                    vn = sVN[:, :, :, :].rearrange("p b c (x e) -> p b (c x) e", x=2)
                    a.done(eng.activation(VGs[:, :, :].unsqueeze(2), vn[:, :, bass.ds(it, 1), :], ACT.Copy), "vg")
                    for i in four:
                        p.wait(eng, it, f"pt{i}")
                        a.done(eng.activation(PT[i][:, :], bank[i][:, 0:3 * P], ACT.Copy), f"ptc{i}")
                self.run(eng, softmax, output, copies)

            def dve(self, eng):
                a, d, p = self.ac, self.dv, self.pe_
                eng.wait_ge(self.kv.mb, 32)

                def scores(eng, it):
                    for i in four:
                        p.wait(eng, it, f"s{i}")
                        d.done(eng.scalar_tensor_tensor(SB[i][:, :].unsqueeze(1), bank[i][:, 0:3 * P].unsqueeze(1),
                                                        SWA_HD ** -0.5, BT[:, bass.ds(it * 4 + i, 1), :], ALU.mult,
                                                        ALU.add), f"b{i}")
                        d.wait(eng, it, f"b{i}")
                        for n, (c0, c1) in enumerate(((0, P), (P, 3 * P))):
                            ins = eng.tensor_reduce(sMX[:, i, n:n + 1], SB[i][:, c0:c1], AX.X, ALU.max)
                        d.done(ins, f"x{i}")
                        d.wait(eng, it, f"x{i}")
                        d.done(eng.tensor_scalar(sNM[:, i, :], sMX[:, i, :], v("sink", it * 4 + i), -1.0, ALU.max,
                                                 ALU.mult), f"nm{i}")

                def low(eng, it):
                    for j in two:
                        self.ac_end.wait(eng, it, f"oh{j}")
                        self.dv_end.done(eng.tensor_tensor(OL[:, bass.ds(it * 2 + j, 1), :],
                                                           bank[6 + j][:, 0:SEQ].unsqueeze(1),
                                                           OH[:, bass.ds(it * 2 + j, 1), :].bitcast(F32),
                                                           ALU.subtract), f"ol{j}")

                def shares(eng, it):
                    for i in four:
                        a.wait(eng, it, f"es{i}")
                        d.done(eng.tensor_tensor(sSM[:, i, :], sSM[:, i, :], sES[:, i, :], ALU.add), f"dn{i}")
                        d.wait(eng, it, f"dn{i}")
                        d.done(eng.reciprocal(sSM[:, i, :], sSM[:, i, :]), f"rc{i}")
                        d.wait(eng, it, f"rc{i}")
                        for n, (c0, c1) in enumerate(((0, P), (P, 3 * P))):
                            ins = eng.tensor_scalar(SB[i][:, c0:c1], SB[i][:, c0:c1], sSM[:, i, n:n + 1], None, ALU.mult)
                        d.done(ins, f"p{i}")
                self.run(eng, scores, low, shares)

            def pool(self, eng):
                pass

            def pe_v(self, eng):
                evacuated(eng, self.kv.st, 0, 3)
                for c in two:
                    for b in two:
                        o = (2 * c + b) * P
                        mm = eng.transpose(bank[5][:, o:o + P], sVT[:, c, b * P:(b + 1) * P], ident)
                mm.then_inc(self.vt, 1)

            def pe(self, eng):
                a, d, p = self.ac, self.dv, self.pe_
                evacuated(eng, self.prev, self.prev.iters - 1, self.prev.groups - 1)

                def scores(eng, it):
                    a.wait(eng, it, "ks")
                    for i in four:
                        q, k = QS[64 * (i % 2):64 * (i % 2) + 64, i // 2, :], KS[64 * (i % 2):64 * (i % 2) + 64, :]
                        a.wait(eng, it, f"ptc{i}", back=1)
                        eng.matmul(bank[i][:, 0:P], q[:, 0:P], k[:, 0:P], start=True, stop=True)
                        p.done(eng.matmul(bank[i][:, P:3 * P], q[:, P:SEQ], k[:, :], start=True, stop=True), f"s{i}")

                def transposes(eng, it):
                    for i in four:
                        d.wait(eng, it, f"p{i}")
                        for t in range(3):
                            mm = eng.transpose(bank[i][:, t * P:(t + 1) * P], SB[i][:, t * P:(t + 1) * P], ident)
                        p.done(mm, f"pt{i}")

                def output(eng, it):
                    for i in four:
                        a.wait(eng, it, f"ptc{i}")
                        self.dv_end.wait(eng, it, f"ol{i // 2}", back=1)
                        out = bank[6 + i // 2][64 * (i % 2):64 * (i % 2) + 64, :]
                        eng.matmul(out[:, 0:P], VGs[:, 0, :], PT[i][:, 0:P], start=True, stop=True)
                        eng.matmul(out[:, P:SEQ], VGs[:, 0, :], PT[i][:, P:2 * P], start=True, stop=False)
                        self.pe_end.done(eng.matmul(out[:, P:SEQ], VGs[:, 1, :], PT[i][:, 2 * P:3 * P], start=False,
                                                    stop=True), f"o{i}")

                self.run(eng, scores, output, transposes)

            def rhs_wait(self, eng):
                def wait(k):
                    if k % 2 == 0:
                        self.dv_end.wait(eng, k // 2, "ol1")
                return wait

        def loaded(eng, c=None):
            eng.wait_ge(s_h0[0 if c is None or c < DC // 2 else 1], 16)

        n1 = norm_before("g0", TM, loaded)
        c_up1 = UpSteps(up1, n1)
        c_down1 = NormedSteps(down1, "g1", 0.5)
        a1 = norm_after(down1, TM)
        n2 = norm_before("g2", TM, a1.chunk)
        c_mg = MGateSteps(mgate, n2)
        c_mqk = ConvSteps(mqk, n2, "acw", "acb", lambda m: QK[:, bass.ds(m, 1), :], 0, 8)
        c_mv = ScaleSteps(mv, n2, lambda m: VT[:, bass.ds(m, 1), :])
        c_mog = ScaleSteps(mog, n2, lambda m: OG[:, bass.ds(m, 1), :], ACT.Sigmoid)
        core1 = MCore(c_mg, mog)
        core1.og_ready = lambda eng: c_mog.funcs.wait(eng, mog.iters - 1, "func3")
        core1.qk_ready = lambda eng: c_mqk.silus.wait(eng, mqk.iters - 1, "silu3")
        c_mout = NormedSteps(mout, "g3", 1.0)
        a3 = norm_after(mout, SEQ)
        n4 = norm_before("g4", SEQ, a3.chunk)
        c_up2 = UpSteps(up2, n4)
        c_down2 = NormedSteps(down2, "g5", 0.5)
        a5 = norm_after(down2, SEQ)
        n6 = norm_before("ga", SEQ, a5.chunk)
        c_gg = GGateSteps(ggate, n6)
        c_gqk = ConvSteps(gqk, n6, "dcw", None, lambda m: dQK[:, bass.ds(m, 1), :], 0, 32)
        c_vz0 = VZSteps(gvz0, n6, 0)
        c_vz = VZSteps(gvz, n6, 1)
        core2 = GCore(c_gg, gvz0, c_vz)
        core2.z_ready = lambda eng: c_vz0.silus.wait(eng, 0, "silu7")
        core2.qkv_ready = lambda eng: c_vz0.silus.wait(eng, 0, "silu7")
        c_gout = AddSteps(gout, [("gf0", XH, XL)])
        n7 = norm_streamed(gout)
        c_up3 = ConvUpSteps(up3, n7, 0)
        c_down3 = AddSteps(down3, [("gkv", XH, XL), ("gb", BH, BL)])
        n8 = norm_streamed(down3)
        c_kv = KVSteps(skv, n8)
        c_sq = ScaleSteps(sq_, n8, lambda m: sQ[:, bass.ds(m, 1), :])
        core3 = SCore(c_kv, sq_)
        c_so = AddSteps(so, [("gf1", XH, XL)])
        n9 = norm_streamed(so)
        c_up4 = ConvUpSteps(up4, n9, 1)
        c_down4 = AddSteps(down4, [])
        n10 = norm_streamed(down4)

        def prime(eng, kind):
            for k, s in primed:
                if k == kind:
                    s.prime(eng)

        def walk_all(eng, kind):
            def go(st, c, **hooks):
                walk(eng, kind, st, c, hooks.get(kind, {}))

            def core(c):
                {"act": c.act, "dve": c.dve, "pool": c.pool}[kind](eng)

            def normed(st, c, after, before):
                if kind == "dve":
                    c.before(eng)
                go(st, c)
                if kind == "act":
                    after.rstd(eng)
                    before.act(eng)
                if kind == "dve":
                    after.dve(eng, before.low)

            def gate_norm(n):
                return {"act": {0: n.square, 3: n.rstd}, "dve": {1: n.dve}}

            def up_norm(n):
                def both(eng):
                    n.square(eng)
                    n.rstd(eng)
                return {"act": {0: both}, "dve": {0: n.dve}}

            for u in range(SLOTS):
                split(eng, kind, stages[0], 0, u)
                if u == 0 and kind == "act":
                    n1.act(eng)
                if u == 0 and kind == "dve":
                    for c in range(DC):
                        n1.low(eng, c)
                if u == 2 and kind == "act":
                    n1.square(eng)
            if kind == "dve":
                n1.dve(eng)
            go(up1, c_up1, act={0: n1.rstd})
            if kind == "dve":
                dve_bias(eng)
            if kind == "pool":
                pool_bias(eng)
            normed(down1, c_down1, a1, n2)
            go(mgate, c_mg, **gate_norm(n2))
            go(mqk, c_mqk)
            go(mv, c_mv)
            go(mog, c_mog)
            core(core1)
            normed(mout, c_mout, a3, n4)
            go(up2, c_up2, **up_norm(n4))
            normed(down2, c_down2, a5, n6)

            def added(st, c):
                if kind == "dve":
                    c.before(eng)
                go(st, c)

            go(ggate, c_gg, **gate_norm(n6))
            go(gqk, c_gqk)
            go(gvz0, c_vz0)
            core(core2)
            added(gout, c_gout)
            go(up3, c_up3, act={0: n7.rstd})
            added(down3, c_down3)
            go(skv, c_kv, act={0: n8.rstd})
            go(sq_, c_sq)
            core(core3)
            added(so, c_so)
            go(up4, c_up4, act={0: n9.rstd})
            added(down4, c_down4)
            if kind == "act":
                n10.rstd(eng)
            if kind == "dve":
                n10.ready(eng)
                for c in range(DC):
                    eng.scalar_tensor_tensor(H[:, c, META:TM], H[:, c, META:TM], gains["gfin"][:, c:c + 1],
                                             R[:, 0:SEQ], ALU.mult, ALU.mult).then_inc(s_fin, 1)

        block = ctx.enter_context(nc.Block())

        @block.sync
        def _(eng):
            eng.dma_start(H[:, 0:DC // 2, :], a["h0"][:, 0:DC // 2, :]).then_inc(s_h0[0], 16)
            eng.dma_start(H[:, DC // 2:DC, :], a["h0"][:, DC // 2:DC, :]).then_inc(s_h0[1], 16)
            run_dma(eng)
            for c in range(0, DC, 2):
                eng.wait_ge(s_fin, c + 2)
                eng.dma_start(a["out"][:, c:c + 2, :], H[:, c:c + 2, META:TM]).then_inc(s_out, 16)
            eng.wait_ge(s_out, 16 * DC // 2)

        @block.gpsimd
        def _(eng):
            prime(eng, "pool")
            eng.wait_ge(s_h0[1], 16)
            eng.dma_start(cst[:, :], a["consts"]).then_inc(s_cst, 16)
            eng.dma_start(onehot[:, :], a["buckets"]).then_inc(s_rel, 16)
            eng.dma_start(rel[0:BUCKETS, :], a["rel_table"]).then_inc(s_rel, 16)
            for s in LO_POOL:
                eng.sem_inc(s_lo[s], 1)
            walk_all(eng, "pool")

        @block.scalar
        def _(eng):
            eng.dma_start(vec[:, :], a["vecs"]).then_inc(s_in, 16)
            prime(eng, "act")
            eng.wait_ge(s_in, 16)
            eng.wait_ge(s_ms, MEMSETS)
            walk_all(eng, "act")

        @block.vector
        def _(eng):
            prime(eng, "dve")
            eng.memset(scratch[:, :], EPS).then_inc(s_ms, 1)
            for s in set(range(SLOTS)) - LO_POOL:
                eng.sem_inc(s_lo[s], 1)
            eng.sem_inc(s_ev, 4)
            eng.memset(ones[:, :], 1.0).then_inc(s_ms, 1)
            eng.memset(mean[:, :], 1.0 / D).then_inc(s_ms, 1)
            for t in TP:
                eng.memset(t[:, 0:3], 0.0).then_inc(s_ms, 1)
            eng.memset(rel[BUCKETS:BUCKETS + 1, :], NEG).then_inc(s_ms, 1)
            eng.wait_ge(s_in, 16)
            walk_all(eng, "dve")

        @block.tensor
        def _(eng):
            prime(eng, "pe")
            for s in range(SLOTS):
                eng.sem_inc(s_pe[s], 1)
            eng.wait_ge(s_ms, MEMSETS)
            multiply(eng, up1, {2: n1.pe}, n1.rhs(eng))
            pe_bias(eng)
            multiply(eng, down1, None, c_up1.rhs_wait(eng))
            a1.pe(eng)
            multiply(eng, mgate, None, n2.rhs(eng))
            multiply(eng, mqk, {1: n2.pe})
            multiply(eng, mv, {0: c_mg.pe})
            multiply(eng, mog)
            core1.pe(eng)
            multiply(eng, mout, None, core1.rhs_wait(eng))
            a3.pe(eng)
            multiply(eng, up2, {2: n4.pe}, n4.rhs(eng))
            multiply(eng, down2, None, c_up2.rhs_wait(eng))
            a5.pe(eng)
            multiply(eng, ggate, None, n6.rhs(eng))
            multiply(eng, gqk, {1: n6.pe})
            multiply(eng, gvz0, {0: c_gg.pe})
            core2.pe(eng)
            multiply(eng, gout, None, core2.rhs_wait(eng))
            multiply(eng, up3, {2: n7.pe}, n7.rhs(eng))
            multiply(eng, down3, None, c_up3.rhs_wait(eng))
            multiply(eng, skv, {2: n8.pe}, n8.rhs(eng))
            multiply(eng, sq_, {0: core3.pe_v}, lambda k: down3.dv.wait(eng, k // 2, f"low1_{k % 2}"))
            core3.pe(eng)
            multiply(eng, so, None, core3.rhs_wait(eng))
            multiply(eng, up4, {2: n9.pe}, n9.rhs(eng))
            multiply(eng, down4, None, c_up4.rhs_wait(eng))
            n10.pe(eng)



def _tiles(w):
    k, m = w.shape
    return w.reshape(k // P, P, m // P, P).transpose(2, 1, 0, 3)


def _bodies(tiles, groups):
    m, p, k, f = tiles.shape
    return np.ascontiguousarray(tiles.reshape(m // groups, groups, p, k, f).transpose(0, 2, 1, 3, 4)
                                .reshape(m // groups, p, groups * k, f))


def _pairs(w):
    t = _tiles(w)
    return _bodies(t.reshape(2, FC, *t.shape[1:]).transpose(1, 0, 2, 3, 4).reshape(t.shape), 4)


def _turns(x, y, n):
    return np.stack([t.reshape(-1, n, *t.shape[1:]) for t in (x, y)], axis=1).reshape(-1, *x.shape[1:])


def _gates(w, n):
    out = np.zeros((D, P), w.dtype)
    out[:, 0:n] = w[:, 0:n]
    out[:, 32:32 + n] = w[:, n:2 * n]
    return _bodies(_tiles(out), 1)


def _col(x):
    return np.ascontiguousarray(x.reshape(-1, P).T)


def _pair_cols(x):
    c = x.reshape(-1, 2, FC, P).transpose(0, 2, 1, 3)
    return _col(c)


def _pad(x, n):
    out = np.zeros((P, n), np.float32)
    out[0:x.shape[0], 0:x.shape[1]] = x
    return out


def kernel(**inputs):
    from concourse import bacc
    from concourse.bass_utils import run_bass_kernel_spmd

    i = {k: np.asarray(x) for k, x in inputs.items()}
    ng = i["norm_gains"][0]
    qk_cols = GDN_QK * P
    w2 = i["a_w_in_2"][0]
    kq = w2[:, 0:2 * qk_cols].reshape(D, 2, GDN_QK, P)[:, ::-1].transpose(0, 2, 1, 3).reshape(D, 2 * qk_cols)
    cw = i["a_conv_w_2"][0]
    cw_kq = cw[:, 0:2 * qk_cols].reshape(4, 2, GDN_QK, P)[:, ::-1].transpose(0, 2, 1, 3).reshape(4, 2 * qk_cols)
    gdn_cw = np.concatenate([cw_kq, cw[:, 2 * qk_cols:]], axis=1)
    vecs = {"acw": _col(i["a_conv_w"][0]), "acb": _col(i["a_conv_b"][0]), "dcw": _col(gdn_cw),
            "onw": _col(i["a_out_norm_w_2"]), "sink": np.repeat(i["b_sinks_2"], P, axis=0),
            "gate": _pad(i["a_gate_b"][0].reshape(2, A_HEADS).T, 2),
            "dn": _pad(np.stack([i["a_a_log_2"][0], i["a_dt_bias_2"][0]], axis=1), 2),
            "ga": _col(i["a_norm_w_2"]), "gkv": _col(i["kv_norm_w_2"]), "gb": _col(i["b_norm_w_2"]),
            "gf0": _col(i["ffn_norm_w_2"][0]), "gf1": _col(i["ffn_norm_w_2"][1]), "gfin": _col(i["final_norm_w_2"])}
    for n in range(6):
        vecs[f"g{n}"] = _col(ng[n])
    for n in range(2):
        vecs[f"fcw{n}"] = _pair_cols(i["ffn_conv_w_2"][n])
        vecs[f"fcb{n}"] = _pair_cols(i["ffn_conv_b_2"][n])
    for n, size in _VEC_SIZES:
        assert vecs[n].shape == (P, size), (n, vecs[n].shape)
    aw = i["a_w_in"][0]
    h0 = np.concatenate([i["meta_tokens"], i["x"][0]], axis=0).T.reshape(DC, P, TM).transpose(1, 0, 2)
    arrays = {
        "vecs": np.concatenate([vecs[n] for n, _ in _VEC_SIZES], axis=1),
        "consts": constants(), "buckets": bucket_rows(), "h0": np.ascontiguousarray(h0),
        "rel_table": i["rel_bias_table_2"],
        "w_up1": _pairs(i["ffn_w_in"][0, 0]), "w_down1": _bodies(_tiles(i["ffn_w_out"][0, 0]), 2),
        "w_up2": _pairs(i["ffn_w_in"][0, 1]), "w_down2": _bodies(_tiles(i["ffn_w_out"][0, 1]), 2),
        "w_mgate": _gates(aw[:, 3072:], A_HEADS), "w_mqk": _bodies(_tiles(aw[:, 0:1024]), 4),
        "w_mv": _bodies(_tiles(aw[:, 1024:2048]), 4), "w_mog": _bodies(_tiles(aw[:, 2048:3072]), 4),
        "w_mout": _bodies(_tiles(i["a_w_out"][0]), 4),
        "w_ggate": _gates(w2[:, 6144:], GDN_V), "w_gqk": _bodies(_tiles(kq), 4),
        "w_gvz": _bodies(_turns(_tiles(w2[:, 2048:4096]), _tiles(w2[:, 4096:6144]), 4), 8),
        "w_gout": _bodies(_tiles(i["a_w_out_2"][0]), 2),
        "w_up3": _pairs(i["ffn_w_up_2"][0]), "w_down3": _bodies(_tiles(i["ffn_w_down_2"][0]), 2),
        "w_skv": _bodies(_tiles(i["w_kv_2"]), 4), "w_sq": _bodies(_tiles(i["b_w_q_2"][0]), 4),
        "w_so": _bodies(_tiles(i["b_w_o_2"][0]), 4),
        "w_up4": _pairs(i["ffn_w_up_2"][1]), "w_down4": _bodies(_tiles(i["ffn_w_down_2"][1]), 2),
    }
    nc = bacc.Bacc("TRN2", target_bir_lowering=False, num_devices=1)
    a = {n: nc.dram_tensor(f"in_{n}", x.shape, F32, kind="ExternalInput").ap() for n, x in arrays.items()}
    a["out"] = nc.dram_tensor("out", (P, DC, SEQ), F32, kind="ExternalOutput").ap()
    program(nc, a)
    r = run_bass_kernel_spmd(nc, [{f"in_{n}": x for n, x in arrays.items()}], core_ids=[0])
    y = r.results[0]["out"]
    return np.ascontiguousarray(y.transpose(2, 1, 0).reshape(1, SEQ, D))
```
